# Optimizing a Trainium2 kernel written in Bass

```python
import math
import jax, jax.numpy as jnp
from jax import lax
import numpy as np

D_MODEL = 1024
BATCH = 1
SEQ = 1024
DEPTH = 1

MEM_LEN = 256
N_MLSTM_HEADS = 4
MLSTM_HEAD_DIM = 128
MLSTM_WIDTH = N_MLSTM_HEADS * MLSTM_HEAD_DIM
CONV_WIDTH = 4
MLSTM_CHUNK = 128
N_DIFF_HEADS = 4
DIFF_QK_DIM = 64
DIFF_V_DIM = 2 * DIFF_QK_DIM
DIFF_WIDTH = N_DIFF_HEADS * DIFF_V_DIM
Q_BLOCK = 128
N_MEM_HEADS = 4
MEM_HEAD_DIM = 128
MEM_WIDTH = N_MEM_HEADS * MEM_HEAD_DIM
MIX_WIDTH = MLSTM_WIDTH + DIFF_WIDTH + MEM_WIDTH
IN_WIDTHS = (MLSTM_WIDTH, MLSTM_WIDTH, MLSTM_WIDTH,
             2 * N_DIFF_HEADS * DIFF_QK_DIM, 2 * N_DIFF_HEADS * DIFF_QK_DIM, DIFF_WIDTH, DIFF_WIDTH,
             MEM_WIDTH, MEM_WIDTH)
IN_WIDTH = 4608
NORM_EPS = 1e-6


def _split_cols(a, widths):
    offs = np.cumsum(widths)[:-1].tolist()
    return jnp.split(a, offs, axis=-1)

def rmsnorm(x, g):
    xf = x.astype(jnp.float32)
    y = xf * lax.rsqrt(jnp.mean(xf * xf, axis=-1, keepdims=True) + NORM_EPS)
    return (y * g.astype(jnp.float32)).astype(x.dtype)

def head_layernorm(h, g):
    mu = jnp.mean(h, axis=-1, keepdims=True)
    var = jnp.mean(jnp.square(h - mu), axis=-1, keepdims=True)
    y = (h - mu) * lax.rsqrt(var + NORM_EPS)
    y = y.reshape(h.shape[0], h.shape[1], -1)
    return y * g.astype(jnp.float32)

def causal_depthwise_conv(x, w, b):
    y = lax.conv_general_dilated(x, w[:, None, :], window_strides=(1,),
                                 padding=[(CONV_WIDTH - 1, 0)],
                                 dimension_numbers=('NWC', 'WIO', 'NWC'),
                                 feature_group_count=x.shape[-1])
    return y + b

def mlstm_chunkwise(q, k, v, i_pre, f_pre):
    B_, H_, S_, dh = q.shape
    L = MLSTM_CHUNK
    nc = S_ // L
    k = k * (dh ** -0.5)
    log_f = jax.nn.log_sigmoid(f_pre)

    def chunks(a):
        a = a.reshape((B_, H_, nc, L) + a.shape[3:])
        return jnp.moveaxis(a, 2, 0)

    qc, kc, vc, ic = chunks(q), chunks(k), chunks(v), chunks(i_pre)
    bc = jnp.cumsum(chunks(log_f), axis=-1)
    tri = jnp.tril(jnp.ones((L, L), dtype=bool))

    def step(carry, inp):
        C, n, m = carry
        qb, kb, vb, ib, bb = inp
        d = bb[..., :, None] - bb[..., None, :] + ib[..., None, :]
        d = jnp.where(tri, d, -jnp.inf)
        g = bb + m[..., None]
        m_t = jnp.maximum(g, jnp.max(d, axis=-1))
        s_qk = jnp.einsum('bhtk,bhsk->bhts', qb, kb) * jnp.exp(d - m_t[..., None])
        inter = jnp.exp(g - m_t)
        num = (jnp.einsum('bhts,bhsv->bhtv', s_qk, vb)
               + inter[..., None] * jnp.einsum('bhvk,bhtk->bhtv', C, qb))
        den = jnp.sum(s_qk, axis=-1) + inter * jnp.einsum('bhk,bhtk->bht', n, qb)
        h = num / jnp.maximum(jnp.abs(den), jnp.exp(-m_t))[..., None]
        b_end = bb[..., -1]
        a = b_end[..., None] - bb + ib
        m_new = jnp.maximum(b_end + m, jnp.max(a, axis=-1))
        wa = jnp.exp(a - m_new[..., None])
        decay = jnp.exp(b_end + m - m_new)
        C_new = decay[..., None, None] * C + jnp.einsum('bhs,bhsv,bhsk->bhvk', wa, vb, kb)
        n_new = decay[..., None] * n + jnp.einsum('bhs,bhsk->bhk', wa, kb)
        return (C_new, n_new, m_new), h

    init = (jnp.zeros((B_, H_, dh, dh), jnp.float32),
            jnp.zeros((B_, H_, dh), jnp.float32),
            jnp.zeros((B_, H_), jnp.float32))
    _, h = lax.scan(step, init, (qc, kc, vc, ic, bc))
    return jnp.moveaxis(h, 0, 2).reshape(B_, H_, S_, dh)

def diff_causal_attention(q, k, v, lam):
    S_ = q.shape[3]
    scale = DIFF_QK_DIM ** -0.5
    outs = []
    for j in range(S_ // Q_BLOCK):
        lo, hi = j * Q_BLOCK, (j + 1) * Q_BLOCK
        s = jnp.einsum('bhmqd,bhmkd->bhmqk', q[:, :, :, lo:hi], k[:, :, :, :hi]).astype(jnp.float32) * scale
        mask = jnp.arange(hi)[None, :] <= jnp.arange(lo, hi)[:, None]
        p = jax.nn.softmax(jnp.where(mask, s, -jnp.inf), axis=-1)
        pd = p[:, :, 0] - lam * p[:, :, 1]
        outs.append(jnp.einsum('bhqk,bhkd->bhqd', pd.astype(v.dtype), v[:, :, :hi]))
    return jnp.concatenate(outs, axis=2)

def first_inputs(seed: int = 0) -> dict:
    key = jax.random.key(seed)
    ks = jax.random.split(key, 24)
    nrm = jax.random.normal
    f32 = jnp.float32
    H = N_MLSTM_HEADS
    b_i = 0.1 * nrm(ks[10], (DEPTH, H), f32)
    b_f = 3.0 + 3.0 * jax.random.uniform(ks[11], (DEPTH, H), f32)
    return {
        'x': nrm(ks[0], (BATCH, SEQ, D_MODEL), f32),
        'mem': nrm(ks[1], (BATCH, MEM_LEN, D_MODEL), f32),
        'norm_g': 1.0 + 0.02 * nrm(ks[2], (DEPTH, D_MODEL), f32),
        'w_in': nrm(ks[3], (DEPTH, D_MODEL, IN_WIDTH), f32) * D_MODEL ** -0.5,
        'conv_w': nrm(ks[4], (DEPTH, CONV_WIDTH, MLSTM_WIDTH), f32) * CONV_WIDTH ** -0.5,
        'conv_b': 0.01 * nrm(ks[5], (DEPTH, MLSTM_WIDTH), f32),
        'wq_m': nrm(ks[6], (DEPTH, H, MLSTM_HEAD_DIM, MLSTM_HEAD_DIM), f32) * MLSTM_HEAD_DIM ** -0.5,
        'wk_m': nrm(ks[7], (DEPTH, H, MLSTM_HEAD_DIM, MLSTM_HEAD_DIM), f32) * MLSTM_HEAD_DIM ** -0.5,
        'wv_m': nrm(ks[8], (DEPTH, H, MLSTM_HEAD_DIM, MLSTM_HEAD_DIM), f32) * MLSTM_HEAD_DIM ** -0.5,
        'w_if': nrm(ks[9], (DEPTH, 3 * MLSTM_WIDTH, 2 * H), f32) * (3 * MLSTM_WIDTH) ** -0.5,
        'b_if': jnp.concatenate([b_i, b_f], axis=-1),
        'mnorm_g': 1.0 + 0.02 * nrm(ks[12], (DEPTH, MLSTM_WIDTH), f32),
        'skip_m': 1.0 + 0.02 * nrm(ks[13], (DEPTH, MLSTM_WIDTH), f32),
        'lam_q1': 0.1 * nrm(ks[14], (DEPTH, DIFF_QK_DIM), f32),
        'lam_k1': 0.1 * nrm(ks[15], (DEPTH, DIFF_QK_DIM), f32),
        'lam_q2': 0.1 * nrm(ks[16], (DEPTH, DIFF_QK_DIM), f32),
        'lam_k2': 0.1 * nrm(ks[17], (DEPTH, DIFF_QK_DIM), f32),
        'dnorm_g': 1.0 + 0.02 * nrm(ks[18], (DEPTH, DIFF_WIDTH), f32),
        'mem_norm_g': 1.0 + 0.02 * nrm(ks[19], (DEPTH, D_MODEL), f32),
        'w_mem_kv': nrm(ks[20], (DEPTH, D_MODEL, 2 * MEM_WIDTH), f32) * D_MODEL ** -0.5,
        'w_out': nrm(ks[21], (DEPTH, MIX_WIDTH, D_MODEL), f32) * MIX_WIDTH ** -0.5,
        'final_g': 1.0 + 0.02 * nrm(ks[22], (D_MODEL,), f32),
    }

def first_block(x, mem, norm_g, w_in, conv_w, conv_b, wq_m, wk_m, wv_m, w_if, b_if, mnorm_g, skip_m,
              lam_q1, lam_k1, lam_q2, lam_k2, dnorm_g, mem_norm_g, w_mem_kv, w_out, final_g):
    B_, S_, _ = x.shape
    Hm, dh = N_MLSTM_HEADS, MLSTM_HEAD_DIM
    Hd, Hc = N_DIFF_HEADS, N_MEM_HEADS
    for l in range(DEPTH):
        h = rmsnorm(x, norm_g[l])
        proj = h @ w_in[l]
        x_m, o_m, z_m, q_d, k_d, v_d, z_d, q_c, z_c = _split_cols(proj, IN_WIDTHS)

        x_cv = jax.nn.silu(causal_depthwise_conv(x_m, conv_w[l], conv_b[l]))
        xch = x_cv.reshape(B_, S_, Hm, dh)
        xmh = x_m.reshape(B_, S_, Hm, dh)
        q = jnp.einsum('bshd,hde->bshe', xch, wq_m[l])
        k = jnp.einsum('bshd,hde->bshe', xch, wk_m[l])
        v = jnp.einsum('bshd,hde->bshe', xmh, wv_m[l])
        qkv = jnp.concatenate([q, k, v], axis=2).reshape(B_, S_, 3 * MLSTM_WIDTH)
        gates = (qkv @ w_if[l] + b_if[l]).astype(jnp.float32)
        i_pre = jnp.transpose(gates[..., :Hm], (0, 2, 1))
        f_pre = jnp.transpose(gates[..., Hm:], (0, 2, 1))
        tr = lambda a: jnp.transpose(a.astype(jnp.float32), (0, 2, 1, 3))
        h_t = mlstm_chunkwise(tr(q), tr(k), tr(v), i_pre, f_pre)
        h_t = jnp.transpose(h_t, (0, 2, 1, 3))
        h_t = jax.nn.sigmoid(o_m.reshape(B_, S_, Hm, dh).astype(jnp.float32)) * h_t
        y_m = head_layernorm(h_t, mnorm_g[l]).astype(x.dtype)
        y_m = (y_m + skip_m[l] * x_cv) * jax.nn.silu(z_m)

        qd = jnp.transpose(q_d.reshape(B_, S_, Hd, 2, DIFF_QK_DIM), (0, 2, 3, 1, 4))
        kd = jnp.transpose(k_d.reshape(B_, S_, Hd, 2, DIFF_QK_DIM), (0, 2, 3, 1, 4))
        vd = jnp.transpose(v_d.reshape(B_, S_, Hd, DIFF_V_DIM), (0, 2, 1, 3))
        lam_init = 0.8 - 0.6 * math.exp(-0.3 * l)
        lam = (jnp.exp(jnp.sum(lam_q1[l].astype(jnp.float32) * lam_k1[l].astype(jnp.float32)))
               - jnp.exp(jnp.sum(lam_q2[l].astype(jnp.float32) * lam_k2[l].astype(jnp.float32)))
               + lam_init)
        od = jnp.transpose(diff_causal_attention(qd, kd, vd, lam), (0, 2, 1, 3))
        od = rmsnorm(od, dnorm_g[l].reshape(Hd, DIFF_V_DIM)) * (1.0 - lam_init)
        y_d = od.reshape(B_, S_, DIFF_WIDTH) * jax.nn.silu(z_d)

        kv = rmsnorm(mem, mem_norm_g[l]) @ w_mem_kv[l]
        km = kv[..., :MEM_WIDTH].reshape(B_, -1, Hc, MEM_HEAD_DIM)
        vm = kv[..., MEM_WIDTH:].reshape(B_, -1, Hc, MEM_HEAD_DIM)
        qc = q_c.reshape(B_, S_, Hc, MEM_HEAD_DIM)
        sc = jnp.einsum('bshd,bmhd->bhsm', qc, km).astype(jnp.float32) * MEM_HEAD_DIM ** -0.5
        pc = jax.nn.softmax(sc, axis=-1).astype(x.dtype)
        oc = jnp.einsum('bhsm,bmhd->bshd', pc, vm).reshape(B_, S_, MEM_WIDTH)
        y_c = oc * jax.nn.silu(z_c)

        y = jnp.concatenate([y_m, y_d, y_c], axis=-1) @ w_out[l]
        x = x + y
    return rmsnorm(x, final_g)


_first_inputs = first_inputs


def first_inputs(seed=0):
    import zlib

    import numpy as np

    out = dict(_first_inputs(seed))
    spreads = {}
    factors = {'norm_g': 3.08,
     'conv_b': 8.0,
     'mnorm_g': 200.0,
     'skip_m': 143.629,
     'lam_q1': 200.0,
     'dnorm_g': 200.0,
     'mem_norm_g': 59.701,
     'final_g': 22.327}
    for name, (base, spread) in spreads.items():
        noise = np.random.default_rng([zlib.crc32(name.encode()), seed]).standard_normal(out[name].shape)
        drawn = base * np.exp(spread * noise) if base else spread * noise
        out[name] = __import__('jax').numpy.asarray(drawn.astype(out[name].dtype))
    for name, factor in factors.items():
        out[name] = (out[name] * factor).astype(out[name].dtype)
    return out


_narrow_inputs = first_inputs


def first_inputs(seed=0):

    out = dict(_narrow_inputs(seed))
    wider = {'mnorm_g': 6.53, 'skip_m': 4.46, 'dnorm_g': 8.35, 'final_g': 3.16}
    for name, times in wider.items():
        mean = out[name].mean()
        out[name] = (mean + times * (out[name] - mean)).astype(out[name].dtype)
    return out


CHUNK = 64
LEFT_CHUNKS = 8
BAND = (LEFT_CHUNKS + 1) * CHUNK
ATT_HEADS = 8
ATT_HEAD_DIM = 64
ATT_WIDTH = ATT_HEADS * ATT_HEAD_DIM
MAX_REL_DIST = 128
SGU_CHUNK = 128
SGU_GROUPS = 4
SGU_WIDTH = 512
SGU_GROUP_DIM = SGU_WIDTH // SGU_GROUPS
N_BRANCHES = 2
IN_WIDTH_2 = 3 * ATT_WIDTH + 2 * SGU_WIDTH + N_BRANCHES * D_MODEL
D_FF = -(-(8 * D_MODEL) // (3 * 256)) * 256
EPS = 1e-6


def rmsnorm_2(x, g):
    xf = x.astype(jnp.float32)
    xf = xf * lax.rsqrt(jnp.mean(xf * xf, axis=-1, keepdims=True) + EPS)
    return (xf * g.astype(jnp.float32)).astype(x.dtype)

def layernorm(x, g, b):
    xf = x.astype(jnp.float32)
    mu = jnp.mean(xf, axis=-1, keepdims=True)
    var = jnp.mean(jnp.square(xf - mu), axis=-1, keepdims=True)
    y = (xf - mu) * lax.rsqrt(var + EPS) * g.astype(jnp.float32) + b.astype(jnp.float32)
    return y.astype(x.dtype)

def chunked_rel_attention(q, k, v, rel_bias):
    B, S, H, Dh = q.shape
    nc = S // CHUNK
    pad = LEFT_CHUNKS * CHUNK
    qc = q.reshape(B, nc, CHUNK, H, Dh)
    kp = jnp.pad(k, ((0, 0), (pad, 0), (0, 0), (0, 0)))
    vp = jnp.pad(v, ((0, 0), (pad, 0), (0, 0), (0, 0)))
    band_idx = jnp.arange(nc)[:, None] * CHUNK + jnp.arange(BAND)[None, :]
    kb = kp[:, band_idx]
    vb = vp[:, band_idx]
    scores = jnp.einsum('bcqhd,bckhd->bhcqk', qc, kb).astype(jnp.float32) * (Dh ** -0.5)
    q_pos = pad + jnp.arange(CHUNK)
    k_pos = jnp.arange(BAND)
    rel = jnp.clip(q_pos[:, None] - k_pos[None, :], -MAX_REL_DIST, MAX_REL_DIST) + MAX_REL_DIST
    bias = rel_bias.astype(jnp.float32)[:, rel]
    scores = scores + bias[None, :, None, :, :]
    key_chunk = jnp.arange(nc)[:, None] - LEFT_CHUNKS + (k_pos // CHUNK)[None, :]
    valid = key_chunk >= 0
    scores = jnp.where(valid[None, None, :, None, :], scores, jnp.float32(-1e30))
    probs = jax.nn.softmax(scores, axis=-1).astype(v.dtype)
    out = jnp.einsum('bhcqk,bckhd->bcqhd', probs, vb)
    return out.reshape(B, S, H * Dh)

def spatial_gating(u, v, ln_g, ln_b, w_s, b_s):
    B, S, _ = v.shape
    ng = S // SGU_CHUNK
    v = layernorm(v, ln_g, ln_b)
    vg = v.reshape(B, ng, SGU_CHUNK, SGU_GROUPS, SGU_GROUP_DIM)
    causal = jnp.tril(jnp.ones((SGU_CHUNK, SGU_CHUNK), dtype=bool))
    w = jnp.where(causal[None], w_s, jnp.zeros_like(w_s))
    mixed = jnp.einsum('gts,bnsgd->bntgd', w, vg) + b_s.T[None, None, :, :, None]
    return u * mixed.reshape(B, S, SGU_WIDTH)

def second_inputs(seed: int = 0) -> dict:
    key = jax.random.key(seed)
    ks = jax.random.split(key, 16)
    f32 = jnp.float32

    def nrm(k, shape, scale):
        return jax.random.normal(k, shape, f32) * scale

    x = nrm(ks[0], (BATCH, SEQ, D_MODEL), 1.0)
    norm_mix = 1.0 + nrm(ks[1], (DEPTH, D_MODEL), 0.02)
    w_in = nrm(ks[2], (DEPTH, D_MODEL, IN_WIDTH_2), D_MODEL ** -0.5)
    att_rel_bias = nrm(ks[3], (DEPTH, ATT_HEADS, 2 * MAX_REL_DIST + 1), 0.1)
    sgu_norm_gain = 1.0 + nrm(ks[4], (DEPTH, SGU_WIDTH), 0.02)
    sgu_norm_bias = nrm(ks[5], (DEPTH, SGU_WIDTH), 0.02)
    sgu_w = nrm(ks[6], (DEPTH, SGU_GROUPS, SGU_CHUNK, SGU_CHUNK), 0.5 * SGU_CHUNK ** -0.5)
    sgu_b = 1.0 + nrm(ks[7], (DEPTH, SGU_GROUPS, SGU_CHUNK), 0.02)
    w_br_att = nrm(ks[8], (DEPTH, ATT_WIDTH, D_MODEL), ATT_WIDTH ** -0.5)
    w_br_sgu = nrm(ks[9], (DEPTH, SGU_WIDTH, D_MODEL), SGU_WIDTH ** -0.5)
    b_gate = nrm(ks[10], (DEPTH, N_BRANCHES, D_MODEL), 0.02)
    w_out = nrm(ks[11], (DEPTH, D_MODEL, D_MODEL), D_MODEL ** -0.5)
    norm_ffn = 1.0 + nrm(ks[12], (DEPTH, D_MODEL), 0.02)
    w_ffn_in = nrm(ks[13], (DEPTH, D_MODEL, 2 * D_FF), D_MODEL ** -0.5)
    w_ffn_out = nrm(ks[14], (DEPTH, D_FF, D_MODEL), D_FF ** -0.5)
    norm_final = 1.0 + nrm(ks[15], (D_MODEL,), 0.02)
    return {"x": x, "norm_mix": norm_mix, "w_in": w_in, "att_rel_bias": att_rel_bias,
            "sgu_norm_gain": sgu_norm_gain, "sgu_norm_bias": sgu_norm_bias,
            "sgu_w": sgu_w, "sgu_b": sgu_b, "w_br_att": w_br_att, "w_br_sgu": w_br_sgu,
            "b_gate": b_gate, "w_out": w_out, "norm_ffn": norm_ffn,
            "w_ffn_in": w_ffn_in, "w_ffn_out": w_ffn_out, "norm_final": norm_final}

def second_block(x, norm_mix, w_in, att_rel_bias, sgu_norm_gain, sgu_norm_bias, sgu_w, sgu_b,
              w_br_att, w_br_sgu, b_gate, w_out, norm_ffn, w_ffn_in, w_ffn_out, norm_final):
    B, S, D = x.shape
    h = x
    for l in range(DEPTH):
        xn = rmsnorm_2(h, norm_mix[l])
        proj = xn @ w_in[l]
        q, k, v, u, vs, gate_logits = jnp.split(
            proj, np.cumsum([ATT_WIDTH, ATT_WIDTH, ATT_WIDTH, SGU_WIDTH, SGU_WIDTH]).tolist(), axis=-1)
        q = q.reshape(B, S, ATT_HEADS, ATT_HEAD_DIM)
        k = k.reshape(B, S, ATT_HEADS, ATT_HEAD_DIM)
        v = v.reshape(B, S, ATT_HEADS, ATT_HEAD_DIM)
        att = chunked_rel_attention(q, k, v, att_rel_bias[l])
        sgu = spatial_gating(jax.nn.gelu(u), jax.nn.gelu(vs), sgu_norm_gain[l], sgu_norm_bias[l],
                             sgu_w[l], sgu_b[l])
        br_att = att @ w_br_att[l]
        br_sgu = sgu @ w_br_sgu[l]
        gates = jax.nn.sigmoid(gate_logits.reshape(B, S, N_BRANCHES, D) + b_gate[l])
        merged = gates[:, :, 0] * br_att + gates[:, :, 1] * br_sgu
        h = h + merged @ w_out[l]
        hn = rmsnorm_2(h, norm_ffn[l])
        g, up = jnp.split(hn @ w_ffn_in[l], 2, axis=-1)
        h = h + (jax.nn.silu(g) * up) @ w_ffn_out[l]
    return rmsnorm_2(h, norm_final)


_first_inputs_2 = second_inputs


def second_inputs(seed=0):
    import zlib

    import numpy as np

    out = dict(_first_inputs_2(seed))
    spreads = {}
    factors = {'norm_mix': 5.586,
     'att_rel_bias': 22.663,
     'sgu_norm_gain': 62.274,
     'sgu_norm_bias': 56.36,
     'sgu_b': 23.324,
     'b_gate': 8.0,
     'norm_ffn': 17.117,
     'norm_final': 8.203}
    for name, (base, spread) in spreads.items():
        noise = np.random.default_rng([zlib.crc32(name.encode()), seed]).standard_normal(out[name].shape)
        drawn = base * np.exp(spread * noise) if base else spread * noise
        out[name] = __import__('jax').numpy.asarray(drawn.astype(out[name].dtype))
    for name, factor in factors.items():
        out[name] = (out[name] * factor).astype(out[name].dtype)
    return out


_narrow_inputs_2 = second_inputs


def second_inputs(seed=0):

    out = dict(_narrow_inputs_2(seed))
    wider = {'att_rel_bias': 4.12,
     'sgu_norm_gain': 3.64,
     'sgu_norm_bias': 3.61,
     'sgu_b': 3.26,
     'norm_final': 3.22}
    for name, times in wider.items():
        mean = out[name].mean()
        out[name] = (mean + times * (out[name] - mean)).astype(out[name].dtype)
    return out


N_META = 16
D_MIX = D_MODEL
D_LRU = D_MIX // 2
D_CC = D_MIX - D_LRU
LRU_HEADS = 8
LRU_HEAD_DIM = D_LRU // LRU_HEADS
CC_GROUPS = 8
LRU_CONV_W = 4
CC_CONV_W = 31
LRU_C = 8.0
D_FF_3 = 4 * D_MODEL


def rmsnorm_3(x, g):
    xf = x.astype(jnp.float32)
    y = xf * lax.rsqrt(jnp.mean(xf * xf, axis=-1, keepdims=True) + EPS)
    return (y * g.astype(jnp.float32)).astype(x.dtype)

def layernorm_3(x, g, b):
    xf = x.astype(jnp.float32)
    mu = jnp.mean(xf, axis=-1, keepdims=True)
    var = jnp.mean(jnp.square(xf - mu), axis=-1, keepdims=True)
    y = (xf - mu) * lax.rsqrt(var + EPS)
    return (y * g.astype(jnp.float32) + b.astype(jnp.float32)).astype(x.dtype)

def causal_depthwise_conv_3(x, w, b):
    k = w.shape[0]
    y = lax.conv_general_dilated(
        x, w[:, None, :].astype(x.dtype), window_strides=(1,), padding=[(k - 1, 0)],
        dimension_numbers=("NWC", "WIO", "NWC"), feature_group_count=x.shape[-1])
    return y + b.astype(x.dtype)

def block_diag_linear(x, w, b):
    B, T, _ = x.shape
    h, dh, _ = w.shape
    y = jnp.einsum("bthi,hij->bthj", x.reshape(B, T, h, dh), w.astype(x.dtype))
    return y.reshape(B, T, h * dh) + b.astype(x.dtype)

def rg_lru(x, w_a, b_a, w_x, b_x, a_param):
    xf = x.astype(jnp.float32)
    r = jax.nn.sigmoid(block_diag_linear(xf, w_a, b_a))
    i = jax.nn.sigmoid(block_diag_linear(xf, w_x, b_x))
    log_a = -LRU_C * r * jax.nn.softplus(-a_param.astype(jnp.float32))
    a = jnp.exp(log_a)
    mult = jnp.sqrt(-jnp.expm1(2.0 * log_a))
    bterm = mult * (i * xf)

    def combine(left, right):
        a1, b1 = left
        a2, b2 = right
        return a1 * a2, a2 * b1 + b2

    _, h = lax.associative_scan(combine, (a, bterm), axis=1)
    return h.astype(x.dtype)

def third_inputs(seed: int = 0) -> dict:
    key = jax.random.key(seed)
    ks = jax.random.split(key, 24)
    f32 = jnp.float32

    def nrm(k, shape, scale):
        return jax.random.normal(k, shape, f32) * scale

    x = jax.random.normal(ks[0], (BATCH, SEQ, D_MODEL), f32)
    meta_tokens = nrm(ks[1], (N_META, D_MODEL), 1.0)
    norm_mix_g = 1.0 + nrm(ks[2], (DEPTH, D_MODEL), 0.02)
    w_in = nrm(ks[3], (DEPTH, D_MODEL, 2 * D_LRU + 2 * D_CC), D_MODEL ** -0.5)
    lru_conv_w = nrm(ks[4], (DEPTH, LRU_CONV_W, D_LRU), LRU_CONV_W ** -0.5)
    lru_conv_b = nrm(ks[5], (DEPTH, D_LRU), 0.01)
    lru_gate_a_w = nrm(ks[6], (DEPTH, LRU_HEADS, LRU_HEAD_DIM, LRU_HEAD_DIM), LRU_HEAD_DIM ** -0.5)
    lru_gate_a_b = nrm(ks[7], (DEPTH, D_LRU), 0.01)
    lru_gate_x_w = nrm(ks[8], (DEPTH, LRU_HEADS, LRU_HEAD_DIM, LRU_HEAD_DIM), LRU_HEAD_DIM ** -0.5)
    lru_gate_x_b = nrm(ks[9], (DEPTH, D_LRU), 0.01)
    a_c = jax.random.uniform(ks[10], (DEPTH, D_LRU), f32, minval=0.9, maxval=0.999)
    a_base = jnp.power(a_c, 1.0 / LRU_C)
    lru_a_param = jnp.log(a_base) - jnp.log1p(-a_base)
    cc_conv_w = nrm(ks[11], (DEPTH, CC_CONV_W, D_CC), CC_CONV_W ** -0.5)
    cc_conv_b = nrm(ks[12], (DEPTH, D_CC), 0.01)
    cc_ln_g = 1.0 + nrm(ks[13], (DEPTH, D_CC), 0.02)
    cc_ln_b = nrm(ks[14], (DEPTH, D_CC), 0.01)
    out_norm_lru_g = 1.0 + nrm(ks[15], (DEPTH, D_LRU), 0.02)
    out_norm_cc_g = 1.0 + nrm(ks[16], (DEPTH, D_CC), 0.02)
    w_out = nrm(ks[17], (DEPTH, D_MIX, D_MODEL), D_MIX ** -0.5)
    norm_mlp_g = 1.0 + nrm(ks[18], (DEPTH, D_MODEL), 0.02)
    w_mlp_up = nrm(ks[19], (DEPTH, D_MODEL, D_FF_3), D_MODEL ** -0.5)
    w_mlp_down = nrm(ks[20], (DEPTH, D_FF_3, D_MODEL), D_FF_3 ** -0.5)
    norm_final_g = 1.0 + nrm(ks[21], (D_MODEL,), 0.02)
    return {
        "x": x, "meta_tokens": meta_tokens, "norm_mix_g": norm_mix_g, "w_in": w_in,
        "lru_conv_w": lru_conv_w, "lru_conv_b": lru_conv_b,
        "lru_gate_a_w": lru_gate_a_w, "lru_gate_a_b": lru_gate_a_b,
        "lru_gate_x_w": lru_gate_x_w, "lru_gate_x_b": lru_gate_x_b,
        "lru_a_param": lru_a_param, "cc_conv_w": cc_conv_w, "cc_conv_b": cc_conv_b,
        "cc_ln_g": cc_ln_g, "cc_ln_b": cc_ln_b,
        "out_norm_lru_g": out_norm_lru_g, "out_norm_cc_g": out_norm_cc_g, "w_out": w_out,
        "norm_mlp_g": norm_mlp_g, "w_mlp_up": w_mlp_up, "w_mlp_down": w_mlp_down,
        "norm_final_g": norm_final_g,
    }

def third_block(x, meta_tokens, norm_mix_g, w_in, lru_conv_w, lru_conv_b, lru_gate_a_w,
              lru_gate_a_b, lru_gate_x_w, lru_gate_x_b, lru_a_param, cc_conv_w, cc_conv_b,
              cc_ln_g, cc_ln_b, out_norm_lru_g, out_norm_cc_g, w_out, norm_mlp_g,
              w_mlp_up, w_mlp_down, norm_final_g):
    B = x.shape[0]
    meta = jnp.broadcast_to(meta_tokens[None].astype(x.dtype), (B, N_META, D_MODEL))
    h = jnp.concatenate([meta, x], axis=1)

    for l in range(DEPTH):
        u = rmsnorm_3(h, norm_mix_g[l])
        proj = u @ w_in[l].astype(u.dtype)
        x_lru, g_lru, v_cc, g_cc = jnp.split(
            proj, [D_LRU, 2 * D_LRU, 2 * D_LRU + D_CC], axis=-1)

        xc = causal_depthwise_conv_3(x_lru, lru_conv_w[l], lru_conv_b[l])
        y_lru = rg_lru(xc, lru_gate_a_w[l], lru_gate_a_b[l], lru_gate_x_w[l],
                       lru_gate_x_b[l], lru_a_param[l]) * jax.nn.gelu(g_lru)

        c = v_cc * jax.nn.sigmoid(g_cc)
        c = causal_depthwise_conv_3(c, cc_conv_w[l], cc_conv_b[l])
        y_cc = jax.nn.silu(layernorm_3(c, cc_ln_g[l], cc_ln_b[l]))

        y = jnp.concatenate([rmsnorm_3(y_lru, out_norm_lru_g[l]),
                             rmsnorm_3(y_cc, out_norm_cc_g[l])], axis=-1)
        h = h + y @ w_out[l].astype(y.dtype)

        m = rmsnorm_3(h, norm_mlp_g[l]) @ w_mlp_up[l].astype(h.dtype)
        h = h + jnp.square(jax.nn.relu(m)) @ w_mlp_down[l].astype(h.dtype)

    out = rmsnorm_3(h, norm_final_g)
    return out[:, N_META:]


_first_inputs_3 = third_inputs


def third_inputs(seed=0):
    import zlib

    import numpy as np

    out = dict(_first_inputs_3(seed))
    spreads = {}
    factors = {'norm_mix_g': 2.914,
     'lru_gate_a_b': 41.134,
     'lru_gate_x_b': 37.685,
     'cc_conv_b': 5.613,
     'cc_ln_g': 63.618,
     'cc_ln_b': 131.547,
     'out_norm_lru_g': 80.359,
     'out_norm_cc_g': 73.299,
     'norm_mlp_g': 14.561,
     'norm_final_g': 21.57,
     'lru_conv_b': 3.528}
    for name, (base, spread) in spreads.items():
        noise = np.random.default_rng([zlib.crc32(name.encode()), seed]).standard_normal(out[name].shape)
        drawn = base * np.exp(spread * noise) if base else spread * noise
        out[name] = __import__('jax').numpy.asarray(drawn.astype(out[name].dtype))
    for name, factor in factors.items():
        out[name] = (out[name] * factor).astype(out[name].dtype)
    return out


_narrow_inputs_3 = third_inputs


def third_inputs(seed=0):

    out = dict(_narrow_inputs_3(seed))
    wider = {'cc_ln_g': 4.17,
     'cc_ln_b': 4.15,
     'out_norm_lru_g': 4.06,
     'out_norm_cc_g': 4.06,
     'norm_final_g': 3.14}
    for name, times in wider.items():
        mean = out[name].mean()
        out[name] = (mean + times * (out[name] - mean)).astype(out[name].dtype)
    return out


def setup_inputs(seed=0):
    out = dict(first_inputs(seed))
    for name, value in second_inputs(seed + 1).items():
        if name != "x":
            out[name + "_2"] = value
    for name, value in third_inputs(seed + 2).items():
        if name != "x":
            out[name + "_3"] = value
    return out


def reference(
    x, mem, norm_g, w_in, conv_w, conv_b, wq_m, wk_m, wv_m, w_if, b_if, mnorm_g, skip_m, lam_q1,
    lam_k1, lam_q2, lam_k2, dnorm_g, mem_norm_g, w_mem_kv, w_out, final_g, norm_mix_2, w_in_2,
    att_rel_bias_2, sgu_norm_gain_2, sgu_norm_bias_2, sgu_w_2, sgu_b_2, w_br_att_2, w_br_sgu_2,
    b_gate_2, w_out_2, norm_ffn_2, w_ffn_in_2, w_ffn_out_2, norm_final_2, meta_tokens_3,
    norm_mix_g_3, w_in_3, lru_conv_w_3, lru_conv_b_3, lru_gate_a_w_3, lru_gate_a_b_3,
    lru_gate_x_w_3, lru_gate_x_b_3, lru_a_param_3, cc_conv_w_3, cc_conv_b_3, cc_ln_g_3,
    cc_ln_b_3, out_norm_lru_g_3, out_norm_cc_g_3, w_out_3, norm_mlp_g_3, w_mlp_up_3,
    w_mlp_down_3, norm_final_g_3,
):
    x = first_block(
        x, mem, norm_g, w_in, conv_w, conv_b, wq_m, wk_m, wv_m, w_if, b_if, mnorm_g, skip_m,
        lam_q1, lam_k1, lam_q2, lam_k2, dnorm_g, mem_norm_g, w_mem_kv, w_out, final_g,
    )
    x = second_block(
        x, norm_mix_2, w_in_2, att_rel_bias_2, sgu_norm_gain_2, sgu_norm_bias_2, sgu_w_2,
        sgu_b_2, w_br_att_2, w_br_sgu_2, b_gate_2, w_out_2, norm_ffn_2, w_ffn_in_2, w_ffn_out_2,
        norm_final_2,
    )
    return third_block(
        x, meta_tokens_3, norm_mix_g_3, w_in_3, lru_conv_w_3, lru_conv_b_3, lru_gate_a_w_3,
        lru_gate_a_b_3, lru_gate_x_w_3, lru_gate_x_b_3, lru_a_param_3, cc_conv_w_3, cc_conv_b_3,
        cc_ln_g_3, cc_ln_b_3, out_norm_lru_g_3, out_norm_cc_g_3, w_out_3, norm_mlp_g_3,
        w_mlp_up_3, w_mlp_down_3, norm_final_g_3,
    )


_drawn_inputs = setup_inputs


def setup_inputs(seed=0):
    import zlib

    import numpy as np

    out = dict(_drawn_inputs(seed))
    spreads = {}
    factors = {}
    for name, (base, spread) in spreads.items():
        noise = np.random.default_rng([zlib.crc32(name.encode()), seed]).standard_normal(out[name].shape)
        drawn = base * np.exp(spread * noise) if base else spread * noise
        out[name] = __import__('jax').numpy.asarray(drawn.astype(out[name].dtype))
    for name, factor in factors.items():
        out[name] = (out[name] * factor).astype(out[name].dtype)
    return out
```

```python
import math
from contextlib import ExitStack

import concourse.bass as bass
from concourse import mybir
from concourse.alu_op_type import AluOpType as ALU

F32 = mybir.dt.float32
F32R = mybir.dt.float32r
ACT = mybir.ActivationFunctionType
AX = mybir.AxisListType.X

P = 128
D = 1024
KB = D // P
T = 1024
NT = T // P
HALF = 512
BANK = 512
QUAD = 4 * BANK
TILES = 16
SLOT = TILES * P
H1 = 4
MEM = 256
EPS = 1e-6
NEG = -1e30
LAM_INIT = 0.8 - 0.6 * math.exp(-0.3 * 0)
HEADS2 = 8
SPAN = 640
FF2 = 22
FF3 = 32
META = 16
LW = T + META
CCK = 31
LRU_HALF = 8.0 / 2


def plan(blocks):
    tiles, where = [], {}
    slot = quad = 0

    def add(name, items, quads):
        nonlocal slot, quad
        assert len(items) % TILES == 0
        where[name] = (slot, quad)
        tiles.extend(items)
        slot += len(items) // TILES
        quad += quads

    def feature(name, w, col, outs, ks=range(KB)):
        add(name, [(w, k, col + o) for o in range(outs) for k in ks], outs // 2)

    def token(name, w, col, outs):
        add(name, [(w, k, col + 2 * s + c) for s in range(outs // 2) for k in range(KB) for c in range(2)], outs // 2)

    if 1 in blocks:
        feature("x_m", "w_in", 0, 4)
        token("o_m", "w_in", 4, 4)
        feature("q_d", "w_in", 12, 4)
        feature("k_d", "w_in", 16, 4)
        token("v_d", "w_in", 20, 4)
        feature("mem_k", "w_mem_kv", 0, 4)
        token("mem_v", "w_mem_kv", 4, 4)
        feature("q_c", "w_in", 28, 4)
        feature("z_m", "w_in", 8, 4)
        feature("z_d", "w_in", 24, 4)
        feature("z_c", "w_in", 32, 4)
        feature("out_1", "w_out", 0, 8, range(12))
    if 2 in blocks:
        feature("q_2", "w_in_2", 0, 4)
        feature("k_2", "w_in_2", 4, 4)
        token("v_2", "w_in_2", 8, 4)
        for branch, gate, w in ((0, 20, "w_br_att_2"), (1, 28, "w_br_sgu_2")):
            if branch == 1:
                token("vs_2", "w_in_2", 16, 4)
                feature("u_2", "w_in_2", 12, 4)
            for pair in range(2):
                feature(f"gate_{branch}{pair}", "w_in_2", gate + 4 * pair, 4)
                feature(f"branch_{branch}{pair}", w, 4 * pair, 4, range(4))
        feature("out_2", "w_out_2", 0, 8)
        for g in range(0, FF2, 4):
            n = min(4, FF2 - g)
            add(f"up_2_{g // 4}", [("w_ffn_in_2", k, (0, FF2)[o] + g + j) for j in range(n) for o in range(2) for k in range(KB)], n)
            feature(f"down_2_{g // 4}", "w_ffn_out_2", 0, 8, range(g, g + n))
    if 3 in blocks:
        for name, col in (("x_lru", 0), ("v_cc", 8), ("g_cc", 12), ("g_lru", 4)):
            add(name, [("w_in_3", k, col + o) for o in range(4) for k in range(KB)], 4)
        feature("out_3", "w_out_3", 0, 8)
        for g in range(FF3 // 4):
            feature(f"up_3_{g}", "w_mlp_up_3", 4 * g, 4)
            feature(f"down_3_{g}", "w_mlp_down_3", 0, 8, range(4 * g, 4 * g + 4))
    return tiles, where


PARAMS = {}


def param_columns():
    at = 0
    for name, n in (("norm_g", 8), ("conv_w", 16), ("conv_b", 4), ("mnorm_g", 4), ("skip_m", 4), ("dnorm_g", 4),
                    ("mem_norm_g", 8), ("final_g", 8), ("norm_mix_2", 8), ("b_gate_2", 16), ("norm_ffn_2", 8),
                    ("norm_final_2", 8), ("norm_mix_g_3", 8), ("lru_conv_w_3", 16), ("lru_conv_b_3", 4),
                    ("lru_gate_a_b_3", 4), ("lru_gate_x_b_3", 4), ("lru_a_param_3", 4), ("cc_conv_w_3", 4 * CCK),
                    ("cc_conv_b_3", 4), ("cc_ln_g_3", 4), ("cc_ln_b_3", 4), ("out_norm_lru_g_3", 4),
                    ("out_norm_cc_g_3", 4), ("norm_mlp_g_3", 8), ("norm_final_g_3", 8), ("b_if", 1), ("lam", 256),
                    ("w_if", 12 * 36), ("ident", 128), ("ones", 128), ("mask_ts", 128), ("mask_qk", 128), ("eps", 1)):
        PARAMS[name] = (at, n)
        at += n
    return at


NPARAM = param_columns()


class Line:

    def __init__(self, eng, sem):
        self.eng, self.sem, self.n = eng, sem, 0

    def step(self, ins):
        ins.then_inc(self.sem, 1)
        self.n += 1
        return self.n

    def wait(self, n=None):
        self.eng.wait_ge(self.sem, self.n if n is None else n)


def wait(eng, sem, n):
    if isinstance(n, int) and n <= 0:
        return
    eng.wait_ge(sem, n)


def up(base, loop):
    return base if loop is None else loop[0] * loop[1] + base

BLOCKS = (1,2,3,)


def build(nc, xT, memT, stream, params, wqkv, sgu, bias2, lru_w, metaT, outT, o_scr, h_scr, blocks=(1, 2, 3)):
    TL, WH = plan(blocks)
    NSLOT = len(TL) // TILES
    with ExitStack() as ctx:
        sems = {}

        def S(name):
            if name not in sems:
                sems[name] = ctx.enter_context(nc.semaphore(name))
            return sems[name]

        base = -(-nc.sbuf_base // 32) * 32

        def at(name, offset, shape, dt=F32):
            return nc.alloc_sbuf_tensor_at(name, shape, dt, offset=base + offset)

        ps = ctx.enter_context(nc.psum_tensor("ps", [P, 8 * BANK], F32))

        RAW = at("raw", 0, [P, 2, TILES, P])
        WHI = at("whi", 16384, [P, 2, TILES, P], F32R)
        WLO = at("wlo", 32768, [P, 2, TILES, P], F32R)
        X = 49152
        XHI = at("xhi", X, [P, KB, T], F32R)
        XLO = at("xlo", X + 32768, [P, KB, T], F32R)
        C = X + 66560
        PAR = at("par", C, [P, NPARAM])
        A = C + 8704
        small_at = [C + -(-4 * NPARAM // 32) * 32]

        def small(name, shape):
            offset = small_at[0]
            small_at[0] += -(-4 * math.prod(shape[1:]) // 32) * 32
            assert small_at[0] <= A
            return at(name, offset, shape)

        def par(name, j=0, n=1, rows=slice(0, P)):
            return PAR[rows, PARAMS[name][0] + j:PARAMS[name][0] + j + n]

        H = at("h1", A, [P, KB, T])

        IDENT, ONES = par("ident", 0, P), par("ones", 0, P)
        EPSC = par("eps")

        def half(quad, ob):
            c = QUAD * (quad % 2) + 2 * BANK * ob
            return ps[:, c:c + 2 * BANK]

        def free(quad):
            return S(f"quad_free{quad % 2}")

        def freed(quad, ob, loop=None):
            return up(2 * (quad // 2) + ob + 1, loop)

        quad_ready, split_done, slot_used, hi_done = S("quad_ready"), S("split_done"), S("slot_used"), S("hi_done")
        raw_loaded = [S("raw_loaded0"), S("raw_loaded1")]

        norm_counts = dict(sq=0, add=0, sum=0, root=0, recip=0, x=0, hi=0, lo=0)

        def norm_set(name, src, n, gain, scr, nb=KB, hi=None, lo=None, out=None):
            N = dict(src=src, n=n, gain=gain, nb=nb, hi=hi, lo=lo, out=out, before=dict(norm_counts),
                     sq=at(f"{name}_sq", scr, [P, 2, n]), acc=at(f"{name}_acc", scr + 8 * n, [P, n]),
                     inv=at(f"{name}_inv", scr + 12 * n, [P, n]))
            applied = nb if gain else 0
            cut = nb if hi else 0
            for step, k in (("sq", nb), ("add", nb - 1), ("sum", 1), ("root", 1), ("recip", min(applied, 1)),
                            ("x", applied), ("hi", cut), ("lo", cut)):
                norm_counts[step] += k
            return N

        def of(N, step, n):
            return S("norm_" + step), N["before"][step] + n

        def norm_square(act, N, b):
            if b >= 2:
                act.wait_ge(*of(N, "add", b - 1))
            dst = N["acc"][:, :] if b == 0 else N["sq"][:, b % 2, :]
            nc.scalar.activation(dst, N["src"](b), ACT.Square).then_inc(S("norm_sq"), 1)

        def norm_add(dve, N, b):
            if b == 0:
                return
            dve.wait_ge(*of(N, "sq", b + 1))
            if b >= 2:
                dve.wait_ge(*of(N, "add", b - 1))
            nc.vector.tensor_tensor(N["acc"][:, :], N["acc"][:, :], N["sq"][:, b % 2, :], ALU.add)\
                .then_inc(S("norm_add"), 1)

        def norm_sum(pe, N):
            pe.wait_ge(*of(N, "add", N["nb"] - 1))
            for c in range(0, N["n"], HALF):
                w = min(HALF, N["n"] - c)
                mm = nc.tensor.matmul(ps[:, c:c + w], ONES, N["acc"][:, c:c + w], start=True, stop=True)
            mm.then_inc(S("norm_sum"), 1)

        def norm_root(act, N):
            act.wait_ge(*of(N, "sum", 1))
            nc.scalar.activation(N["inv"][:, :], ps[:, 0:N["n"]], ACT.Sqrt, bias=EPSC,
                                 scale=1.0 / (N["nb"] * P)).then_inc(S("norm_root"), 1)

        def norm_apply(dve, N):
            dve.wait_ge(*of(N, "root", 1))
            nc.vector.reciprocal(N["inv"][:, :], N["inv"][:, :]).then_inc(S("norm_recip"), 1)
            dve.wait_ge(*of(N, "recip", 1))
            for b in range(N["nb"] + 1):
                if b < N["nb"]:
                    dst = N["out"](b) if N["out"] else N["sq"][:, b % 2, :]
                    if not N["out"] and b >= 2:
                        dve.wait_ge(*of(N, "lo", b - 1))
                    nc.vector.scalar_tensor_tensor(dst, N["src"](b), N["gain"](b), N["inv"][:, :], ALU.mult, ALU.mult)\
                        .then_inc(S("norm_x"), 1)
                if b >= 1 and not N["out"]:
                    dve.wait_ge(*of(N, "hi", b))
                    nc.vector.tensor_tensor(N["lo"](b - 1), N["sq"][:, (b - 1) % 2, :], N["hi"](b - 1).bitcast(F32),
                                            ALU.subtract).then_inc(S("norm_lo"), 1)

        def norm_hi(act, N):
            for b in range(N["nb"]):
                act.wait_ge(*of(N, "x", b + 1))
                nc.scalar.activation(N["hi"](b), N["sq"][:, b % 2, :], ACT.Copy).then_inc(S("norm_hi"), 1)

        def slot_start(pe, slot, loop):
            pe.wait_ge(split_done, up(slot + 1, loop))

        def quad_start(pe, quad, loop=None):
            n = 2 * (quad // 2)
            if loop is not None or n > 0:
                pe.wait_ge(free(quad), up(n, loop))

        def feature_tiles(pe, where, outs, ks, xhi, xlo, chunks=((0, HALF, 0), (HALF, HALF, BANK)), ready=None,
                          qloop=None, sloop=None, o_per_quad=2):
            slot, quad = where
            t = 0
            for o in range(outs):
                q = quad + o // o_per_quad
                if o % o_per_quad == 0:
                    quad_start(pe, q, qloop)
                c0 = QUAD * (q % 2) + 2 * BANK * (o % o_per_quad)
                for n, k in enumerate(ks):
                    s, r = slot + t // TILES, (slot + t // TILES) % 2
                    first = t % TILES == 0
                    if first:
                        slot_start(pe, s, sloop)
                    if ready and o == 0:
                        pe.wait_ge(*ready(n))
                    w_hi, w_lo = WHI[:, r, t % TILES, :], WLO[:, r, t % TILES, :]
                    for m, (w, x) in enumerate(((w_hi, xhi), (w_hi, xlo), (w_lo, xhi))):
                        for a, width, c in chunks:
                            mm = nc.tensor.matmul(ps[:, c0 + c:c0 + c + width], w, x(k, a, width),
                                                  start=(n == 0 and m == 0), stop=(n == len(ks) - 1 and m == 2))
                            if first and (s > 0 or sloop is not None):
                                mm.then_inc(slot_used, 1)
                            first = False
                    t += 1
                if o % o_per_quad == o_per_quad - 1:
                    mm.then_inc(quad_ready, 1)

        def token_tiles(pe, where, slots, xhi, xlo, nt=NT, ready=None):
            slot, quad = where
            for i in range(slots):
                s, q = slot + i, quad + i
                r = s % 2
                quad_start(pe, q)
                slot_start(pe, s, None)
                first = s > 0
                for tt in range(nt):
                    c = QUAD * (q % 2) + 256 * tt
                    for k in range(KB):
                        if ready and i == 0 and tt == 0:
                            pe.wait_ge(*ready(k))
                        w_hi = WHI[:, r, 2 * k:2 * k + 2, :].rearrange("p a b -> p (a b)")
                        w_lo = WLO[:, r, 2 * k:2 * k + 2, :].rearrange("p a b -> p (a b)")
                        a = tt * P
                        for m, (x, w) in enumerate(((xhi, w_hi), (xhi, w_lo), (xlo, w_hi))):
                            mm = nc.tensor.matmul(ps[:, c:c + 256], x(k, a, P), w, start=(k == 0 and m == 0),
                                                  stop=(k == KB - 1 and m == 2))
                            if first:
                                mm.then_inc(slot_used, 1)
                            first = False
                mm.then_inc(quad_ready, 1)

        xhi = lambda k, a, w: XHI[:, k, a:a + w]
        xlo = lambda k, a, w: XLO[:, k, a:a + w]

        block = ctx.enter_context(nc.Block())

        @block.sync
        def _(sp):
            def load(s, r, loop):
                sp.dma_start(RAW[:, r], stream[s].rearrange("p (t c) -> p t c", c=P)).then_inc(raw_loaded[r], 16)

            load(0, 0, None)
            load(1, 1, None)
            with sp.Fori(1, NSLOT // 2) as i:
                for r in range(2):
                    sp.wait_ge(split_done, i * 2 + (r - 1))
                    sp.dma_start(RAW[:, r], stream[bass.ds(i * 2 + r, 1)].rearrange("s p (t c) -> p (s t) c", c=P))\
                        .then_inc(raw_loaded[r], 16)
            if NSLOT % 2:
                sp.wait_ge(split_done, NSLOT - 2)
                load(NSLOT - 1, 0, None)

        @block.gpsimd
        def _(pool):
            def split(r, loads, done, used):
                pool.wait_ge(raw_loaded[r], loads)
                if used is not None:
                    pool.wait_ge(slot_used, used)
                flat = lambda x: x[:, r].rearrange("p t c -> p (t c)")
                one = par("ones").to_broadcast([P, SLOT])
                nc.gpsimd.tensor_tensor(flat(WHI), flat(RAW), one, ALU.mult).then_inc(hi_done, 1)
                pool.wait_ge(hi_done, done)
                nc.gpsimd.tensor_tensor(WLO[:, r], RAW[:, r], WHI[:, r].bitcast(F32), ALU.subtract)\
                    .then_inc(split_done, 1)

            pool.wait_ge(S("par_loaded"), 16)
            split(0, 16, 1, None)
            split(1, 16, 2, None)
            with pool.Fori(1, NSLOT // 2) as i:
                for r in range(2):
                    split(r, i * 16 + 16, i * 2 + (r + 1), i * 2 + (r - 1))
            if NSLOT % 2:
                split(0, 16 * (NSLOT // 2 + 1), NSLOT, NSLOT - 2)

        if 1 in blocks:
            XS = at("x_in", A, [P, KB, T])
            NRM1 = norm_set("n1", lambda b: XS[:, b, :], T, lambda b: par("norm_g", b), A + 32768,
                            hi=lambda b: XHI[:, b, :], lo=lambda b: XLO[:, b, :])
            PR = at("pre", A, [P, 12, T])
            XCV = PR[:, 0:4, :]
            QT = at("q_t", A + 16384, [P, H1, T])
            KT = at("k_t", A + 32768, [P, H1, T])
            OSTG = at("o_staged", A + 16384, [P, 2, NT, 256])
            V1 = at("v_one", A + 49152, [P, NT, H1, P + 1])
            XM_AT = A + 65664
            XM = at("x_m", XM_AT, [P, H1, T + 3])
            WQKV = at("w_qkv", XM_AT + 16448, [P, 3, H1, P])
            R1 = at("row_1", XM_AT, [4, T])
            R4 = at("row_4", XM_AT + 4096, [4, T])
            R0 = at("row_0", XM_AT + 8192, [4, T])
            R2 = at("row_2", XM_AT + 12288, [4, T])
            R3 = at("row_3", XM_AT + 16384, [4, T])
            CH = XM_AT + 8192
            EW = at("e_w", CH, [P, H1, P])
            QS = at("q_s", CH + 2048, [P, H1, P])
            KW = at("k_w", CH + 4096, [P, H1, P])
            HN = at("h_n", CH + 6144, [P, H1, P])
            OSC = at("o_sig", CH + 8192, [P, 2, HALF])
            CS = at("c_state", CH + 12288, [P, H1, P + 1])
            COL = small("cols", [P, NT, 12])
            MPREV = small("m_prev", [4, NT])
            DEC = small("decay", [P, 4])
            DN = small("denom", [P, 4])
            ST = small("stats", [P, 4, 6])
            MV = small("mean_var", [P, 4, 2])
            SD = small("std", [P, 4])
            LM = small("lam", [P, 4])
            GD = small("g_d", [P, 4])
            SM = small("soft", [P, 4, 8])
            OS1 = small("o_stat", [P, 4, 2])
            SMC = small("soft_c", [P, 2, 12])
            LTMP = at("lam_tmp", A + 86016, [P, 64])

            KD = KT
            VD = at("v_d", A + 49152, [P, NT, HALF])
            P0 = [at("p0_0", A + 65536, [P, 896]), at("p0_1", A + 69120, [P, T])]
            P1 = [at("p1_0", A + 73216, [P, 896]), at("p1_1", A + 76800, [P, T])]
            PTD = at("p_t", A + 80896, [P, T])
            ON = at("o_n", A + 84992, [P, 2, P])

            KM = at("k_mem", A + 49152, [P, H1, MEM])
            VM = at("v_mem", A + 53248, [P, 2, HALF])
            MXH = at("mem_hi", A + 57344, [P, KB, MEM], F32R)
            MXL = at("mem_lo", A + 65536, [P, KB, MEM], F32R)
            MS = at("mem_in", A + 73728, [P, KB, MEM])
            NRMM = norm_set("nm", lambda b: MS[:, b, :], MEM, lambda b: par("mem_norm_g", b), A + 81920,
                            hi=lambda b: MXH[:, b, :], lo=lambda b: MXL[:, b, :])
            mhi = lambda k, a, w: MXH[:, k, a:a + w]
            mlo = lambda k, a, w: MXL[:, k, a:a + w]
            QC = PR[:, 8:12, :]
            PC = at("p_c", A + 57344, [P, 2, H1 * MEM])
            PTC = at("p_ct", A + 65536, [P, 2 * H1 * P])

            YH = at("y_hi", A + 49152, [P, 8, T], F32R)
            YHC = at("y_hi_c", X, [P, 4, T], F32R)
            YL = at("y_lo", A, [P, 12, T], F32R)
            SIL = at("silu_z", A + 81920, [P, T])
            yhi = lambda k, a, w: YH[:, k, a:a + w] if k < 8 else YHC[:, k - 8, a:a + w]
            ylo = lambda k, a, w: YL[:, k, a:a + w]
            HX = at("x_again", X + 16384, [P, KB, T])
            NRMF = norm_set("nf", lambda b: HX[:, b, :], T, lambda b: par("final_g", b), X + 49152,
                            out=lambda b: H[:, b, :])
            STEPS = [(h, j) for h in range(H1) for j in range(NT)]
            SC1 = float(P) ** -0.5
            SCD = 64.0 ** -0.5

        def num(h):
            c = BANK * (4 + h // 2) + (P + 1) * (h % 2)
            return ps[:, c:c + P + 1]

        def cup(h):
            c = BANK * (6 + h // 2) + (P + 1) * (h % 2)
            return ps[:, c:c + P + 1]

        def work(n):
            return 2 * BANK + 2 * BANK * (n % 2)

        def pe_block1(pe):
            pe.wait_ge(S("par_loaded"), 16)
            norm_sum(pe, NRM1)
            feature_tiles(pe, WH["x_m"], 4, range(KB), xhi, xlo, ready=lambda n: of(NRM1, "lo", n + 1))
            token_tiles(pe, WH["o_m"], 2, xhi, xlo)
            pe.wait_ge(S("wqkv_loaded"), 16)
            for q in WH["o_m"][1], WH["o_m"][1] + 1:
                quad_start(pe, q + 2)
            for n in range(13):
                if n < 12:
                    h = n % 4
                    kind = n // 4
                    if kind == 1:
                        pe.wait_ge(S("silu_done"), h + 1)
                    wait(pe, S("qkv_kept"), n - 1)
                    for c in range(2):
                        x = XM[:, h, 3 + HALF * c:3 + HALF * (c + 1)] if kind == 0 else XCV[:, h, HALF * c:HALF * (c + 1)]
                        mm = nc.tensor.matmul(ps[:, work(n) + HALF * c:work(n) + HALF * (c + 1)],
                                              WQKV[:, (2, 0, 1)[kind], h, :], x, start=True, stop=True)
                    mm.then_inc(S("qkv_ready"), 1)
                if n >= 1:
                    m = n - 1
                    src = KT[:, m % 2, :] if m < 4 else (QT if m < 8 else KT)[:, m % 4, :]
                    blk = (8, 0, 4)[m // 4] + m % 4
                    pe.wait_ge(S("qkv_kept"), m + 1)
                    for c in range(2):
                        mm = nc.tensor.matmul(ps[0:36, HALF * c:HALF * (c + 1)], par("w_if", 36 * blk, 36),
                                              src[:, HALF * c:HALF * (c + 1)], start=(m == 0), stop=(m == 11))
                    mm.then_inc(S("gate_sum"), 1)
                if n == 3:
                    for tt in range(NT):
                        wait(pe, S("vt_kept"), tt - 1)
                        for g in range(H1):
                            c = BANK * (6 + tt % 2) + P * g
                            mm = nc.tensor.matmul(ps[:, c:c + P], XM[:, g, 3 + P * tt:3 + P * (tt + 1)], WQKV[:, 2, g, :],
                                                  start=True, stop=True)
                        mm.then_inc(S("vt_ready"), 1)
            pe.wait_ge(S("rows_a"), 6)
            for c in range(NT):
                for n, row in enumerate((R3, R0, R2)):
                    a = 2 * BANK + 12 * c + 4 * n
                    mm = nc.tensor.transpose(ps[:, a:a + 4], row[:, P * c:P * (c + 1)], IDENT[0:4, 0:4])
            mm.then_inc(S("cols_ready"), 1)
            pe.wait_ge(S("rows_v"), 13)
            pe.wait_ge(S("cols_kept"), 1)
            for c in range(NT):
                wait(pe, S("pre_done"), c)
                for h in range(H1):
                    sel = IDENT[0:4, h:h + 1].to_broadcast([4, P])
                    nc.tensor.matmul(ps[:, P * h:P * (h + 1)], sel, R4[:, P * c:P * (c + 1)], start=True, stop=True)
                for h in range(H1):
                    sel = IDENT[0:4, h:h + 1].to_broadcast([4, P])
                    mm = nc.tensor.matmul(ps[:, BANK + P * h:BANK + P * (h + 1)], sel, R1[:, P * c:P * (c + 1)],
                                          start=True, stop=True)
                mm.then_inc(S("bc_ready"), 1)
                for h in range(H1):
                    mm = nc.tensor.matmul(ps[:, 2 * BANK + P * h:2 * BANK + P * (h + 1)], KT[:, h, P * c:P * (c + 1)],
                                          QT[:, h, P * c:P * (c + 1)], start=True, stop=True)
                mm.then_inc(S("sc_ready"), 1)
                for h in range(H1):
                    mm = nc.tensor.transpose(ps[:, 3 * BANK + P * h:3 * BANK + P * (h + 1)], KT[:, h, P * c:P * (c + 1)], IDENT)
                mm.then_inc(S("kt_ready"), 1)
                pe.wait_ge(S("pt_done"), c + 1)
                wait(pe, S("c_done"), c)
                for h in range(H1):
                    mm = nc.tensor.matmul(num(h), EW[:, h, :], V1[:, c, h, :], start=True, stop=(c == 0))
                    if c:
                        mm = nc.tensor.matmul(num(h), QS[:, h, :], CS[:, h, :], start=False, stop=True)
                mm.then_inc(S("num_ready"), 1)
                for h in range(H1):
                    mm = nc.tensor.matmul(cup(h), KW[:, h, :], V1[:, c, h, :], start=True, stop=True)
                mm.then_inc(S("cu_ready"), 1)
                pe.wait_ge(S("hn_done"), c + 1)
                for h in range(H1):
                    mm = nc.tensor.transpose(ps[:, P * h:P * (h + 1)], HN[:, h, :], IDENT)
                mm.then_inc(S("ht_ready"), 1)
            pe.wait_ge(S("pre_done"), NT)

            feature_tiles(pe, WH["q_d"], 4, range(KB), xhi, xlo)
            feature_tiles(pe, WH["k_d"], 4, range(KB), xhi, xlo)
            token_tiles(pe, WH["v_d"], 2, xhi, xlo)
            last = WH["v_d"][1] + 1
            quad_start(pe, last + 1)
            quad_start(pe, last + 2)
            n_steps = len(STEPS)
            for i in range(n_steps + 2):
                if i < n_steps:
                    h, j = STEPS[i]
                    wait(pe, S("d_exp"), 2 * i)
                    for m in range(2):
                        rows = slice(64 * m, 64 * m + 64)
                        n = P * (j + 1)
                        for c in range(0, n, HALF):
                            w = min(HALF, n - c)
                            diag = c + w == n
                            mm = nc.tensor.matmul(ps[:, 2 * BANK * m + c:2 * BANK * m + c + w], QT[rows, h, P * j:P * (j + 1)],
                                                  KD[rows, h, c:c + w], start=True, stop=not diag)
                            if diag:
                                e = 2 * BANK * m + n - P
                                mm = nc.tensor.matmul(ps[:, e:e + P], IDENT, par("mask_qk", 0, P), start=False, stop=True)
                        mm.then_inc(S("d_scores"), 1)
                if 1 <= i <= n_steps:
                    s, (h, j) = i - 1, STEPS[i - 1]
                    pe.wait_ge(S("d_p"), s + 1)
                    wait(pe, S("d_ptk"), s)
                    for k in range(j + 1):
                        mm = nc.tensor.transpose(ps[:, 4 * BANK + P * k:4 * BANK + P * (k + 1)],
                                                 P0[s % 2][:, P * k:P * (k + 1)], IDENT)
                    mm.then_inc(S("d_pt"), 1)
                    pe.wait_ge(S("d_ptk"), s + 1)
                    wait(pe, S("d_on"), s)
                    for k in range(j + 1):
                        mm = nc.tensor.matmul(ps[:, 6 * BANK:6 * BANK + P], PTD[:, P * k:P * (k + 1)],
                                              VD[:, k, P * h:P * (h + 1)], start=(k == 0), stop=(k == j))
                    mm.then_inc(S("d_o"), 1)
                if i >= 2:
                    s = i - 2
                    pe.wait_ge(S("d_on"), s + 1)
                    wait(pe, S("d_od"), s)
                    nc.tensor.transpose(ps[:, 7 * BANK:7 * BANK + P], ON[:, s % 2, :], IDENT).then_inc(S("d_ot"), 1)
            pe.wait_ge(S("d_od"), n_steps)
            pe.wait_ge(S("d_ptk"), n_steps)

            norm_sum(pe, NRMM)
            mem_chunk = ((0, MEM, 0),)
            feature_tiles(pe, WH["mem_k"], 4, range(KB), mhi, mlo, chunks=mem_chunk, ready=lambda n: of(NRMM, "lo", n + 1))
            token_tiles(pe, WH["mem_v"], 2, mhi, mlo, nt=2)
            feature_tiles(pe, WH["q_c"], 4, range(KB), xhi, xlo)
            last = WH["q_c"][1] + 1
            quad_start(pe, last + 1)
            quad_start(pe, last + 2)
            for j in range(NT + 1):
                if j < NT:
                    wait(pe, S("c_exp"), j)
                    for h in range(H1):
                        mm = nc.tensor.matmul(ps[:, MEM * h:MEM * (h + 1)], QC[:, h, P * j:P * (j + 1)], KM[:, h, :],
                                              start=True, stop=True)
                    mm.then_inc(S("c_scores"), 1)
                if j >= 1:
                    s = j - 1
                    pe.wait_ge(S("c_p"), s + 1)
                    wait(pe, S("c_ptk"), s)
                    for n in range(2 * H1):
                        mm = nc.tensor.transpose(ps[:, 2 * BANK + P * n:2 * BANK + P * (n + 1)],
                                                 PC[:, s % 2, P * n:P * (n + 1)], IDENT)
                    mm.then_inc(S("c_pt"), 1)
                    pe.wait_ge(S("c_ptk"), s + 1)
                    wait(pe, S("c_oc"), s)
                    for h in range(H1):
                        for m in range(2):
                            mm = nc.tensor.matmul(ps[:, 4 * BANK + P * h:4 * BANK + P * (h + 1)], VM[:, m, P * h:P * (h + 1)],
                                                  PTC[:, P * (2 * h + m):P * (2 * h + m + 1)], start=(m == 0), stop=(m == 1))
                    mm.then_inc(S("c_o"), 1)
            pe.wait_ge(S("c_oc"), NT)

            for z in ("z_m", "z_d", "z_c"):
                feature_tiles(pe, WH[z], 4, range(KB), xhi, xlo)
            feature_tiles(pe, WH["out_1"], 8, range(12), yhi, ylo, ready=lambda n: (S("y_lo"), n + 1))
            norm_sum(pe, NRMF)

        def act_block1(act):
            for b in range(0, KB, 2):
                act.dma_start(XS[:, b:b + 2, :], xT[P * b:P * (b + 2), :].rearrange("(b p) t -> p b t", p=P))\
                    .then_inc(S(f"x_in{b // 2}"), 16)
            act.dma_start(WQKV[:, :, :, :].rearrange("p a h c -> p (a h c)"), wqkv).then_inc(S("wqkv_loaded"), 16)
            act.wait_ge(S("par_loaded"), 16)
            for b in range(KB):
                act.wait_ge(S(f"x_in{b // 2}"), 16)
                norm_square(act, NRM1, b)
            norm_root(act, NRM1)
            norm_hi(act, NRM1)
            q0 = WH["x_m"][1]
            for b in range(4):
                q = q0 + b // 2
                act.wait_ge(quad_ready, q + 1)
                nc.scalar.activation(XM[:, b, 3:3 + T], half(q, b % 2), ACT.Copy).then_inc(free(q), 1)
            q0 = WH["o_m"][1]
            for s in range(2):
                q = q0 + s
                act.wait_ge(quad_ready, q + 1)
                for ob in range(2):
                    dst = OSTG[:, s, 4 * ob:4 * ob + 4, :].rearrange("p t c -> p (t c)")
                    nc.scalar.activation(dst, half(q, ob), ACT.Sigmoid).then_inc(free(q), 1)
            for s in range(2):
                act.wait_ge(free(q0 + s), freed(q0 + s, 1))
                act.dma_start(o_scr.rearrange("t p c -> p t c")[:, :, 256 * s:256 * (s + 1)], OSTG[:, s])\
                    .then_inc(S("o_stored"), 16)
            for n in range(12):
                act.wait_ge(S("qkv_ready"), n + 1)
                if n == 4:
                    act.wait_ge(S("o_stored"), 32)
                if n in (2, 3):
                    act.wait_ge(S("gate_sum"), n - 1)
                if n == 8:
                    act.wait_ge(S("gate_sum"), 4)
                dst = KT[:, n % 2, :] if n < 4 else (QT if n < 8 else KT)[:, n % 4, :]
                nc.scalar.activation(dst, ps[:, work(n):work(n) + 2 * BANK], ACT.Copy).then_inc(S("qkv_kept"), 1)
                if n == 3:
                    act.wait_ge(S("ones_set"), 1)
                    for tt in range(NT):
                        act.wait_ge(S("vt_ready"), tt + 1)
                        c = BANK * (6 + tt % 2)
                        nc.scalar.activation(V1[:, tt, :, 0:P], ps[:, c:c + BANK].rearrange("p (h d) -> p h d", h=H1),
                                             ACT.Copy).then_inc(S("vt_kept"), 1)
                    for b in range(4):
                        act.wait_ge(S("conv_done"), 4 * (b + 1))
                        nc.scalar.activation(XCV[:, b, :], XCV[:, b, :], ACT.Silu).then_inc(S("silu_done"), 1)
            for b in range(4):
                nc.scalar.activation(XCV[:, b, :], XCV[:, b, :], ACT.Copy, scale=par("skip_m", b)).then_inc(S("skip_done"), 1)
            act.wait_ge(S("rows_v"), 1)
            bf = par("b_if", rows=slice(32, 36))
            nc.scalar.activation(R1[:, :], ps[32:36, 0:T], ACT.Abs, bias=bf).then_inc(S("rows_a"), 1)
            act.wait_ge(S("rows_a"), 1)
            nc.scalar.activation(R1[:, :], R1[:, :], ACT.Exp, scale=-1.0).then_inc(S("rows_a"), 1)
            act.wait_ge(S("rows_a"), 2)
            nc.scalar.activation(R1[:, :], R1[:, :], ACT.Ln, bias=1.0).then_inc(S("rows_a"), 1)
            for n, (row, scale, need) in enumerate(((R4, 1.0, 10), (R2, -1.0, 11), (R0, 1.0, 12))):
                act.wait_ge(S("rows_v"), need)
                nc.scalar.activation(row[:, :], row[:, :], ACT.Exp, scale=scale).then_inc(S("rows_a"), 1)
            act.wait_ge(S("cols_ready"), 1)
            for c in range(NT):
                wait(act, S("h_done"), c - 1)
                act.dma_start(OSC[:, c % 2, :], o_scr[c]).then_inc(S(f"o_back{c % 2}"), 16)
                act.wait_ge(S("e_done"), c + 1)
                nc.scalar.activation(EW[:, :, :], EW[:, :, :], ACT.Exp).then_inc(S("w_exp"), 1)
                act.wait_ge(S("mv_done"), c + 1)
                nc.scalar.activation(SD[:, :], MV[:, :, 1], ACT.Sqrt, bias=EPSC).then_inc(S("sd_done"), 1)

            for name, dst in (("q_d", QT), ("k_d", KD)):
                q0 = WH[name][1]
                for b in range(4):
                    q = q0 + b // 2
                    act.wait_ge(quad_ready, q + 1)
                    nc.scalar.activation(dst[:, b, :], half(q, b % 2), ACT.Copy).then_inc(free(q), 1)
            q0 = WH["v_d"][1]
            for s in range(2):
                act.wait_ge(quad_ready, q0 + s + 1)
                for ob in range(2):
                    nc.scalar.activation(VD[:, 4 * ob:4 * ob + 4, 256 * s:256 * (s + 1)],
                                         half(q0 + s, ob).rearrange("p (t c) -> p t c", t=4), ACT.Copy).then_inc(free(q0 + s), 1)
            act.wait_ge(S("lam_v"), 2)
            nc.scalar.activation(LM[:, 0:2], LM[:, 0:2], ACT.Exp).then_inc(S("lam_a"), 1)
            n_steps = len(STEPS)
            for i in range(n_steps + 2):
                if i < n_steps:
                    n = P * (STEPS[i][1] + 1)
                    act.wait_ge(S("d_nm"), i + 1)
                    for m, buf in enumerate((P0[i % 2], P1[i % 2])):
                        nc.scalar.activation(buf[:, 0:n], ps[:, 2 * BANK * m:2 * BANK * m + n], ACT.Exp,
                                             bias=SM[:, i % 4, 2 + m:3 + m], scale=SCD,
                                             accum_out=SM[:, i % 4, 4 + m:5 + m]).then_inc(S("d_exp"), 1)
                if 1 <= i <= n_steps:
                    s, (h, j) = i - 1, STEPS[i - 1]
                    n = P * (j + 1)
                    act.wait_ge(S("d_pt"), s + 1)
                    wait(act, S("d_o"), s)
                    nc.scalar.activation(PTD[:, 0:n], ps[:, 4 * BANK:4 * BANK + n], ACT.Copy).then_inc(S("d_ptk"), 1)
                    act.wait_ge(S("d_o"), s + 1)
                    wait(act, S("d_on"), s - 1)
                    nc.scalar.activation(ON[:, s % 2, :], ps[:, 6 * BANK:6 * BANK + P], ACT.Square,
                                         accum_out=OS1[:, s % 4, 0:1]).then_inc(S("d_sq"), 1)
                    act.wait_ge(S("d_sq"), s + 1)
                    nc.scalar.activation(OS1[:, s % 4, 1:2], OS1[:, s % 4, 0:1], ACT.Sqrt, bias=EPSC, scale=1.0 / P)\
                        .then_inc(S("d_sd"), 1)
                if i >= 2:
                    s, (h, j) = i - 2, STEPS[i - 2]
                    act.wait_ge(S("d_ot"), s + 1)
                    nc.scalar.activation(PR[:, 4 + h, P * j:P * (j + 1)], ps[:, 7 * BANK:7 * BANK + P], ACT.Copy,
                                         scale=GD[:, h:h + 1]).then_inc(S("d_od"), 1)
            act.dma_start(MS[:, :, :], memT.rearrange("(b p) t -> p b t", p=P)).then_inc(S("mem_in"), 16)
            act.wait_ge(S("mem_in"), 16)
            for b in range(KB):
                norm_square(act, NRMM, b)
            norm_root(act, NRMM)
            norm_hi(act, NRMM)
            q0 = WH["mem_k"][1]
            for b in range(4):
                q = q0 + b // 2
                act.wait_ge(quad_ready, q + 1)
                nc.scalar.activation(KM[:, b, :], half(q, b % 2)[:, 0:MEM], ACT.Copy).then_inc(free(q), 1)
            q0 = WH["mem_v"][1]
            for s in range(2):
                act.wait_ge(quad_ready, q0 + s + 1)
                nc.scalar.activation(VM[:, :, 256 * s:256 * (s + 1)],
                                     half(q0 + s, 0)[:, 0:512].rearrange("p (t c) -> p t c", t=2), ACT.Copy).then_inc(free(q0 + s), 2)
            q0 = WH["q_c"][1]
            for b in range(4):
                q = q0 + b // 2
                act.wait_ge(quad_ready, q + 1)
                nc.scalar.activation(QC[:, b, :], half(q, b % 2), ACT.Copy).then_inc(free(q), 1)
            for j in range(NT + 1):
                if j < NT:
                    act.wait_ge(S("c_nm"), j + 1)
                    for h in range(H1):
                        ins = nc.scalar.activation(PC[:, j % 2, MEM * h:MEM * (h + 1)], ps[:, MEM * h:MEM * (h + 1)],
                                                   ACT.Exp, bias=SMC[:, j % 2, 4 + h:5 + h], scale=SC1,
                                                   accum_out=SMC[:, j % 2, 8 + h:9 + h])
                    ins.then_inc(S("c_exp"), 1)
                if j >= 1:
                    act.wait_ge(S("c_pt"), j)
                    wait(act, S("c_o"), j - 1)
                    nc.scalar.activation(PTC[:, :], ps[:, 2 * BANK:4 * BANK], ACT.Copy).then_inc(S("c_ptk"), 1)
            q0 = WH["z_m"][1]
            for zb in range(13):
                if zb < 12:
                    q = q0 + zb // 2
                    act.wait_ge(quad_ready, q + 1)
                    wait(act, S("y_done"), zb)
                    nc.scalar.activation(SIL[:, :], half(q, zb % 2), ACT.Silu).then_inc(free(q), 1)
                if 1 <= zb <= 8:
                    act.wait_ge(S("y_done"), zb)
                    nc.scalar.activation(YH[:, zb - 1, :], PR[:, zb - 1, :], ACT.Copy).then_inc(S("y_hi"), 1)
            for b in range(0, KB, 2):
                act.dma_start(HX[:, b:b + 2, :], xT[P * b:P * (b + 2), :].rearrange("(b p) t -> p b t", p=P))\
                    .then_inc(S(f"x_again{b // 2}"), 16)
            for zb in range(8, 12):
                act.wait_ge(S("y_done"), zb + 1)
                nc.scalar.activation(YHC[:, zb - 8, :], PR[:, zb, :], ACT.Copy).then_inc(S("y_hi"), 1)
            for b in range(KB):
                q = WH["out_1"][1] + b // 2
                act.wait_ge(free(q), freed(q, b % 2))
                norm_square(act, NRMF, b)
            norm_root(act, NRMF)

        def dve_block1(dve):
            v = Line(dve, S("dve_line"))
            dve.wait_ge(S("par_loaded"), 16)
            for b in range(KB):
                norm_add(dve, NRM1, b)
            norm_apply(dve, NRM1)
            dve.wait_ge(quad_ready, WH["x_m"][1] + 1)
            v.step(nc.vector.memset(XM[:, :, 0:3], 0.0))
            nc.vector.memset(V1[:, :, :, P:P + 1], 1.0).then_inc(S("ones_set"), 1)
            for b in range(4):
                q = WH["x_m"][1] + b // 2
                dve.wait_ge(free(q), freed(q, b % 2))
                v.wait()
                nc.vector.tensor_scalar(XCV[:, b, :], XM[:, b, 0:T], par("conv_w", b), par("conv_b", b), ALU.mult, ALU.add)\
                    .then_inc(S("conv_done"), 1)
                for k in range(1, 4):
                    dve.wait_ge(S("conv_done"), 4 * b + k)
                    nc.vector.scalar_tensor_tensor(XCV[:, b, :], XM[:, b, k:k + T], par("conv_w", 4 * k + b), XCV[:, b, :],
                                                   ALU.mult, ALU.add).then_inc(S("conv_done"), 1)
            rows = Line(dve, S("rows_v"))
            dve.wait_ge(S("gate_sum"), 12)
            nc_v = nc.vector
            rows.step(nc_v.tensor_scalar(R0[:, :], ps[32:36, 0:T], par("b_if", rows=slice(32, 36)), 0.0, ALU.add, ALU.min))
            v.step(nc_v.memset(R4[:, :], 1.0))
            v.wait()
            v.step(nc_v.memset(R4[:, 0:T:P], 0.0))
            v.wait()
            dve.wait_ge(S("rows_a"), 3)
            rows.wait(1)
            rows.step(nc_v.tensor_tensor(R0[:, :], R0[:, :], R1[:, :], ALU.subtract))
            rows.wait()
            rows.step(nc_v.tensor_tensor_scan(R2[:, :], R4[:, :], R0[:, :], 0.0, ALU.mult, ALU.add))
            rows.wait()
            rows.step(nc_v.scalar_tensor_tensor(R3[:, :], ps[0:4, 0:T], par("b_if", rows=slice(0, 4)), R2[:, :],
                                                ALU.add, ALU.subtract))
            rows.step(nc_v.memset(R0[:, :], 0.0))
            rows.wait()
            rows.step(nc_v.tensor_copy(R0[:, P:T:P], R2[:, P - 1:T - P:P]))
            rows.wait()
            rows.step(nc_v.tensor_tensor_scan(R1[:, :], R0[:, :], R3[:, :], 0.0, ALU.add, ALU.max))
            rows.step(nc_v.memset(MPREV[:, 0:1], 0.0))
            rows.wait()
            rows.step(nc_v.tensor_tensor(MPREV[:, 1:NT], R2[:, P - 1:T - P:P], R1[:, P - 1:T - P:P], ALU.add))
            rows.wait()
            v3 = lambda r: r[:, :].rearrange("p (c l) -> p c l", c=NT)
            rows.step(nc_v.tensor_tensor(v3(R4), MPREV[:, :].unsqueeze(2).to_broadcast([4, NT, P]), v3(R1), ALU.subtract))
            rows.step(nc_v.tensor_tensor(R2[:, :], R2[:, :], R1[:, :], ALU.add))
            rows.step(nc_v.tensor_tensor(v3(R0), v3(R3), v3(R1)[:, :, P - 1:P].to_broadcast([4, NT, P]), ALU.subtract))
            rows.wait()
            rows.step(nc_v.tensor_scalar(R1[:, :], R1[:, :], -1.0, None, ALU.mult))
            dve.wait_ge(S("cols_ready"), 1)
            nc_v.tensor_copy(COL[:, :, :], ps[:, 2 * BANK:2 * BANK + 96].rearrange("p (c n) -> p c n", c=NT))\
                .then_inc(S("cols_kept"), 1)
            dve.wait_ge(S("cols_kept"), 1)
            dve.wait_ge(S("skip_done"), 4)
            for c in range(NT):
                dve.wait_ge(S("bc_ready"), c + 1)
                wait(dve, S("pre_done"), c)
                wait(dve, S("num_ready"), c)
                for h in range(H1):
                    ins = nc_v.scalar_tensor_tensor(EW[:, h, :], ps[:, BANK + P * h:BANK + P * (h + 1)], COL[:, c, h:h + 1],
                                                    par("mask_ts", 0, P), ALU.add, ALU.add)
                ins.then_inc(S("e_done"), 1)
                v.step(nc_v.tensor_tensor(QS[:, :, :], ps[:, 0:BANK].rearrange("p (h t) -> p h t", h=H1),
                                          QT[:, :, P * c:P * (c + 1)], ALU.mult))
                v.step(nc_v.tensor_copy(DEC[:, :], ps[:, P - 1:BANK:P]))
                dve.wait_ge(S("kt_ready"), c + 1)
                wait(dve, S("cu_ready"), c)
                for h in range(H1):
                    v.step(nc_v.tensor_scalar(KW[:, h, :], ps[:, 3 * BANK + P * h:3 * BANK + P * (h + 1)],
                                              COL[:, c, 4 + h:5 + h], SC1, ALU.mult, ALU.mult))
                dve.wait_ge(S("w_exp"), c + 1)
                dve.wait_ge(S("sc_ready"), c + 1)
                v.wait()
                nc_v.scalar_tensor_tensor(EW[:, :, :].rearrange("p h t -> p (h t)"), ps[:, 2 * BANK:3 * BANK], SC1,
                                          EW[:, :, :].rearrange("p h t -> p (h t)"), ALU.mult, ALU.mult).then_inc(S("pt_done"), 1)
                dve.wait_ge(S("cu_ready"), c + 1)
                for h in range(H1):
                    if c == 0:
                        ins = nc_v.tensor_copy(CS[:, h, :], cup(h))
                    else:
                        ins = nc_v.scalar_tensor_tensor(CS[:, h, :], CS[:, h, :], DEC[:, h:h + 1], cup(h), ALU.mult, ALU.add)
                    ins.then_inc(S("c_upd"), 1) if h < H1 - 1 else ins.then_inc(S("c_done"), 1)
                dn = ps[:, 4 * BANK:6 * BANK].rearrange("p (b x) -> p b x", b=2)[:, :, 0:2 * (P + 1)]\
                    .rearrange("p b (h w) -> p b h w", w=P + 1)[:, :, :, P]
                v.step(nc_v.tensor_scalar(DN[:, :].rearrange("p (b h) -> p b h", b=2), dn, -1.0, None, ALU.mult))
                v.wait()
                v.step(nc_v.tensor_tensor(DN[:, :].rearrange("p (b h) -> p b h", b=2), dn,
                                          DN[:, :].rearrange("p (b h) -> p b h", b=2), ALU.max))
                v.wait()
                v.step(nc_v.tensor_tensor(DN[:, :], DN[:, :], COL[:, c, 8:12], ALU.max))
                v.wait()
                v.step(nc_v.reciprocal(DN[:, :], DN[:, :]))
                v.wait()
                dve.wait_ge(S(f"o_back{c % 2}"), 16 * (c // 2 + 1))
                wait(dve, S("ht_ready"), c)
                for h in range(H1):
                    ins = nc_v.scalar_tensor_tensor(HN[:, h, :], num(h)[:, 0:P], DN[:, h:h + 1],
                                                    OSC[:, c % 2, P * h:P * (h + 1)], ALU.mult, ALU.mult)
                ins.then_inc(S("h_done"), 1)
                dve.wait_ge(S("h_done"), c + 1)
                for h in range(H1):
                    v.step(nc_v.bn_stats(ST[:, h, :], HN[:, h, :]))
                v.wait()
                for h in range(H1):
                    ins = nc_v.bn_aggr(MV[:, h, :], ST[:, h, :])
                ins.then_inc(S("mv_done"), 1)
                dve.wait_ge(S("sd_done"), c + 1)
                v.step(nc_v.reciprocal(SD[:, :], SD[:, :]))
                v.wait()
                for h in range(H1):
                    ins = nc_v.tensor_scalar(HN[:, h, :], HN[:, h, :], MV[:, h, 0:1], SD[:, h:h + 1], ALU.subtract, ALU.mult)
                ins.then_inc(S("hn_done"), 1)
                dve.wait_ge(S("ht_ready"), c + 1)
                for h in range(H1):
                    x = PR[:, h, P * c:P * (c + 1)]
                    ins = nc_v.scalar_tensor_tensor(x, ps[:, P * h:P * (h + 1)], par("mnorm_g", h), x, ALU.mult, ALU.add)
                ins.then_inc(S("pre_done"), 1)

            for m in range(2):
                nc_v.tensor_tensor_reduce(LTMP[:, :], par("lam", 128 * m, 64), par("lam", 128 * m + 64, 64), 1.0, 0.0,
                                          ALU.mult, ALU.add, LM[:, m:m + 1]).then_inc(S("lam_v"), 1)
                dve.wait_ge(S("lam_v"), m + 1)
            v.step(nc_v.tensor_scalar(GD[:, :], par("dnorm_g", 0, 4), 1.0 - LAM_INIT, None, ALU.mult))
            dve.wait_ge(S("lam_a"), 1)
            v.step(nc_v.scalar_tensor_tensor(LM[:, 2:3], LM[:, 1:2], -LAM_INIT, LM[:, 0:1], ALU.add, ALU.subtract))
            v.wait()
            n_steps = len(STEPS)
            for i in range(n_steps + 2):
                if i < n_steps:
                    n = P * (STEPS[i][1] + 1)
                    for m in range(2):
                        dve.wait_ge(S("d_scores"), 2 * i + m + 1)
                        v.step(nc_v.tensor_reduce(SM[:, i % 4, m:m + 1], ps[:, 2 * BANK * m:2 * BANK * m + n], AX, ALU.max))
                    v.wait()
                    nc_v.tensor_scalar(SM[:, i % 4, 2:4], SM[:, i % 4, 0:2], -SCD, None, ALU.mult).then_inc(S("d_nm"), 1)
                if 1 <= i <= n_steps:
                    s, (h, j) = i - 1, STEPS[i - 1]
                    n = P * (j + 1)
                    dve.wait_ge(S("d_exp"), 2 * s + 2)
                    v.step(nc_v.reciprocal(SM[:, s % 4, 6:8], SM[:, s % 4, 4:6]))
                    v.wait()
                    v.step(nc_v.tensor_scalar(P1[s % 2][:, 0:n], P1[s % 2][:, 0:n], SM[:, s % 4, 7:8], LM[:, 2:3],
                                              ALU.mult, ALU.mult))
                    v.wait()
                    nc_v.scalar_tensor_tensor(P0[s % 2][:, 0:n], P0[s % 2][:, 0:n], SM[:, s % 4, 6:7], P1[s % 2][:, 0:n],
                                              ALU.mult, ALU.add).then_inc(S("d_p"), 1)
                if i >= 1 and i <= n_steps:
                    s = i - 1
                    dve.wait_ge(S("d_sd"), s + 1)
                    wait(dve, S("d_ot"), s - 1)
                    v.step(nc_v.reciprocal(OS1[:, s % 4, 1:2], OS1[:, s % 4, 1:2]))
                    v.wait()
                    nc_v.tensor_scalar(ON[:, s % 2, :], ps[:, 6 * BANK:6 * BANK + P], OS1[:, s % 4, 1:2], None, ALU.mult)\
                        .then_inc(S("d_on"), 1)
            for b in range(KB):
                norm_add(dve, NRMM, b)
            norm_apply(dve, NRMM)
            for j in range(NT + 1):
                if j < NT:
                    dve.wait_ge(S("c_scores"), j + 1)
                    v.step(nc_v.tensor_reduce(SMC[:, j % 2, 0:4], ps[:, 0:H1 * MEM].rearrange("p (h m) -> p h m", h=H1), AX, ALU.max))
                    v.wait()
                    nc_v.tensor_scalar(SMC[:, j % 2, 4:8], SMC[:, j % 2, 0:4], -SC1, None, ALU.mult).then_inc(S("c_nm"), 1)
                if j >= 1:
                    s = j - 1
                    dve.wait_ge(S("c_exp"), s + 1)
                    v.step(nc_v.reciprocal(SMC[:, s % 2, 8:12], SMC[:, s % 2, 8:12]))
                    v.wait()
                    p = PC[:, s % 2, :].rearrange("p (h m) -> p h m", h=H1)
                    nc_v.tensor_tensor(p, p, SMC[:, s % 2, 8:12].unsqueeze(2).to_broadcast([P, H1, MEM]), ALU.mult)\
                        .then_inc(S("c_p"), 1)
                    dve.wait_ge(S("c_o"), s + 1)
                    nc_v.tensor_copy(QC[:, :, P * s:P * (s + 1)], ps[:, 4 * BANK:5 * BANK].rearrange("p (h q) -> p h q", h=H1))\
                        .then_inc(S("c_oc"), 1)
            q0 = WH["z_m"][1]
            for zb in range(13):
                if zb < 12:
                    q = q0 + zb // 2
                    dve.wait_ge(free(q), freed(q, zb % 2))
                    nc_v.tensor_tensor(PR[:, zb, :], PR[:, zb, :], SIL[:, :], ALU.mult).then_inc(S("y_done"), 1)
                if 1 <= zb <= 8:
                    dve.wait_ge(S("y_hi"), zb)
                    dve.wait_ge(S("y_done"), zb)
                    nc_v.tensor_tensor(YL[:, zb - 1, :], PR[:, zb - 1, :], YH[:, zb - 1, :].bitcast(F32), ALU.subtract)\
                        .then_inc(S("y_lo"), 1)
            for zb in range(8, 12):
                dve.wait_ge(S("y_hi"), zb + 1)
                nc_v.tensor_tensor(YL[:, zb, :], PR[:, zb, :], YHC[:, zb - 8, :].bitcast(F32), ALU.subtract)\
                    .then_inc(S("y_lo"), 1)
            for b in range(KB):
                q = WH["out_1"][1] + b // 2
                dve.wait_ge(quad_ready, q + 1)
                dve.wait_ge(S(f"x_again{b // 2}"), 16)
                nc_v.tensor_tensor(HX[:, b, :], HX[:, b, :], half(q, b % 2), ALU.add).then_inc(free(q), 1)
                if b >= 1:
                    norm_add(dve, NRMF, b - 1)
            norm_add(dve, NRMF, KB - 1)
            norm_apply(dve, NRMF)

        HH = at("hidden_hi", A + 49152, [P, 4, T], F32R)
        HL = at("hidden_lo", A + 65536, [P, 4, T], F32R)
        FA = at("ff_act", A + 32768, [P, 2, T])
        FT = at("ff_tmp", A + 40960, [P, 2, T])
        hhi = lambda k, a, w: HH[:, k, a:a + w]
        hlo = lambda k, a, w: HL[:, k, a:a + w]

        def pe_group(pe, k, n, up_where, down_where, blocks_before, loop, ready):
            sl = loop and (loop[0], loop[1])
            ql = loop and (loop[0], loop[2])
            outs = 2 * n if k == "f2" else n
            feature_tiles(pe, up_where, outs, range(KB), xhi, xlo, ready=ready, sloop=sl, qloop=ql)
            bl = loop and (loop[0], n)
            feature_tiles(pe, down_where, 8, range(n), hhi, hlo, sloop=sl, qloop=ql,
                          ready=lambda m: (S(k + "_lo"), up(blocks_before + m + 1, bl)))

        def made(eng, k, j, up_quad, blocks_before, loop):
            if k == "f2":
                eng.wait_ge(free(up_quad + j), freed(up_quad + j, 1, loop and (loop[0], loop[2])))
            else:
                eng.wait_ge(S("f3_x"), up(blocks_before + j + 1, loop and (loop[0], 4)))

        def act_group(act, k, n, up_quad, blocks_before, loop):
            ql, bl = loop and (loop[0], loop[2]), loop and (loop[0], n)
            for j in range(n + 1):
                if j < n:
                    q, ob = (up_quad + j, 0) if k == "f2" else (up_quad + j // 2, j % 2)
                    act.wait_ge(quad_ready, up(q + 1, ql))
                    if j >= 2:
                        made(act, k, j - 2, up_quad, blocks_before, loop)
                    nc.scalar.activation(FA[:, j % 2, :], half(q, ob), ACT.Silu if k == "f2" else ACT.Relu)\
                        .then_inc(free(q), 1)
                if j >= 1:
                    made(act, k, j - 1, up_quad, blocks_before, loop)
                    nc.scalar.activation(HH[:, j - 1, :], FT[:, (j - 1) % 2, :], ACT.Copy).then_inc(S(k + "_hi"), 1)

        def dve_group(dve, k, n, up_quad, down_quad, blocks_before, loop, stream_tile, N=None):
            ql, bl = loop and (loop[0], loop[2]), loop and (loop[0], n)
            for j in range(n + 1):
                if j < n:
                    if j >= 2:
                        dve.wait_ge(S(k + "_lo"), up(blocks_before + j - 1, bl))
                    if k == "f2":
                        q = up_quad + j
                        dve.wait_ge(free(q), freed(q, 0, ql))
                        nc.vector.tensor_tensor(FT[:, j % 2, :], FA[:, j % 2, :], half(q, 1), ALU.mult).then_inc(free(q), 1)
                    else:
                        q = up_quad + j // 2
                        dve.wait_ge(free(q), freed(q, j % 2, ql))
                        nc.vector.tensor_tensor(FT[:, j % 2, :], FA[:, j % 2, :], FA[:, j % 2, :], ALU.mult)\
                            .then_inc(S(k + "_x"), 1)
                if j >= 1:
                    made(dve, k, j - 1, up_quad, blocks_before, loop)
                    dve.wait_ge(S(k + "_hi"), up(blocks_before + j, bl))
                    nc.vector.tensor_tensor(HL[:, j - 1, :], FT[:, (j - 1) % 2, :], HH[:, j - 1, :].bitcast(F32), ALU.subtract)\
                        .then_inc(S(k + "_lo"), 1)
            for b in range(KB):
                q = down_quad + b // 2
                dve.wait_ge(quad_ready, up(q + 1, ql))
                nc.vector.tensor_tensor(stream_tile[:, b, :], stream_tile[:, b, :], half(q, b % 2), ALU.add).then_inc(free(q), 1)
                if N and b >= 1:
                    norm_add(dve, N, b - 1)
            if N:
                norm_add(dve, N, KB - 1)

        def layer(k):
            b, ff = (2, FF2) if k == "f2" else (3, FF3)
            slots, quads = (6, 8) if k == "f2" else (4, 6)
            return lambda g: (WH[f"up_{b}_{g}"], WH[f"down_{b}_{g}"]), ff // 4, ff % 4, slots, quads

        def pe_groups(pe, k, ready):
            at_group, full, rest, slots, quads = layer(k)
            pe_group(pe, k, 4, *at_group(0), 0, None, ready)
            with pe.Fori(1, full) as i:
                pe_group(pe, k, 4, *at_group(0), 0, (i, slots, quads), None)
            if rest:
                pe_group(pe, k, rest, *at_group(full), 4 * full, None, None)

        def act_groups(act, k):
            at_group, full, rest, slots, quads = layer(k)
            act_group(act, k, 4, at_group(0)[0][1], 0, None)
            with act.Fori(1, full) as i:
                act_group(act, k, 4, at_group(0)[0][1], 0, (i, slots, quads))
            if rest:
                act_group(act, k, rest, at_group(full)[0][1], 4 * full, None)

        def dve_groups(dve, k, stream_tile, N):
            at_group, full, rest, slots, quads = layer(k)
            up_q, down_q = at_group(0)[0][1], at_group(0)[1][1]
            last = full if rest else full - 1
            dve_group(dve, k, 4, up_q, down_q, 0, None, stream_tile)
            with dve.Fori(1, last) as i:
                dve_group(dve, k, 4, up_q, down_q, 0, (i, slots, quads), stream_tile)
            dve_group(dve, k, rest or 4, at_group(last)[0][1], at_group(last)[1][1], 4 * last, None, stream_tile, N)

        if 2 in blocks:
            NRM2 = norm_set("n2", lambda b: H[:, b, :], T, lambda b: par("norm_mix_2", b), A + 32768,
                            hi=lambda b: XHI[:, b, :], lo=lambda b: XLO[:, b, :])
            Q2 = at("q_2", A, [P, 4, T])
            K2 = at("k_2", A + 16384, [P, 4, T])
            V2 = at("v_2", A + 32768, [P, NT, HALF])
            BIAS = at("bias_2", A + 49152, [P, HEADS2, SPAN])
            P2 = at("p_2", A + 69632, [P, 2, SPAN])
            PT2 = at("p_t2", A + 74752, [P, SPAN])
            ATOK = at("att_tok", A + 77312, [P, 2, HALF])
            AT = at("att", A, [P, 4, T])
            ATH = at("att_hi", A + 16384, [P, 4, T], F32R)
            ATL = at("att_lo", A + 32768, [P, 4, T], F32R)
            MX2 = small("max_2", [P, 2, 2])
            L2 = small("sum_2", [P, 2, HEADS2])
            SG = at("gate_sig", A, [P, 4, T])
            MG = at("merged", A + 49152, [P, KB, T])
            VS = at("vs", A + 16384, [P, NT, HALF])
            U2 = at("u_gelu", A + 32768, [P, 4, T])
            SGW = at("sgu_w", A + 81920, [P, 1024])
            SGN = at("sgu_norm", A, [P, 1024])
            TS = at("sgu_tmp", A + 4096, [P, 2, T])
            SH = at("sgu_hi", A + 16384, [P, 4, T], F32R)
            SL = at("sgu_lo", A + 32768, [P, 4, T], F32R)
            TMG = at("merge_tmp", A + 81920, [P, T])
            ST2 = small("stats_2", [P, NT, 6])
            MV2 = small("mean_var_2", [P, NT, 2])
            H2 = at("h2", A, [P, KB, T])
            NRMG = norm_set("n2g", lambda b: H2[:, b, :], T, lambda b: par("norm_ffn_2", b), A + 32768,
                            hi=lambda b: XHI[:, b, :], lo=lambda b: XLO[:, b, :])
            NRMO = norm_set("n2o", lambda b: H2[:, b, :], T, lambda b: par("norm_final_2", b), A + 32768,
                            out=lambda b: H2[:, b, :])
            ahi, alo = (lambda k, a, w: ATH[:, k, a:a + w]), (lambda k, a, w: ATL[:, k, a:a + w])
            shi, slo = (lambda k, a, w: SH[:, k, a:a + w]), (lambda k, a, w: SL[:, k, a:a + w])
            STEPS2 = [(j, h) for j in range(NT) for h in range(HEADS2)]
            FULL2 = FF2 // 4

        def span(j):
            n = min(P * (j + 1), SPAN)
            return P * (j + 1) - n, n, SPAN - n

        def pe_block2(pe):
            norm_sum(pe, NRM2)
            feature_tiles(pe, WH["q_2"], 4, range(KB), xhi, xlo, ready=lambda n: of(NRM2, "lo", n + 1))
            feature_tiles(pe, WH["k_2"], 4, range(KB), xhi, xlo)
            token_tiles(pe, WH["v_2"], 2, xhi, xlo)
            last = WH["v_2"][1] + 1
            quad_start(pe, last + 1)
            quad_start(pe, last + 2)
            n_steps = len(STEPS2)
            for i in range(n_steps + 1):
                if i < n_steps:
                    j, h = STEPS2[i]
                    k0, n, _ = span(j)
                    rows = slice(64 * (h % 2), 64 * (h % 2) + 64)
                    wait(pe, S("a_max"), i - 1)
                    for c in range(0, n, HALF):
                        w = min(HALF, n - c)
                        a = 2 * BANK * (i % 2) + c
                        mm = nc.tensor.matmul(ps[:, a:a + w], Q2[rows, h // 2, P * j:P * (j + 1)],
                                              K2[rows, h // 2, k0 + c:k0 + c + w], start=True, stop=True)
                    mm.then_inc(S("a_scores"), 1)
                if i >= 1:
                    s, (j, h) = i - 1, STEPS2[i - 1]
                    k0, n, _ = span(j)
                    pe.wait_ge(S("a_exp"), s + 1)
                    wait(pe, S("a_ptk"), s)
                    for k in range(n // P):
                        mm = nc.tensor.transpose(ps[:, 4 * BANK + P * k:4 * BANK + P * (k + 1)],
                                                 P2[:, s % 2, P * k:P * (k + 1)], IDENT)
                    mm.then_inc(S("a_pt"), 1)
                    pe.wait_ge(S("a_ptk"), s + 1)
                    if h == 0:
                        wait(pe, S("a_tok"), j)
                    for k in range(n // P):
                        mm = nc.tensor.matmul(ps[:, 6 * BANK + 64 * h:6 * BANK + 64 * (h + 1)], PT2[:, P * k:P * (k + 1)],
                                              V2[:, k0 // P + k, 64 * h:64 * (h + 1)], start=(k == 0), stop=(k == n // P - 1))
                    mm.then_inc(S("a_o"), 1)
                    if h == HEADS2 - 1:
                        pe.wait_ge(S("a_tok"), j + 1)
                        wait(pe, S("a_att"), j)
                        for b in range(4):
                            mm = nc.tensor.transpose(ps[:, 7 * BANK + P * b:7 * BANK + P * (b + 1)],
                                                     ATOK[:, j % 2, P * b:P * (b + 1)], IDENT)
                        mm.then_inc(S("a_ot"), 1)
            pe.wait_ge(S("a_att"), NT)
            pe.wait_ge(S("a_max"), n_steps)
            for pair in range(2):
                feature_tiles(pe, WH[f"gate_0{pair}"], 4, range(KB), xhi, xlo)
                feature_tiles(pe, WH[f"branch_0{pair}"], 4, range(4), ahi, alo,
                              ready=(lambda n: (S("att_lo"), n + 1)) if pair == 0 else None)
            token_tiles(pe, WH["vs_2"], 2, xhi, xlo)
            feature_tiles(pe, WH["u_2"], 4, range(KB), xhi, xlo)
            last = WH["u_2"][1] + 1
            quad_start(pe, last + 1)
            quad_start(pe, last + 2)
            pe.wait_ge(S("vn"), 3 * NT)
            for g in range(4):
                for tt in range(NT):
                    c = 2 * BANK * g + P * tt
                    mm = nc.tensor.matmul(ps[:, c:c + P], VS[:, tt, P * g:P * (g + 1)], SGW[:, P * g:P * (g + 1)],
                                          start=True, stop=True)
                mm.then_inc(S("mixed"), 1)
            pe.wait_ge(S("sgu_v"), 8)
            for pair in range(2):
                feature_tiles(pe, WH[f"gate_1{pair}"], 4, range(KB), xhi, xlo)
                feature_tiles(pe, WH[f"branch_1{pair}"], 4, range(4), shi, slo,
                              ready=(lambda n: (S("sgu_lo_done"), n + 1)) if pair == 0 else None)
            feature_tiles(pe, WH["out_2"], 8, range(KB), xhi, xlo, ready=lambda n: (S("mg_lo"), n + 1))
            norm_sum(pe, NRMG)
            ready = lambda n: of(NRMG, "lo", n + 1)
            pe_groups(pe, "f2", ready)
            norm_sum(pe, NRMO)

        def act_block2(act):
            if 1 not in blocks:
                for b in range(KB):
                    act.dma_start(H[:, b, :], xT[P * b:P * (b + 1), :]).then_inc(S("h_in"), 16)
                act.wait_ge(S("h_in"), 16 * KB)
                act.wait_ge(S("par_loaded"), 16)
            for b in range(KB):
                if 1 in blocks:
                    act.wait_ge(*of(NRMF, "x", b + 1))
                norm_square(act, NRM2, b)
            act.dma_start(h_scr.rearrange("(b p) t -> p b t", p=P), H[:, :, :]).then_inc(S("h_spilled"), 16)
            act.dma_start(BIAS[:, :, :], bias2.rearrange("p (h k) -> p h k", h=HEADS2)).then_inc(S("bias_loaded"), 16)
            norm_root(act, NRM2)
            norm_hi(act, NRM2)
            act.wait_ge(S("h_spilled"), 16)
            for name, dst, scale in (("q_2", Q2, 64.0 ** -0.5), ("k_2", K2, 1.0)):
                q0 = WH[name][1]
                for b in range(4):
                    q = q0 + b // 2
                    act.wait_ge(quad_ready, q + 1)
                    nc.scalar.activation(dst[:, b, :], half(q, b % 2), ACT.Copy, scale=scale).then_inc(free(q), 1)
            q0 = WH["v_2"][1]
            for s in range(2):
                act.wait_ge(quad_ready, q0 + s + 1)
                for ob in range(2):
                    nc.scalar.activation(V2[:, 4 * ob:4 * ob + 4, 256 * s:256 * (s + 1)],
                                         half(q0 + s, ob).rearrange("p (t c) -> p t c", t=4), ACT.Copy).then_inc(free(q0 + s), 1)
            n_steps = len(STEPS2)
            for i in range(n_steps + 1):
                if i < n_steps:
                    j, h = STEPS2[i]
                    _, n, _ = span(j)
                    act.wait_ge(S("a_nm"), i + 1)
                    nc.scalar.activation(P2[:, i % 2, 0:n], P2[:, i % 2, 0:n], ACT.Exp, bias=MX2[:, i % 2, 1:2],
                                         accum_out=L2[:, j % 2, h:h + 1]).then_inc(S("a_exp"), 1)
                if i >= 1:
                    s, (j, h) = i - 1, STEPS2[i - 1]
                    _, n, _ = span(j)
                    act.wait_ge(S("a_pt"), s + 1)
                    wait(act, S("a_o"), s)
                    nc.scalar.activation(PT2[:, 0:n], ps[:, 4 * BANK:4 * BANK + n], ACT.Copy).then_inc(S("a_ptk"), 1)
                    if h == HEADS2 - 1:
                        act.wait_ge(S("a_ot"), j + 1)
                        nc.scalar.activation(AT[:, :, P * j:P * (j + 1)],
                                             ps[:, 7 * BANK:8 * BANK].rearrange("p (b t) -> p b t", b=4), ACT.Copy)\
                            .then_inc(S("a_att"), 1)
            act.wait_ge(S("a_att"), NT)
            for b in range(4):
                nc.scalar.activation(ATH[:, b, :], AT[:, b, :], ACT.Copy).then_inc(S("att_hi_done"), 1)

            def gates(branch, pair):
                q0 = WH[f"gate_{branch}{pair}"][1]
                for b in range(4):
                    q = q0 + b // 2
                    act.wait_ge(quad_ready, q + 1)
                    if pair:
                        before = WH[f"branch_{branch}0"][1] + b // 2
                        act.wait_ge(free(before), freed(before, b % 2))
                    nc.scalar.activation(SG[:, b, :], half(q, b % 2), ACT.Sigmoid,
                                         bias=par("b_gate_2", 8 * branch + 4 * pair + b)).then_inc(free(q), 1)

            act.wait_ge(S("att_lo"), 4)
            gates(0, 0)
            gates(0, 1)
            q0 = WH["vs_2"][1]
            for q in range(WH["branch_01"][1], WH["branch_01"][1] + 2):
                act.wait_ge(free(q), freed(q, 1))
            act.dma_start(SGW[:, :], sgu[:, 0:1024]).then_inc(S("sgu_loaded"), 16)
            act.dma_start(SGN[:, :], sgu[:, 1024:2048]).then_inc(S("sgu_loaded"), 16)
            for s in range(2):
                act.wait_ge(quad_ready, q0 + s + 1)
                for ob in range(2):
                    nc.scalar.activation(VS[:, 4 * ob:4 * ob + 4, 256 * s:256 * (s + 1)],
                                         half(q0 + s, ob).rearrange("p (t c) -> p t c", t=4), ACT.Gelu_apprx_tanh)\
                        .then_inc(free(q0 + s), 1)
            q0 = WH["u_2"][1]
            for b in range(4):
                q = q0 + b // 2
                act.wait_ge(quad_ready, q + 1)
                nc.scalar.activation(U2[:, b, :], half(q, b % 2), ACT.Gelu_apprx_tanh).then_inc(free(q), 1)
            act.wait_ge(S("vs_mv"), NT)
            nc.scalar.activation(MV2[:, :, 1], MV2[:, :, 1], ACT.Sqrt, bias=EPSC).then_inc(S("vs_sd"), 1)
            for g in range(4):
                act.wait_ge(S("sgu_v"), 2 * g + 2)
                if g == 0:
                    act.wait_ge(S("mixed"), 4)
                nc.scalar.activation(SH[:, g, :], U2[:, g, :], ACT.Copy).then_inc(S("sgu_hi_done"), 1)
            gates(1, 0)
            gates(1, 1)
            for q in range(WH["branch_11"][1], WH["branch_11"][1] + 2):
                act.wait_ge(free(q), freed(q, 1))
            act.dma_start(H2[:, :, :], h_scr.rearrange("(b p) t -> p b t", p=P)).then_inc(S("h2_loaded"), 16)
            for b in range(KB):
                act.wait_ge(S("merged"), b + 1)
                nc.scalar.activation(XHI[:, b, :], MG[:, b, :], ACT.Copy).then_inc(S("mg_hi"), 1)
            for b in range(KB):
                q = WH["out_2"][1] + b // 2
                act.wait_ge(free(q), freed(q, b % 2))
                norm_square(act, NRMG, b)
            norm_root(act, NRMG)
            norm_hi(act, NRMG)
            act.wait_ge(*of(NRMG, "lo", KB))
            act_groups(act, "f2")
            q0 = WH[f"down_2_{(FF2 - 1) // 4}"][1]
            for b in range(KB):
                q = q0 + b // 2
                act.wait_ge(free(q), freed(q, b % 2))
                norm_square(act, NRMO, b)
            norm_root(act, NRMO)

        def dve_block2(dve):
            v = Line(dve, S("dve_line2"))
            dve.wait_ge(S("par_loaded"), 16)
            for b in range(KB):
                norm_add(dve, NRM2, b)
            norm_apply(dve, NRM2)
            dve.wait_ge(S("bias_loaded"), 16)
            n_steps = len(STEPS2)
            for i in range(n_steps + 1):
                if i < n_steps:
                    j, h = STEPS2[i]
                    _, n, c = span(j)
                    dve.wait_ge(S("a_scores"), i + 1)
                    wait(dve, S("a_pt"), i - 1)
                    a = 2 * BANK * (i % 2)
                    nc.vector.tensor_tensor_reduce(P2[:, i % 2, 0:n], ps[:, a:a + n], BIAS[:, h, c:SPAN], 1.0, 4 * NEG,
                                                   ALU.add, ALU.max, MX2[:, i % 2, 0:1]).then_inc(S("a_max"), 1)
                    dve.wait_ge(S("a_max"), i + 1)
                    nc.vector.tensor_scalar(MX2[:, i % 2, 1:2], MX2[:, i % 2, 0:1], -1.0, None, ALU.mult).then_inc(S("a_nm"), 1)
                if i >= 1 and STEPS2[i - 1][1] == HEADS2 - 1:
                    j = STEPS2[i - 1][0]
                    dve.wait_ge(S("a_exp"), i)
                    v.step(nc.vector.reciprocal(L2[:, j % 2, :], L2[:, j % 2, :]))
                    v.wait()
                    dve.wait_ge(S("a_o"), i)
                    wait(dve, S("a_ot"), j - 1)
                    nc.vector.tensor_tensor(ATOK[:, j % 2, :].rearrange("p (h d) -> p h d", h=HEADS2),
                                            ps[:, 6 * BANK:7 * BANK].rearrange("p (h d) -> p h d", h=HEADS2),
                                            L2[:, j % 2, :].unsqueeze(2).to_broadcast([P, HEADS2, 64]), ALU.mult)\
                        .then_inc(S("a_tok"), 1)
            for b in range(4):
                dve.wait_ge(S("att_hi_done"), b + 1)
                ins = nc.vector.tensor_tensor(ATL[:, b, :], AT[:, b, :], ATH[:, b, :].bitcast(F32), ALU.subtract)
                ins.then_inc(S("att_lo"), 1)

            def merge(branch, pair):
                for b in range(4):
                    q, o = WH[f"branch_{branch}{pair}"][1] + b // 2, 4 * pair + b
                    gate = WH[f"gate_{branch}{pair}"][1] + b // 2
                    dve.wait_ge(quad_ready, q + 1)
                    dve.wait_ge(free(gate), freed(gate, b % 2))
                    if branch == 0:
                        nc.vector.tensor_tensor(MG[:, o, :], SG[:, b, :], half(q, b % 2), ALU.mult).then_inc(free(q), 1)
                    else:
                        wait(dve, S("merged"), o)
                        nc.vector.tensor_tensor(TMG[:, :], SG[:, b, :], half(q, b % 2), ALU.mult).then_inc(free(q), 1)
                        dve.wait_ge(free(q), freed(q, b % 2))
                        nc.vector.tensor_tensor(MG[:, o, :], MG[:, o, :], TMG[:, :], ALU.add).then_inc(S("merged"), 1)

            merge(0, 0)
            merge(0, 1)
            dve.wait_ge(S("sgu_loaded"), 32)
            q0 = WH["vs_2"][1]
            for s in range(2):
                dve.wait_ge(free(q0 + s), freed(q0 + s, 1))
            for tt in range(NT):
                v.step(nc.vector.bn_stats(ST2[:, tt, :], VS[:, tt, :]))
            v.wait()
            for tt in range(NT):
                nc.vector.bn_aggr(MV2[:, tt, :], ST2[:, tt, :]).then_inc(S("vs_mv"), 1)
            dve.wait_ge(S("vs_sd"), 1)
            v.step(nc.vector.reciprocal(MV2[:, :, 1], MV2[:, :, 1]))
            v.wait()
            for tt in range(NT):
                x = VS[:, tt, :]
                nc.vector.tensor_scalar(x, x, MV2[:, tt, 0:1], MV2[:, tt, 1:2], ALU.subtract, ALU.mult).then_inc(S("vn"), 1)
                dve.wait_ge(S("vn"), 3 * tt + 1)
                nc.vector.tensor_tensor(x, x, SGN[:, 0:HALF], ALU.mult).then_inc(S("vn"), 1)
                dve.wait_ge(S("vn"), 3 * tt + 2)
                nc.vector.tensor_tensor(x, x, SGN[:, HALF:2 * HALF], ALU.add).then_inc(S("vn"), 1)
            uq = WH["u_2"][1]
            for g in range(4):
                dve.wait_ge(S("mixed"), g + 1)
                dve.wait_ge(free(uq + g // 2), freed(uq + g // 2, g % 2))
                wait(dve, S("sgu_v"), 2 * g)
                mixed = ps[:, 2 * BANK * g:2 * BANK * (g + 1)].rearrange("p (t c) -> p t c", t=NT)
                bias = SGW[:, HALF + P * g:HALF + P * (g + 1)].unsqueeze(1).to_broadcast([P, NT, P])
                nc.vector.tensor_tensor(TS[:, g % 2, :].rearrange("p (t c) -> p t c", t=NT), mixed, bias, ALU.add)\
                    .then_inc(S("sgu_v"), 1)
                dve.wait_ge(S("sgu_v"), 2 * g + 1)
                nc.vector.tensor_tensor(U2[:, g, :], U2[:, g, :], TS[:, g % 2, :], ALU.mult).then_inc(S("sgu_v"), 1)
            for g in range(4):
                dve.wait_ge(S("sgu_hi_done"), g + 1)
                nc.vector.tensor_tensor(SL[:, g, :], U2[:, g, :], SH[:, g, :].bitcast(F32), ALU.subtract)\
                    .then_inc(S("sgu_lo_done"), 1)
            merge(1, 0)
            merge(1, 1)
            for b in range(KB):
                dve.wait_ge(S("mg_hi"), b + 1)
                nc.vector.tensor_tensor(XLO[:, b, :], MG[:, b, :], XHI[:, b, :].bitcast(F32), ALU.subtract).then_inc(S("mg_lo"), 1)
            dve.wait_ge(S("h2_loaded"), 16)
            for b in range(KB):
                q = WH["out_2"][1] + b // 2
                dve.wait_ge(quad_ready, q + 1)
                nc.vector.tensor_tensor(H2[:, b, :], H2[:, b, :], half(q, b % 2), ALU.add).then_inc(free(q), 1)
                if b >= 1:
                    norm_add(dve, NRMG, b - 1)
            norm_add(dve, NRMG, KB - 1)
            norm_apply(dve, NRMG)
            dve.wait_ge(*of(NRMG, "lo", KB))
            dve_groups(dve, "f2", H2, NRMO)
            norm_apply(dve, NRMO)

        if 3 in blocks:
            H2I = H2 if 2 in blocks else at("h2", A, [P, KB, T])
            MT = at("meta", A + 49152, [P, KB, META])
            XH3 = at("xhi3", X, [P, KB, LW], F32R)
            XL3 = at("xlo3", X + 33280, [P, KB, LW], F32R)
            NRM3M = norm_set("n3m", lambda b: MT[:, b, :], META, lambda b: par("norm_mix_g_3", b), A + 49664,
                             hi=lambda b: XH3[:, b, T:LW], lo=lambda b: XL3[:, b, T:LW])
            NRM3 = norm_set("n3", lambda b: H2I[:, b, :], T, lambda b: par("norm_mix_g_3", b), A + 32768,
                            hi=lambda b: XH3[:, b, 0:T], lo=lambda b: XL3[:, b, 0:T])
            x3hi, x3lo = (lambda k, a, w: XH3[:, k, a:a + w]), (lambda k, a, w: XL3[:, k, a:a + w])
            PADC = CCK - 1
            CC = at("c_in", A, [P, 4, PADC + LW])
            CCO = at("c_out", A + 17152, [P, 4, T])
            SGC = at("c_gate", A + 17152, [P, 2, LW])
            XL_ = at("x_lru", A + 33536, [P, 4, 3 + LW])
            YL3 = at("y_lru", A + 33536, [P, 4, T])
            GL = at("g_lru", A + 50240, [P, 4, T])
            TX = at("l_x", A + 66624, [P, LW])
            TI = at("l_i", A + 70784, [P, LW])
            TU = at("l_u", A + 74944, [P, LW])
            TR = at("l_r", A + 79104, [P, LW])
            LRUW = at("lru_w", A + 83264, [P, 2, 4, P])
            NC4 = small("lru_rate", [P, 4])
            NCT = small("lru_rate_tmp", [P, 4])
            NRML = norm_set("nl", lambda b: YL3[:, b, :], T, lambda b: par("out_norm_lru_g_3", b), A + 66624, nb=4,
                            hi=lambda b: XHI[:, b, :], lo=lambda b: XLO[:, b, :])
            NRMV = norm_set("nv", lambda b: CCO[:, b, :], T, None, A, nb=4)
            NRMC = norm_set("nc", lambda b: CCO[:, b, :], T, lambda b: par("out_norm_cc_g_3", b), A, nb=4,
                            hi=lambda b: XHI[:, 4 + b, :], lo=lambda b: XLO[:, 4 + b, :])
            H3 = at("h3", A, [P, KB, T])
            NRMP = norm_set("n3p", lambda b: H3[:, b, :], T, lambda b: par("norm_mlp_g_3", b), A + 32768,
                            hi=lambda b: XHI[:, b, :], lo=lambda b: XLO[:, b, :])
            NRME = norm_set("n3o", lambda b: H3[:, b, :], T, lambda b: par("norm_final_g_3", b), A + 32768,
                            out=lambda b: H3[:, b, :])
            PIECES = [(g, a, w) for a, w in ((0, HALF), (HALF, HALF), (T, META)) for g in range(2)]

        def trio(q, a=0, w=T):
            c = 3 * BANK * (q % 2)
            return ps[:, c + a:c + a + w]

        def piece_cols(a, w):
            s = 0 if a == T else a + META
            return slice(s, s + w)

        def pe_trios(pe, name, first_out, n, ready=None):
            slot, quad = WH[name]
            t0 = first_out * KB
            for o in range(first_out, first_out + n):
                q = quad + o
                pe.wait_ge(free(q), 2 * (q // 2)) if q >= 2 else None
                c0 = 3 * BANK * (q % 2)
                for k in range(KB):
                    t = o * KB + k
                    s = slot + t // TILES
                    r = s % 2
                    first = t % TILES == 0
                    if first:
                        slot_start(pe, s, None)
                    if ready and o == 0:
                        pe.wait_ge(*ready(k))
                    w_hi, w_lo = WHI[:, r, t % TILES, :], WLO[:, r, t % TILES, :]
                    for m, (w, x) in enumerate(((w_hi, x3hi), (w_hi, x3lo), (w_lo, x3hi))):
                        for a, width in ((0, HALF), (HALF, HALF), (T, META)):
                            mm = nc.tensor.matmul(ps[:, c0 + a:c0 + a + width], w, x(k, a, width),
                                                  start=(k == 0 and m == 0), stop=(k == KB - 1 and m == 2))
                            if first and s > 0:
                                mm.then_inc(slot_used, 1)
                            first = False
                mm.then_inc(quad_ready, 1)

        def pe_block3(pe):
            norm_sum(pe, NRM3M)
            pe.wait_ge(*of(NRM3M, "root", 1))
            norm_sum(pe, NRM3)
            pe.wait_ge(*of(NRM3M, "lo", KB))
            ready = lambda n: of(NRM3, "lo", n + 1)
            pe_trios(pe, "x_lru", 0, 4, ready)
            pe.wait_ge(S("lru_w_loaded"), 16)
            n = 0
            for b in range(4):
                name = ("v_cc", "g_cc")[b // 2]
                pe_trios(pe, name, 2 * (b % 2), 2)
                pe.wait_ge(S("l_conv"), 4 * (b + 1))
                for g, a, w in PIECES:
                    wait(pe, S("l_gate"), n - 1)
                    nc.tensor.matmul(ps[:, BANK * (6 + n % 2):BANK * (6 + n % 2) + w], LRUW[:, g, b, :], TX[:, piece_cols(a, w)],
                                     start=True, stop=True).then_inc(S("l_piece"), 1)
                    n += 1
            pe_trios(pe, "g_lru", 0, 4)
            last = WH["g_lru"][1] + 3
            for q in (last - 1, last):
                pe.wait_ge(free(q), 2 * (q // 2) + 2)
            norm_sum(pe, NRML)
            pe.wait_ge(*of(NRML, "root", 1))
            pe.wait_ge(S("cc_conv"), 4 * CCK)
            for c in range(0, T, HALF):
                for b in range(4):
                    mm = nc.tensor.matmul(ps[:, c:c + HALF], ONES, CCO[:, b, c:c + HALF], start=(b == 0), stop=(b == 3))
            mm.then_inc(S("cc_sum"), 1)
            pe.wait_ge(S("cc_mean"), 1)
            norm_sum(pe, NRMV)
            pe.wait_ge(*of(NRMV, "root", 1))
            norm_sum(pe, NRMC)
            pe.wait_ge(*of(NRMC, "root", 1))
            feature_tiles(pe, WH["out_3"], 8, range(KB), xhi, xlo,
                          ready=lambda n: of(NRML, "lo", n + 1) if n < 4 else of(NRMC, "lo", n - 3))
            norm_sum(pe, NRMP)
            pe_groups(pe, "f3", lambda n: of(NRMP, "lo", n + 1))
            norm_sum(pe, NRME)

        def act_block3(act):
            if 2 not in blocks:
                for b in range(KB):
                    act.dma_start(H2I[:, b, :], xT[P * b:P * (b + 1), :]).then_inc(S("h2_in"), 16)
                act.wait_ge(S("h2_in"), 16 * KB)
                act.wait_ge(S("par_loaded"), 16)
            else:
                act.wait_ge(*of(NRMO, "sum", 1))
            act.dma_start(MT[:, :, :], metaT.rearrange("(b p) t -> p b t", p=P)).then_inc(S("meta_loaded"), 16)
            act.dma_start(LRUW[:, :, :, :].rearrange("p g b c -> p (g b c)"), lru_w).then_inc(S("lru_w_loaded"), 16)
            act.wait_ge(S("meta_loaded"), 16)
            for b in range(KB):
                norm_square(act, NRM3M, b)
            norm_root(act, NRM3M)
            norm_hi(act, NRM3M)
            for b in range(KB):
                if 2 in blocks:
                    act.wait_ge(*of(NRMO, "x", b + 1))
                norm_square(act, NRM3, b)
            act.dma_start(h_scr.rearrange("(b p) t -> p b t", p=P), H2I[:, :, :]).then_inc(S("h2_spilled"), 16)
            norm_root(act, NRM3)
            norm_hi(act, NRM3)
            nc.scalar.activation(NCT[:, :], par("lru_a_param_3", 0, 4), ACT.Abs).then_inc(S("rate_a"), 1)
            act.wait_ge(S("rate_a"), 1)
            nc.scalar.activation(NCT[:, :], NCT[:, :], ACT.Exp, scale=-1.0).then_inc(S("rate_a"), 1)
            act.wait_ge(S("rate_a"), 2)
            nc.scalar.activation(NCT[:, :], NCT[:, :], ACT.Ln, bias=1.0).then_inc(S("rate_a"), 1)
            act.wait_ge(S("h2_spilled"), 16)
            q0 = WH["x_lru"][1]
            for b in range(4):
                act.wait_ge(quad_ready, q0 + b + 1)
                nc.scalar.activation(XL_[:, b, 3 + META:3 + LW], trio(q0 + b), ACT.Copy).then_inc(free(q0 + b), 1)
                nc.scalar.activation(XL_[:, b, 3:3 + META], trio(q0 + b, T, META), ACT.Copy).then_inc(free(q0 + b), 1)
            act.wait_ge(S("rate_v"), 2)
            n = 0
            for b in range(4):
                name = ("v_cc", "g_cc")[b // 2]
                q0 = WH[name][1]
                for o in range(2 * (b % 2), 2 * (b % 2) + 2):
                    act.wait_ge(quad_ready, q0 + o + 1)
                    if name == "v_cc":
                        nc.scalar.activation(CC[:, o, PADC + META:PADC + LW], trio(q0 + o), ACT.Copy).then_inc(free(q0 + o), 1)
                        nc.scalar.activation(CC[:, o, PADC:PADC + META], trio(q0 + o, T, META), ACT.Copy).then_inc(free(q0 + o), 1)
                    else:
                        wait(act, S("c_gated"), o - 1)
                        nc.scalar.activation(SGC[:, o % 2, META:LW], trio(q0 + o), ACT.Sigmoid).then_inc(free(q0 + o), 1)
                        nc.scalar.activation(SGC[:, o % 2, 0:META], trio(q0 + o, T, META), ACT.Sigmoid).then_inc(free(q0 + o), 1)
                wait(act, S("l_scan"), b)
                for g, a, w in PIECES:
                    act.wait_ge(S("l_piece"), n + 1)
                    dst, bias = (TU, par("lru_gate_a_b_3", b)) if g == 0 else (TI, par("lru_gate_x_b_3", b))
                    nc.scalar.activation(dst[:, piece_cols(a, w)], ps[:, BANK * (6 + n % 2):BANK * (6 + n % 2) + w], ACT.Sigmoid,
                                         bias=bias).then_inc(S("l_gate"), 1)
                    n += 1
                act.wait_ge(S("l_gate"), n)
                nc.scalar.activation(TU[:, :], TU[:, :], ACT.Tanh, scale=NC4[:, b:b + 1]).then_inc(S("l_u"), 1)
                act.wait_ge(S("l_ix"), b + 1)
                act.wait_ge(S("l_u"), b + 1)
                nc.scalar.activation(TX[:, :], TU[:, :], ACT.Sqrt).then_inc(S("l_sq"), 1)
            q0 = WH["g_lru"][1]
            for b in range(4):
                act.wait_ge(quad_ready, q0 + b + 1)
                nc.scalar.activation(GL[:, b, :], trio(q0 + b), ACT.Gelu_apprx_tanh).then_inc(free(q0 + b), 2)
            for b in range(4):
                act.wait_ge(S("y_lru_done"), b + 1)
                norm_square(act, NRML, b)
            norm_root(act, NRML)
            norm_hi(act, NRML)
            act.wait_ge(S("cc_mean"), 1)
            for b in range(4):
                norm_square(act, NRMV, b)
            norm_root(act, NRMV)
            for b in range(4):
                act.wait_ge(S("cc_inv"), b + 1)
                nc.scalar.activation(CCO[:, b, :], CCO[:, b, :], ACT.Silu, bias=par("cc_ln_b_3", b),
                                     scale=par("cc_ln_g_3", b)).then_inc(S("cc_silu"), 1)
            for b in range(4):
                act.wait_ge(S("cc_silu"), b + 1)
                norm_square(act, NRMC, b)
            norm_root(act, NRMC)
            norm_hi(act, NRMC)
            act.wait_ge(*of(NRMC, "lo", 4))
            act.dma_start(H3[:, :, :], h_scr.rearrange("(b p) t -> p b t", p=P)).then_inc(S("h3_loaded"), 16)
            for b in range(KB):
                q = WH["out_3"][1] + b // 2
                act.wait_ge(free(q), freed(q, b % 2))
                norm_square(act, NRMP, b)
            norm_root(act, NRMP)
            norm_hi(act, NRMP)
            act.wait_ge(*of(NRMP, "lo", KB))
            act_groups(act, "f3")
            q0 = WH[f"down_3_{FF3 // 4 - 1}"][1]
            for b in range(KB):
                q = q0 + b // 2
                act.wait_ge(free(q), freed(q, b % 2))
                norm_square(act, NRME, b)
            norm_root(act, NRME)

        def dve_block3(dve):
            v = Line(dve, S("dve_line3"))
            dve.wait_ge(S("par_loaded"), 16)
            for b in range(KB):
                norm_add(dve, NRM3M, b)
            norm_apply(dve, NRM3M)
            for b in range(KB):
                norm_add(dve, NRM3, b)
            norm_apply(dve, NRM3)
            dve.wait_ge(S("h2_spilled"), 16)
            dve.wait_ge(*of(NRM3, "lo", KB))
            v.step(nc.vector.memset(CC[:, :, 0:PADC], 0.0))
            v.step(nc.vector.memset(XL_[:, :, 0:3], 0.0))
            v.wait()
            v.step(nc.vector.tensor_scalar(NC4[:, :], par("lru_a_param_3", 0, 4), -1.0, 0.0, ALU.mult, ALU.max))
            v.wait()
            dve.wait_ge(S("rate_a"), 3)
            nc.vector.tensor_tensor(NC4[:, :], NC4[:, :], NCT[:, :], ALU.add).then_inc(S("rate_v"), 1)
            dve.wait_ge(S("rate_v"), 1)
            nc.vector.tensor_scalar(NC4[:, :], NC4[:, :], LRU_HALF, None, ALU.mult).then_inc(S("rate_v"), 1)
            qx = WH["x_lru"][1]
            for b in range(4):
                dve.wait_ge(free(qx + b), 2 * ((qx + b) // 2) + 2)
                wait(dve, S("l_scan"), b)
                if b:
                    dve.wait_ge(S("y_kept"), b)
                nc.vector.tensor_scalar(TX[:, :], XL_[:, b, 0:LW], par("lru_conv_w_3", b), par("lru_conv_b_3", b),
                                        ALU.mult, ALU.add).then_inc(S("l_conv"), 1)
                for k in range(1, 4):
                    dve.wait_ge(S("l_conv"), 4 * b + k)
                    nc.vector.scalar_tensor_tensor(TX[:, :], XL_[:, b, k:k + LW], par("lru_conv_w_3", 4 * k + b), TX[:, :],
                                                   ALU.mult, ALU.add).then_inc(S("l_conv"), 1)
                dve.wait_ge(S("l_gate"), 6 * (b + 1))
                dve.wait_ge(S("l_conv"), 4 * b + 4)
                nc.vector.tensor_tensor(TI[:, :], TI[:, :], TX[:, :], ALU.mult).then_inc(S("l_ix"), 1)
                dve.wait_ge(S("l_u"), b + 1)
                v.step(nc.vector.tensor_scalar(TR[:, :], TU[:, :], 1.0, None, ALU.add))
                v.wait()
                v.step(nc.vector.reciprocal(TR[:, :], TR[:, :]))
                v.wait()
                dve.wait_ge(S("l_sq"), b + 1)
                v.step(nc.vector.scalar_tensor_tensor(TU[:, :], TU[:, :], 1.0, TR[:, :], ALU.subtract, ALU.mult, reverse0=True))
                dve.wait_ge(S("l_ix"), b + 1)
                v.step(nc.vector.scalar_tensor_tensor(TI[:, :], TI[:, :], 2.0, TX[:, :], ALU.mult, ALU.mult))
                v.wait()
                v.step(nc.vector.tensor_tensor(TI[:, :], TI[:, :], TR[:, :], ALU.mult))
                v.wait()
                nc.vector.tensor_tensor_scan(TX[:, :], TU[:, :], TI[:, :], 0.0, ALU.mult, ALU.add).then_inc(S("l_scan"), 1)
                dve.wait_ge(S("l_scan"), b + 1)
                nc.vector.tensor_copy(YL3[:, b, :], TX[:, META:LW]).then_inc(S("y_kept"), 1)
                qg = WH["g_cc"][1]
                for o in ((), (), (0, 1), (2, 3))[b]:
                    dve.wait_ge(free(qg + o), 2 * ((qg + o) // 2) + 2)
                    c = CC[:, o, PADC:PADC + LW]
                    nc.vector.tensor_tensor(c, c, SGC[:, o % 2, :], ALU.mult).then_inc(S("c_gated"), 1)
            dve.wait_ge(S("c_gated"), 4)
            for b in range(4):
                nc.vector.tensor_scalar(CCO[:, b, :], CC[:, b, META:META + T], par("cc_conv_w_3", b), par("cc_conv_b_3", b),
                                        ALU.mult, ALU.add).then_inc(S("cc_conv"), 1)
                for k in range(1, CCK):
                    dve.wait_ge(S("cc_conv"), CCK * b + k)
                    nc.vector.scalar_tensor_tensor(CCO[:, b, :], CC[:, b, META + k:META + k + T], par("cc_conv_w_3", 4 * k + b),
                                                   CCO[:, b, :], ALU.mult, ALU.add).then_inc(S("cc_conv"), 1)
            qg = WH["g_lru"][1]
            dve.wait_ge(S("y_kept"), 4)
            for b in range(4):
                dve.wait_ge(free(qg + b), 2 * ((qg + b) // 2) + 2)
                nc.vector.tensor_tensor(YL3[:, b, :], YL3[:, b, :], GL[:, b, :], ALU.mult).then_inc(S("y_lru_done"), 1)
            for b in range(4):
                norm_add(dve, NRML, b)
            norm_apply(dve, NRML)
            dve.wait_ge(S("cc_sum"), 1)
            for b in range(4):
                ins = nc.vector.scalar_tensor_tensor(CCO[:, b, :], ps[:, 0:T], -1.0 / 512, CCO[:, b, :], ALU.mult, ALU.add)
                ins.then_inc(S("cc_mean"), 1) if b == 3 else v.step(ins)
            for b in range(4):
                norm_add(dve, NRMV, b)
            dve.wait_ge(*of(NRMV, "root", 1))
            v.step(nc.vector.reciprocal(NRMV["inv"][:, :], NRMV["inv"][:, :]))
            v.wait()
            for b in range(4):
                nc.vector.tensor_tensor(CCO[:, b, :], CCO[:, b, :], NRMV["inv"][:, :], ALU.mult).then_inc(S("cc_inv"), 1)
            for b in range(4):
                norm_add(dve, NRMC, b)
            norm_apply(dve, NRMC)
            dve.wait_ge(S("h3_loaded"), 16)
            for b in range(KB):
                q = WH["out_3"][1] + b // 2
                dve.wait_ge(quad_ready, q + 1)
                nc.vector.tensor_tensor(H3[:, b, :], H3[:, b, :], half(q, b % 2), ALU.add).then_inc(free(q), 1)
                if b >= 1:
                    norm_add(dve, NRMP, b - 1)
            norm_add(dve, NRMP, KB - 1)
            norm_apply(dve, NRMP)
            dve.wait_ge(*of(NRMP, "lo", KB))
            dve_groups(dve, "f3", H3, NRME)
            norm_apply(dve, NRME)

        @block.tensor
        def _(pe):
            if 1 in blocks:
                pe_block1(pe)
            if 2 in blocks:
                pe_block2(pe)
            if 3 in blocks:
                pe_block3(pe)

        @block.vector
        def _(dve):
            if 1 in blocks:
                dve_block1(dve)
            if 2 in blocks:
                dve_block2(dve)
            if 3 in blocks:
                dve_block3(dve)

        @block.scalar
        def _(act):
            act.dma_start(PAR[:, :], params).then_inc(S("par_loaded"), 16)
            if 1 in blocks:
                act_block1(act)
            if 2 in blocks:
                act_block2(act)
            if 3 in blocks:
                act_block3(act)
            for b in range(KB):
                act.wait_ge(*of(NRME, "x", b + 1))
                act.dma_start(outT[P * b:P * (b + 1), :], H3[:, b, :]).then_inc(S("stored"), 16)
            act.wait_ge(S("stored"), 16 * KB)


def kernel(**inputs):
    import numpy as np
    import concourse.bacc as bacc
    from concourse.bass_utils import run_bass_kernel_spmd as run

    a = {k: np.asarray(v) for k, v in inputs.items()}
    a = {k: (v[0] if v.ndim > 1 and v.shape[0] == 1 else v) for k, v in a.items()}
    tiles, _ = plan(BLOCKS)
    stream = np.empty((len(tiles) // TILES, P, TILES, P), np.float32)
    for n, (w, k, c) in enumerate(tiles):
        stream[n // TILES, :, n % TILES, :] = a[w][P * k:P * (k + 1), P * c:P * (c + 1)]

    params = np.zeros((P, NPARAM), np.float32)

    def put(name, value):
        at, n = PARAMS[name]
        params[:, at:at + n] = value

    for name in ("norm_g", "conv_b", "mnorm_g", "skip_m", "dnorm_g", "mem_norm_g", "final_g", "norm_mix_2", "b_gate_2",
                 "norm_ffn_2", "norm_final_2", "norm_mix_g_3", "lru_conv_b_3", "lru_gate_a_b_3", "lru_gate_x_b_3",
                 "lru_a_param_3", "cc_conv_b_3", "cc_ln_g_3", "cc_ln_b_3", "out_norm_lru_g_3", "out_norm_cc_g_3",
                 "norm_mlp_g_3", "norm_final_g_3", "conv_w", "lru_conv_w_3", "cc_conv_w_3"):
        put(name, a[name].reshape(-1, P).T)
    params[0:4, PARAMS["b_if"][0]] = a["b_if"][0:4]
    params[32:36, PARAMS["b_if"][0]] = a["b_if"][4:8]
    put("lam", np.concatenate([a["lam_q1"], a["lam_k1"], a["lam_q2"], a["lam_k2"]])[None, :])
    w_if = np.zeros((P, 12, 36), np.float32)
    w_if[:, :, 0:4] = a["w_if"].reshape(12, P, 8)[:, :, 0:4].transpose(1, 0, 2)
    w_if[:, :, 32:36] = a["w_if"].reshape(12, P, 8)[:, :, 4:8].transpose(1, 0, 2)
    put("w_if", w_if.reshape(P, -1))
    i = np.arange(P)
    put("ident", i[:, None] == i[None, :])
    put("ones", 1.0)
    put("mask_ts", np.where(i[:, None] <= i[None, :], 0.0, NEG))
    put("mask_qk", np.where(i[None, :] <= i[:, None], 0.0, NEG))
    put("eps", EPS)

    wqkv = np.stack([a["wq_m"], a["wk_m"], a["wv_m"]]).transpose(2, 0, 1, 3).reshape(P, -1)

    row, col = np.arange(P)[:, None], np.arange(SPAN)[None, :]
    rel = np.clip(SPAN - P + row - col, -128, 128) + 128
    unseen = ((row < 64) & (col >= SPAN - 64)) | ((row >= 64) & (col < 64))
    bias2 = np.where(unseen[:, None, :], np.float32(NEG), a["att_rel_bias_2"][:, rel].transpose(1, 0, 2)).astype(np.float32)

    low = i[:, None] <= i[None, :]
    sgu = np.concatenate([np.where(low[:, None, :], a["sgu_w_2"].transpose(2, 0, 1), np.float32(0)).reshape(P, -1)]
                         + [np.broadcast_to(a[n].reshape(1, -1), (P, 512)) for n in ("sgu_b_2", "sgu_norm_gain_2", "sgu_norm_bias_2")],
                         axis=1).astype(np.float32)

    lru_w = np.zeros((2, 4, P, P), np.float32)
    for g, name in enumerate(("lru_gate_a_w_3", "lru_gate_x_w_3")):
        for h in range(8):
            o = 64 * (h % 2)
            lru_w[g, h // 2, o:o + 64, o:o + 64] = a[name][h]
    lru_w = lru_w.transpose(2, 0, 1, 3).reshape(P, -1)

    arrays = {"xT": a["x"].T, "memT": a["mem"].T, "stream": stream.reshape(-1, P, SLOT), "params": params, "wqkv": wqkv,
              "sgu": sgu, "bias2": bias2.reshape(P, -1), "lru_w": lru_w, "metaT": a["meta_tokens_3"].T}
    arrays = {k: np.ascontiguousarray(v, dtype=np.float32) for k, v in arrays.items()}
    nc = bacc.Bacc("TRN2", target_bir_lowering=False, num_devices=1)
    args = [nc.dram_tensor(k, v.shape, F32, kind="ExternalInput").ap() for k, v in arrays.items()]
    args.append(nc.dram_tensor("outT", (D, T), F32, kind="ExternalOutput").ap())
    args.append(nc.dram_tensor("o_scr", (NT, P, 512), F32, kind="Internal").ap())
    args.append(nc.dram_tensor("h_scr", (D, T), F32, kind="Internal").ap())
    build(nc, *args, blocks=BLOCKS)
    r = run(nc, [arrays], core_ids=[0])
    return np.ascontiguousarray(r.results[0]["outT"].T)[None]
```

```python
import math
from contextlib import ExitStack

import concourse.bass as bass
from concourse import mybir
from concourse.alu_op_type import AluOpType as ALU

F32 = mybir.dt.float32
F32R = mybir.dt.float32r
ACT = mybir.ActivationFunctionType
AX = mybir.AxisListType.X

P = 128
D = 1024
KB = D // P
T = 1024
NT = T // P
HALF = 512
BANK = 512
QUAD = 4 * BANK
TILES = 16
SLOT = TILES * P
H1 = 4
MEM = 256
EPS = 1e-6
NEG = -1e30
LAM_INIT = 0.8 - 0.6 * math.exp(-0.3 * 0)
HEADS2 = 8
SPAN = 640
FF2 = 22
FF3 = 32
META = 16
LW = T + META
CCK = 31
LRU_C = 8.0


PAIRS3 = (("x_0", (0, 1)), ("vg_0", (8, 12)), ("x_2", (2, 3)), ("vg_1", (9, 13)), ("vg_2", (10, 14)), ("vg_3", (11, 15)),
          ("g_0", (4, 5)), ("g_2", (6, 7)))


def plan(blocks):
    tiles, where = [], {}
    slot = quad = 0

    def add(name, items, quads):
        nonlocal slot, quad
        assert len(items) % TILES == 0
        where[name] = (slot, quad)
        tiles.extend(items)
        slot += len(items) // TILES
        quad += quads

    def feature(name, w, col, outs, ks=range(KB)):
        add(name, [(w, k, col + o) for o in range(outs) for k in ks], outs // 2)

    def token(name, w, col, outs):
        add(name, [(w, k, col + 2 * s + c) for s in range(outs // 2) for k in range(KB) for c in range(2)], outs // 2)

    if 1 in blocks:
        feature("x_m", "w_in", 0, 4)
        token("o_m", "w_in", 4, 4)
        feature("q_d", "w_in", 12, 4)
        feature("k_d", "w_in", 16, 4)
        token("v_d", "w_in", 20, 4)
        feature("mem_k", "w_mem_kv", 0, 4)
        token("mem_v", "w_mem_kv", 4, 4)
        feature("q_c", "w_in", 28, 4)
        feature("z_m", "w_in", 8, 4)
        feature("z_d", "w_in", 24, 4)
        feature("z_c", "w_in", 32, 4)
        feature("out_1", "w_out", 0, 8, range(12))
    if 2 in blocks:
        feature("q_2", "w_in_2", 0, 4)
        feature("k_2", "w_in_2", 4, 4)
        token("v_2", "w_in_2", 8, 4)
        for branch, gate, w in ((0, 20, "w_br_att_2"), (1, 28, "w_br_sgu_2")):
            if branch == 1:
                token("vs_2", "w_in_2", 16, 4)
                feature("u_2", "w_in_2", 12, 4)
            for pair in range(2):
                feature(f"gate_{branch}{pair}", "w_in_2", gate + 4 * pair, 4)
                feature(f"branch_{branch}{pair}", w, 4 * pair, 4, range(4))
        feature("out_2", "w_out_2", 0, 8)
        for g in range(0, FF2, 4):
            n = min(4, FF2 - g)
            add(f"up_2_{g // 4}", [("w_ffn_in_2", k, (0, FF2)[o] + g + j) for j in range(n) for o in range(2) for k in range(KB)], n)
            feature(f"down_2_{g // 4}", "w_ffn_out_2", 0, 8, range(g, g + n))
    if 3 in blocks:
        for name, cols in PAIRS3:
            add(name, [("w_in_3", k, col) for col in cols for k in range(KB)], 2)
        feature("out_3", "w_out_3", 0, 8)
        for g in range(FF3 // 4):
            add(f"up_3_{g}", [("w_mlp_up_3", k, 4 * g + j) for j in range(4) for k in range(KB)], 4)
            feature(f"down_3_{g}", "w_mlp_down_3", 0, 8, range(4 * g, 4 * g + 4))
    return tiles, where


PARAMS = {}


def param_columns():
    at = 0
    for name, n in (("norm_g", 8), ("conv_w", 16), ("conv_b", 4), ("mnorm_g", 4), ("skip_m", 4), ("dnorm_g", 4),
                    ("mem_norm_g", 8), ("final_g", 8), ("norm_mix_2", 8), ("b_gate_2", 16), ("norm_ffn_2", 8),
                    ("norm_final_2", 8), ("norm_mix_g_3", 8), ("lru_conv_w_3", 16), ("lru_conv_b_3", 4),
                    ("lru_gate_a_b_3", 4), ("lru_gate_x_b_3", 4), ("lru_a_param_3", 4), ("cc_conv_w_3", 4 * CCK),
                    ("cc_conv_b_3", 4), ("cc_ln_g_3", 4), ("cc_ln_b_3", 4), ("out_norm_lru_g_3", 4),
                    ("out_norm_cc_g_3", 4), ("norm_mlp_g_3", 8), ("norm_final_g_3", 8), ("b_if", 1), ("lam", 256),
                    ("w_if", 12 * 36), ("ident", 128), ("ones", 128), ("mask_ts", 128), ("mask_qk", 128), ("eps", 1)):
        PARAMS[name] = (at, n)
        at += n
    return at


NPARAM = param_columns()


class Line:

    def __init__(self, eng, sem):
        self.eng, self.sem, self.n = eng, sem, 0

    def step(self, ins):
        ins.then_inc(self.sem, 1)
        self.n += 1
        return self.n

    def wait(self, n=None):
        self.eng.wait_ge(self.sem, self.n if n is None else n)


def wait(eng, sem, n):
    if isinstance(n, int) and n <= 0:
        return
    eng.wait_ge(sem, n)


def up(base, loop):
    return base if loop is None else loop[0] * loop[1] + base

BLOCKS = (1,2,3,)


def build(nc, xT, memT, stream, params, wqkv, sgu, bias2, lru_w, metaT, outT, o_scr, h_scr, blocks=(1, 2, 3)):
    TL, WH = plan(blocks)
    NSLOT = len(TL) // TILES
    with ExitStack() as ctx:
        sems = {}

        def S(name):
            if name not in sems:
                sems[name] = ctx.enter_context(nc.semaphore(name))
            return sems[name]

        base = -(-nc.sbuf_base // 32) * 32

        def at(name, offset, shape, dt=F32):
            return nc.alloc_sbuf_tensor_at(name, shape, dt, offset=base + offset)

        ps = ctx.enter_context(nc.psum_tensor("ps", [P, 8 * BANK], F32))

        RAW = at("raw", 0, [P, 2, TILES, P])
        WHI = at("whi", 16384, [P, 2, TILES, P], F32R)
        WLO = at("wlo", 32768, [P, 2, TILES, P], F32R)
        X = 49152
        XHI = at("xhi", X, [P, KB, T], F32R)
        XLO = at("xlo", X + 32768, [P, KB, T], F32R)
        C = X + 66560
        PAR = at("par", C, [P, NPARAM])
        A = C + 8512
        small_at = [C + -(-4 * NPARAM // 32) * 32]

        def small(name, shape):
            offset = small_at[0]
            small_at[0] += -(-4 * math.prod(shape[1:]) // 32) * 32
            assert small_at[0] <= A
            return at(name, offset, shape)

        def par(name, j=0, n=1, rows=slice(0, P)):
            return PAR[rows, PARAMS[name][0] + j:PARAMS[name][0] + j + n]

        NCOL = small("norm_columns", [P, KB])
        H = at("h1", A, [P, KB, T])

        IDENT, ONES = par("ident", 0, P), par("ones", 0, P)
        EPSC = par("eps")

        def half(quad, ob):
            c = QUAD * (quad % 2) + 2 * BANK * ob
            return ps[:, c:c + 2 * BANK]

        def free(quad):
            return S(f"quad_free{quad % 2}")

        def freed(quad, ob, loop=None):
            return up(2 * (quad // 2) + ob + 1, loop)

        quad_ready, split_done, slot_used, hi_done = S("quad_ready"), S("split_done"), S("slot_used"), S("hi_done")
        raw_loaded = [S("raw_loaded0"), S("raw_loaded1")]

        norm_counts = dict(sq=0, add=0, sum=0, root=0, recip=0, diag=0, inv=0, x=0, hi=0, lo=0)

        def norm_set(name, src, n, gain, scr, before, nb=KB, hi=None, lo=None, out=None, bank=0):
            N = dict(bank=QUAD * ((before + 1) % 2) + BANK * bank, src=src, n=n, gain=gain, nb=nb, hi=hi, lo=lo, out=out, before=dict(norm_counts),
                     sq=at(f"{name}_sq", scr, [P, 2, n]), acc=at(f"{name}_acc", scr + 8 * n, [P, n]),
                     diag=at(f"{name}_diag", scr + 12 * n, [P, n]))
            applied = nb if gain else 0
            cut = nb if hi else 0
            for step, k in (("sq", nb), ("add", nb - 1), ("sum", 1), ("root", 1), ("recip", 1), ("diag", 1),
                            ("inv", 1), ("x", applied), ("hi", cut), ("lo", cut)):
                norm_counts[step] += k
            return N

        def of(N, step, n):
            return S("norm_" + step), N["before"][step] + n

        def norm_square(act, N, b):
            if b >= 2:
                act.wait_ge(*of(N, "add", b - 1))
            dst = N["acc"][:, :] if b == 0 else N["sq"][:, b % 2, :]
            nc.scalar.activation(dst, N["src"](b), ACT.Square).then_inc(S("norm_sq"), 1)

        def norm_add(dve, N, b):
            if b == 0:
                return
            dve.wait_ge(*of(N, "sq", b + 1))
            if b >= 2:
                dve.wait_ge(*of(N, "add", b - 1))
            nc.vector.tensor_tensor(N["acc"][:, :], N["acc"][:, :], N["sq"][:, b % 2, :], ALU.add)\
                .then_inc(S("norm_add"), 1)

        def norm_tiles(N):
            return [(j, min(P, N["n"] - P * j)) for j in range(-(-N["n"] // P))]

        def norm_sum(pe, N):
            pe.wait_ge(*of(N, "add", N["nb"] - 1))
            for j, w in norm_tiles(N):
                mm = nc.tensor.matmul(ps[0:w, N["bank"] + j:N["bank"] + j + 1], N["acc"][:, P * j:P * j + w],
                                      par("ones", 0, 1), start=True, stop=True)
            mm.then_inc(S("norm_sum"), 1)
            pe.wait_ge(*of(N, "diag", 1))
            for c in range(0, N["n"], HALF):
                w, rows = min(HALF, N["n"] - c), min(P, N["n"])
                mm = nc.tensor.matmul(ps[:, N["bank"] + c:N["bank"] + c + w], ONES[0:rows, :], N["diag"][0:rows, c:c + w],
                                      start=True, stop=True)
            mm.then_inc(S("norm_inv"), 1)

        def norm_root(act, N):
            act.wait_ge(*of(N, "sum", 1))
            tiles, rows = len(norm_tiles(N)), min(P, N["n"])
            nc.scalar.activation(NCOL[0:rows, 0:tiles], ps[0:rows, N["bank"]:N["bank"] + tiles], ACT.Sqrt, bias=EPSC[0:rows, :],
                                 scale=1.0 / (N["nb"] * P)).then_inc(S("norm_root"), 1)

        def norm_inv(dve, N):
            tiles, rows = len(norm_tiles(N)), min(P, N["n"])
            dve.wait_ge(*of(N, "root", 1))
            nc.vector.reciprocal(NCOL[0:rows, 0:tiles], NCOL[0:rows, 0:tiles]).then_inc(S("norm_recip"), 1)
            dve.wait_ge(*of(N, "recip", 1))
            nc.vector.tensor_tensor(N["diag"][0:rows, :].rearrange("p (j t) -> p j t", j=tiles),
                                    IDENT[0:rows, 0:rows].unsqueeze(1).to_broadcast([rows, tiles, rows]),
                                    NCOL[0:rows, 0:tiles].unsqueeze(2).to_broadcast([rows, tiles, rows]), ALU.mult)\
                .then_inc(S("norm_diag"), 1)
            dve.wait_ge(*of(N, "inv", 1))
            return ps[:, N["bank"]:N["bank"] + N["n"]]

        def norm_apply(dve, N, following=None):
            inv = norm_inv(dve, N)
            for b in range(N["nb"] + 1):
                if b < N["nb"]:
                    dst = N["out"](b) if N["out"] else N["sq"][:, b % 2, :]
                    if not N["out"] and b >= 2:
                        dve.wait_ge(*of(N, "lo", b - 1))
                    nc.vector.scalar_tensor_tensor(dst, N["src"](b), N["gain"](b), inv, ALU.mult, ALU.mult)\
                        .then_inc(S("norm_x"), 1)
                if following and b >= 1:
                    norm_add(dve, following, b - 1)
                if b >= 1 and not N["out"]:
                    dve.wait_ge(*of(N, "hi", b))
                    nc.vector.tensor_tensor(N["lo"](b - 1), N["sq"][:, (b - 1) % 2, :], N["hi"](b - 1).bitcast(F32),
                                            ALU.subtract).then_inc(S("norm_lo"), 1)

        def norm_hi(act, N):
            for b in range(N["nb"]):
                act.wait_ge(*of(N, "x", b + 1))
                nc.scalar.activation(N["hi"](b), N["sq"][:, b % 2, :], ACT.Copy).then_inc(S("norm_hi"), 1)

        def slot_start(pe, slot, loop):
            pe.wait_ge(split_done, up(slot + 1, loop))

        def quad_start(pe, quad, loop=None):
            n = 2 * (quad // 2)
            if loop is not None or n > 0:
                pe.wait_ge(free(quad), up(n, loop))

        def feature_tiles(pe, where, outs, ks, xhi, xlo, chunks=((0, HALF, 0), (HALF, HALF, BANK)), ready=None,
                          qloop=None, sloop=None, o_per_quad=2):
            slot, quad = where
            t = 0
            for o in range(outs):
                q = quad + o // o_per_quad
                if o % o_per_quad == 0:
                    quad_start(pe, q, qloop)
                c0 = QUAD * (q % 2) + 2 * BANK * (o % o_per_quad)
                for n, k in enumerate(ks):
                    s, r = slot + t // TILES, (slot + t // TILES) % 2
                    first = t % TILES == 0
                    if first:
                        slot_start(pe, s, sloop)
                    if ready and o == 0:
                        pe.wait_ge(*ready(n))
                    w_hi, w_lo = WHI[:, r, t % TILES, :], WLO[:, r, t % TILES, :]
                    for m, (w, x) in enumerate(((w_hi, xhi), (w_hi, xlo), (w_lo, xhi))):
                        for a, width, c in chunks:
                            mm = nc.tensor.matmul(ps[:, c0 + c:c0 + c + width], w, x(k, a, width),
                                                  start=(n == 0 and m == 0), stop=(n == len(ks) - 1 and m == 2))
                            if first and (s > 0 or sloop is not None):
                                mm.then_inc(slot_used, 1)
                            first = False
                    t += 1
                if o % o_per_quad == o_per_quad - 1:
                    mm.then_inc(quad_ready, 1)

        def token_tiles(pe, where, slots, xhi, xlo, nt=NT, ready=None):
            slot, quad = where
            for i in range(slots):
                s, q = slot + i, quad + i
                r = s % 2
                quad_start(pe, q)
                slot_start(pe, s, None)
                first = s > 0
                for tt in range(nt):
                    c = QUAD * (q % 2) + 256 * tt
                    for k in range(KB):
                        if ready and i == 0 and tt == 0:
                            pe.wait_ge(*ready(k))
                        w_hi = WHI[:, r, 2 * k:2 * k + 2, :].rearrange("p a b -> p (a b)")
                        w_lo = WLO[:, r, 2 * k:2 * k + 2, :].rearrange("p a b -> p (a b)")
                        a = tt * P
                        for m, (x, w) in enumerate(((xhi, w_hi), (xhi, w_lo), (xlo, w_hi))):
                            mm = nc.tensor.matmul(ps[:, c:c + 256], x(k, a, P), w, start=(k == 0 and m == 0),
                                                  stop=(k == KB - 1 and m == 2))
                            if first:
                                mm.then_inc(slot_used, 1)
                            first = False
                mm.then_inc(quad_ready, 1)

        xhi = lambda k, a, w: XHI[:, k, a:a + w]
        xlo = lambda k, a, w: XLO[:, k, a:a + w]

        block = ctx.enter_context(nc.Block())

        @block.sync
        def _(sp):
            def load(s, r, loop):
                sp.dma_start(RAW[:, r], stream[s].rearrange("p (t c) -> p t c", c=P)).then_inc(raw_loaded[r], 16)

            load(0, 0, None)
            load(1, 1, None)
            with sp.Fori(1, NSLOT // 2) as i:
                for r in range(2):
                    sp.wait_ge(split_done, i * 2 + (r - 1))
                    sp.dma_start(RAW[:, r], stream[bass.ds(i * 2 + r, 1)].rearrange("s p (t c) -> p (s t) c", c=P))\
                        .then_inc(raw_loaded[r], 16)
            if NSLOT % 2:
                sp.wait_ge(split_done, NSLOT - 2)
                load(NSLOT - 1, 0, None)

        @block.gpsimd
        def _(pool):
            def split(r, loads, done, used):
                pool.wait_ge(raw_loaded[r], loads)
                if used is not None:
                    pool.wait_ge(slot_used, used)
                flat = lambda x: x[:, r].rearrange("p t c -> p (t c)")
                one = par("ones").to_broadcast([P, SLOT])
                nc.gpsimd.tensor_tensor(flat(WHI), flat(RAW), one, ALU.mult).then_inc(hi_done, 1)
                pool.wait_ge(hi_done, done)
                nc.gpsimd.tensor_tensor(WLO[:, r], RAW[:, r], WHI[:, r].bitcast(F32), ALU.subtract)\
                    .then_inc(split_done, 1)

            pool.wait_ge(S("par_loaded"), 16)
            split(0, 16, 1, None)
            split(1, 16, 2, None)
            with pool.Fori(1, NSLOT // 2) as i:
                for r in range(2):
                    split(r, i * 16 + 16, i * 2 + (r + 1), i * 2 + (r - 1))
            if NSLOT % 2:
                split(0, 16 * (NSLOT // 2 + 1), NSLOT, NSLOT - 2)

        if 1 in blocks:
            XS = at("x_in", A, [P, KB, T])
            NRM1 = norm_set("n1", lambda b: XS[:, b, :], T, lambda b: par("norm_g", b), A + 32768, WH["x_m"][1],
                            hi=lambda b: XHI[:, b, :], lo=lambda b: XLO[:, b, :])
            PR = at("pre", A, [P, 12, T])
            XCV = PR[:, 0:4, :]
            QT = at("q_t", A + 16384, [P, H1, T])
            KT = at("k_t", A + 32768, [P, H1, T])
            OSTG = at("o_staged", A + 16384, [P, 2, NT, 256])
            V1 = at("v_one", A + 49152, [P, NT, H1, P + 1])
            XM_AT = A + 65664
            XM = at("x_m", XM_AT, [P, H1, T + 3])
            WQKV = at("w_qkv", XM_AT + 16448, [P, 3, H1, P])
            R1 = at("row_1", XM_AT, [4, T])
            R4 = at("row_4", XM_AT + 4096, [4, T])
            R0 = at("row_0", XM_AT + 8192, [4, T])
            R2 = at("row_2", XM_AT + 12288, [4, T])
            R3 = at("row_3", XM_AT + 16384, [4, T])
            CH = XM_AT + 8192
            EW = at("e_w", CH, [P, H1, P])
            QS = at("q_s", CH + 2048, [P, H1, P])
            KW = at("k_w", CH + 4096, [P, H1, P])
            OSC = at("o_sig", CH + 6144, [P, 2, HALF])
            CS = at("c_state", CH + 10240, [P, H1, P + 1])
            COL = small("cols", [P, NT, 12])
            MPREV = small("m_prev", [4, NT])
            DEC = small("decay", [P, 4])
            DN = small("denom", [P, 4])
            ST = small("stats", [P, 4, 6])
            MV = small("mean_var", [P, NT * H1, 2])
            SD = small("std", [P, NT * H1])
            LM = small("lam", [P, 4])
            GD = small("g_d", [P, 4])
            SM = small("soft", [P, 4, 8])
            OS1 = small("o_stat", [P, 2, H1 * NT])
            SMC = small("soft_c", [P, 2, 12])
            LTMP = at("lam_tmp", A + 65536, [P, 64])

            KD = KT
            VD = at("v_d", A + 49152, [P, NT, HALF])
            P0 = [at("p0_0", A + 65536, [P, 896]), at("p0_1", A + 69120, [P, T])]
            P1 = [at("p1_0", A + 73216, [P, 896]), at("p1_1", A + 76800, [P, T])]
            PTD = [at("p_t0", A + 84992, [P, 896]), at("p_t1", A + 80896, [P, T])]
            OSQ = at("o_squares", X + 65536, [P, 2, P])

            KM = at("k_mem", A + 49152, [P, H1, MEM])
            VM = at("v_mem", A + 53248, [P, 2, HALF])
            MXH = at("mem_hi", A + 57344, [P, KB, MEM], F32R)
            MXL = at("mem_lo", A + 65536, [P, KB, MEM], F32R)
            MS = at("mem_in", A + 73728, [P, KB, MEM])
            NRMM = norm_set("nm", lambda b: MS[:, b, :], MEM, lambda b: par("mem_norm_g", b), A + 81920, WH["mem_k"][1],
                            hi=lambda b: MXH[:, b, :], lo=lambda b: MXL[:, b, :])
            mhi = lambda k, a, w: MXH[:, k, a:a + w]
            mlo = lambda k, a, w: MXL[:, k, a:a + w]
            QC = PR[:, 8:12, :]
            PC = at("p_c", A + 57344, [P, 2, H1 * MEM])
            PTC = at("p_ct", A + 65536, [P, 2 * H1 * P])

            YH = at("y_hi", A + 49152, [P, 8, T], F32R)
            YHC = at("y_hi_c", X, [P, 4, T], F32R)
            YL = at("y_lo", A, [P, 12, T], F32R)
            SIL = at("silu_z", A + 81920, [P, T])
            yhi = lambda k, a, w: YH[:, k, a:a + w] if k < 8 else YHC[:, k - 8, a:a + w]
            ylo = lambda k, a, w: YL[:, k, a:a + w]
            HX = at("x_again", X + 16384, [P, KB, T])
            NRMF = norm_set("nf", lambda b: HX[:, b, :], T, lambda b: par("final_g", b), X + 49152, 0,
                            out=lambda b: H[:, b, :])
            STEPS = [(h, j) for h in range(H1) for j in range(NT)]
            SC1 = float(P) ** -0.5
            SCD = 64.0 ** -0.5

        def num(h):
            c = BANK * (4 + h // 2) + (P + 1) * (h % 2)
            return ps[:, c:c + P + 1]

        def cup(h):
            c = BANK * (6 + h // 2) + (P + 1) * (h % 2)
            return ps[:, c:c + P + 1]

        def work(n):
            return 2 * BANK + 2 * BANK * (n % 2)

        def pe_block1(pe):
            pe.wait_ge(S("par_loaded"), 16)
            norm_sum(pe, NRM1)
            feature_tiles(pe, WH["x_m"], 4, range(KB), xhi, xlo, ready=lambda n: of(NRM1, "lo", n + 1))
            token_tiles(pe, WH["o_m"], 2, xhi, xlo)
            pe.wait_ge(S("wqkv_loaded"), 16)
            for q in WH["o_m"][1], WH["o_m"][1] + 1:
                quad_start(pe, q + 2)
            for n in range(13):
                if n < 12:
                    h = n % 4
                    kind = n // 4
                    if kind == 1:
                        pe.wait_ge(S("silu_done"), h + 1)
                    wait(pe, S("qkv_kept"), n - 1)
                    for c in range(2):
                        x = XM[:, h, 3 + HALF * c:3 + HALF * (c + 1)] if kind == 0 else XCV[:, h, HALF * c:HALF * (c + 1)]
                        mm = nc.tensor.matmul(ps[:, work(n) + HALF * c:work(n) + HALF * (c + 1)],
                                              WQKV[:, (2, 0, 1)[kind], h, :], x, start=True, stop=True)
                    mm.then_inc(S("qkv_ready"), 1)
                if n >= 1:
                    m = n - 1
                    src = KT[:, m % 2, :] if m < 4 else (QT if m < 8 else KT)[:, m % 4, :]
                    blk = (8, 0, 4)[m // 4] + m % 4
                    pe.wait_ge(S("qkv_kept"), m + 1)
                    for c in range(2):
                        mm = nc.tensor.matmul(ps[0:36, HALF * c:HALF * (c + 1)], par("w_if", 36 * blk, 36),
                                              src[:, HALF * c:HALF * (c + 1)], start=(m == 0), stop=(m == 11))
                    mm.then_inc(S("gate_sum"), 1)
                if n == 3:
                    for tt in range(NT):
                        wait(pe, S("vt_kept"), tt - 1)
                        for g in range(H1):
                            c = BANK * (6 + tt % 2) + P * g
                            mm = nc.tensor.matmul(ps[:, c:c + P], XM[:, g, 3 + P * tt:3 + P * (tt + 1)], WQKV[:, 2, g, :],
                                                  start=True, stop=True)
                        mm.then_inc(S("vt_ready"), 1)
            pe.wait_ge(S("rows_a"), 6)
            for c in range(NT):
                for n, row in enumerate((R3, R0, R2)):
                    a = 2 * BANK + 12 * c + 4 * n
                    mm = nc.tensor.transpose(ps[:, a:a + 4], row[:, P * c:P * (c + 1)], IDENT[0:4, 0:4])
            mm.then_inc(S("cols_ready"), 1)
            pe.wait_ge(S("rows_v"), 13)
            pe.wait_ge(S("cols_kept"), 1)
            for c in range(NT + 1):
                if c >= 1:
                    pe.wait_ge(S("pt_done"), c)
                    wait(pe, S("c_done"), c - 1)
                    for h in range(H1):
                        mm = nc.tensor.matmul(num(h), EW[:, h, :], V1[:, c - 1, h, :], start=True, stop=(c == 1))
                        if c > 1:
                            mm = nc.tensor.matmul(num(h), QS[:, h, :], CS[:, h, :], start=False, stop=True)
                    mm.then_inc(S("num_ready"), 1)
                    for h in range(H1):
                        mm = nc.tensor.matmul(cup(h), KW[:, h, :], V1[:, c - 1, h, :], start=True, stop=True)
                    mm.then_inc(S("cu_ready"), 1)
                if c < NT:
                    for h in range(H1):
                        sel = IDENT[0:4, h:h + 1].to_broadcast([4, P])
                        nc.tensor.matmul(ps[:, P * h:P * (h + 1)], sel, R4[:, P * c:P * (c + 1)], start=True, stop=True)
                    for h in range(H1):
                        sel = IDENT[0:4, h:h + 1].to_broadcast([4, P])
                        mm = nc.tensor.matmul(ps[:, BANK + P * h:BANK + P * (h + 1)], sel, R1[:, P * c:P * (c + 1)],
                                              start=True, stop=True)
                    mm.then_inc(S("bc_ready"), 1)
                    for h in range(H1):
                        mm = nc.tensor.transpose(ps[:, 3 * BANK + P * h:3 * BANK + P * (h + 1)], KT[:, h, P * c:P * (c + 1)],
                                                 IDENT)
                    mm.then_inc(S("kt_ready"), 1)
                    for h in range(H1):
                        mm = nc.tensor.matmul(ps[:, 2 * BANK + P * h:2 * BANK + P * (h + 1)], KT[:, h, P * c:P * (c + 1)],
                                              QT[:, h, P * c:P * (c + 1)], start=True, stop=True)
                    mm.then_inc(S("sc_ready"), 1)

            slot, quad = WH["q_d"]
            feature_tiles(pe, (slot, quad), 2, range(KB), xhi, xlo)
            pe.wait_ge(S("c_done"), NT)
            for g in range(2 * H1):
                pe.wait_ge(S("hn_done"), g + 1)
                wait(pe, S("pre_done"), g - 1)
                for k in range(4):
                    c = BANK * (6 + g % 2) + P * k
                    mm = nc.tensor.transpose(ps[:, c:c + P], QT[:, g // 2, P * (4 * (g % 2) + k):P * (4 * (g % 2) + k + 1)], IDENT)
                mm.then_inc(S("ht_ready"), 1)
            pe.wait_ge(S("pre_done"), 2 * H1)
            feature_tiles(pe, (slot + 1, quad + 1), 2, range(KB), xhi, xlo)
            feature_tiles(pe, WH["k_d"], 4, range(KB), xhi, xlo)
            token_tiles(pe, WH["v_d"], 2, xhi, xlo)
            last = WH["v_d"][1] + 1
            quad_start(pe, last + 1)
            quad_start(pe, last + 2)
            n_steps = len(STEPS)
            for i in range(n_steps + 2):
                if i < n_steps:
                    h, j = STEPS[i]
                    for m in range(2):
                        wait(pe, S("d_exp"), 2 * i + m - 1)
                        rows = slice(64 * m, 64 * m + 64)
                        n = P * (j + 1)
                        for c in range(0, n, HALF):
                            w = min(HALF, n - c)
                            diag = c + w == n
                            mm = nc.tensor.matmul(ps[:, 2 * BANK * m + c:2 * BANK * m + c + w], QT[rows, h, P * j:P * (j + 1)],
                                                  KD[rows, h, c:c + w], start=True, stop=not diag)
                            if diag:
                                e = 2 * BANK * m + n - P
                                mm = nc.tensor.matmul(ps[:, e:e + P], IDENT, par("mask_qk", 0, P), start=False, stop=True)
                        mm.then_inc(S("d_scores"), 1)
                if 1 <= i <= n_steps:
                    s, (h, j) = i - 1, STEPS[i - 1]
                    pe.wait_ge(S("d_p"), s + 1)
                    wait(pe, S("d_ptk"), s)
                    for k in range(j + 1):
                        mm = nc.tensor.transpose(ps[:, 4 * BANK + P * k:4 * BANK + P * (k + 1)],
                                                 P0[s % 2][:, P * k:P * (k + 1)], IDENT)
                    mm.then_inc(S("d_pt"), 1)
                if i >= 2:
                    s, (h, j) = i - 2, STEPS[i - 2]
                    c = BANK * (6 + s % 2)
                    pe.wait_ge(S("d_ptk"), s + 1)
                    wait(pe, S("d_on"), s - 1)
                    for k in range(j + 1):
                        mm = nc.tensor.matmul(ps[:, c:c + P], PTD[s % 2][:, P * k:P * (k + 1)],
                                              VD[:, k, P * h:P * (h + 1)], start=(k == 0), stop=(k == j))
                    mm.then_inc(S("d_o"), 1)
            for g in range(2 * H1):
                pe.wait_ge(S("d_norm"), g // 2 + 1)
                if g < 2:
                    pe.wait_ge(S("d_on"), n_steps)
                wait(pe, S("d_od"), g - 1)
                for k in range(4):
                    c = BANK * (6 + g % 2) + P * k
                    mm = nc.tensor.transpose(ps[:, c:c + P], QT[:, g // 2, P * (4 * (g % 2) + k):P * (4 * (g % 2) + k + 1)], IDENT)
                mm.then_inc(S("d_ot"), 1)
            pe.wait_ge(S("d_od"), 2 * H1)

            norm_sum(pe, NRMM)
            mem_chunk = ((0, MEM, 0),)
            feature_tiles(pe, WH["mem_k"], 4, range(KB), mhi, mlo, chunks=mem_chunk, ready=lambda n: of(NRMM, "lo", n + 1))
            token_tiles(pe, WH["mem_v"], 2, mhi, mlo, nt=2)
            feature_tiles(pe, WH["q_c"], 4, range(KB), xhi, xlo)
            last = WH["q_c"][1] + 1
            quad_start(pe, last + 1)
            quad_start(pe, last + 2)
            for j in range(NT + 1):
                if j < NT:
                    wait(pe, S("c_exp"), j)
                    for h in range(H1):
                        mm = nc.tensor.matmul(ps[:, MEM * h:MEM * (h + 1)], QC[:, h, P * j:P * (j + 1)], KM[:, h, :],
                                              start=True, stop=True)
                    mm.then_inc(S("c_scores"), 1)
                if j >= 1:
                    s = j - 1
                    pe.wait_ge(S("c_p"), s + 1)
                    wait(pe, S("c_ptk"), s)
                    for n in range(2 * H1):
                        mm = nc.tensor.transpose(ps[:, 2 * BANK + P * n:2 * BANK + P * (n + 1)],
                                                 PC[:, s % 2, P * n:P * (n + 1)], IDENT)
                    mm.then_inc(S("c_pt"), 1)
                    pe.wait_ge(S("c_ptk"), s + 1)
                    wait(pe, S("c_oc"), s)
                    for h in range(H1):
                        for m in range(2):
                            mm = nc.tensor.matmul(ps[:, 4 * BANK + P * h:4 * BANK + P * (h + 1)], VM[:, m, P * h:P * (h + 1)],
                                                  PTC[:, P * (2 * h + m):P * (2 * h + m + 1)], start=(m == 0), stop=(m == 1))
                    mm.then_inc(S("c_o"), 1)
            pe.wait_ge(S("c_oc"), NT)

            for z in ("z_m", "z_d", "z_c"):
                feature_tiles(pe, WH[z], 4, range(KB), xhi, xlo)
            feature_tiles(pe, WH["out_1"], 8, range(12), yhi, ylo, ready=lambda n: (S("y_lo"), n + 1))
            norm_sum(pe, NRMF)

        def act_block1(act):
            for b in range(0, KB, 2):
                act.dma_start(XS[:, b:b + 2, :], xT[P * b:P * (b + 2), :].rearrange("(b p) t -> p b t", p=P))\
                    .then_inc(S(f"x_in{b // 2}"), 16)
            act.dma_start(WQKV[:, :, :, :].rearrange("p a h c -> p (a h c)"), wqkv).then_inc(S("wqkv_loaded"), 16)
            act.wait_ge(S("par_loaded"), 16)
            for b in range(KB):
                act.wait_ge(S(f"x_in{b // 2}"), 16)
                norm_square(act, NRM1, b)
            norm_root(act, NRM1)
            norm_hi(act, NRM1)
            q0 = WH["x_m"][1]
            for b in range(4):
                q = q0 + b // 2
                act.wait_ge(quad_ready, q + 1)
                nc.scalar.activation(XM[:, b, 3:3 + T], half(q, b % 2), ACT.Copy).then_inc(free(q), 1)
            q0 = WH["o_m"][1]
            for s in range(2):
                q = q0 + s
                act.wait_ge(quad_ready, q + 1)
                for ob in range(2):
                    dst = OSTG[:, s, 4 * ob:4 * ob + 4, :].rearrange("p t c -> p (t c)")
                    nc.scalar.activation(dst, half(q, ob), ACT.Sigmoid).then_inc(free(q), 1)
            for s in range(2):
                act.wait_ge(free(q0 + s), freed(q0 + s, 1))
                act.dma_start(o_scr.rearrange("t p c -> p t c")[:, :, 256 * s:256 * (s + 1)], OSTG[:, s])\
                    .then_inc(S("o_stored"), 16)
            for n in range(12):
                act.wait_ge(S("qkv_ready"), n + 1)
                if n == 4:
                    act.wait_ge(S("o_stored"), 32)
                if n in (2, 3):
                    act.wait_ge(S("gate_sum"), n - 1)
                if n == 8:
                    act.wait_ge(S("gate_sum"), 4)
                dst = KT[:, n % 2, :] if n < 4 else (QT if n < 8 else KT)[:, n % 4, :]
                nc.scalar.activation(dst, ps[:, work(n):work(n) + 2 * BANK], ACT.Copy).then_inc(S("qkv_kept"), 1)
                if n == 3:
                    act.wait_ge(S("ones_set"), 1)
                    for tt in range(NT):
                        act.wait_ge(S("vt_ready"), tt + 1)
                        c = BANK * (6 + tt % 2)
                        nc.scalar.activation(V1[:, tt, :, 0:P], ps[:, c:c + BANK].rearrange("p (h d) -> p h d", h=H1),
                                             ACT.Copy).then_inc(S("vt_kept"), 1)
                    for b in range(4):
                        act.wait_ge(S("conv_done"), 4 * (b + 1))
                        nc.scalar.activation(XCV[:, b, :], XCV[:, b, :], ACT.Silu).then_inc(S("silu_done"), 1)
            for b in range(4):
                nc.scalar.activation(XCV[:, b, :], XCV[:, b, :], ACT.Copy, scale=par("skip_m", b)).then_inc(S("skip_done"), 1)
            act.wait_ge(S("rows_v"), 1)
            bf = par("b_if", rows=slice(32, 36))
            nc.scalar.activation(R1[:, :], ps[32:36, 0:T], ACT.Abs, bias=bf).then_inc(S("rows_a"), 1)
            act.wait_ge(S("rows_a"), 1)
            nc.scalar.activation(R1[:, :], R1[:, :], ACT.Exp, scale=-1.0).then_inc(S("rows_a"), 1)
            act.wait_ge(S("rows_a"), 2)
            nc.scalar.activation(R1[:, :], R1[:, :], ACT.Ln, bias=1.0).then_inc(S("rows_a"), 1)
            for n, (row, scale, need) in enumerate(((R4, 1.0, 10), (R2, -1.0, 11), (R0, 1.0, 12))):
                act.wait_ge(S("rows_v"), need)
                nc.scalar.activation(row[:, :], row[:, :], ACT.Exp, scale=scale).then_inc(S("rows_a"), 1)
            act.wait_ge(S("cols_ready"), 1)
            act.dma_start(OSC[:, 0, :], o_scr[0]).then_inc(S("o_back0"), 16)
            for c in range(NT):
                act.wait_ge(S("e_done"), c + 1)
                nc.scalar.activation(EW[:, :, :], EW[:, :, :], ACT.Exp).then_inc(S("w_exp"), 1)
                if c + 1 < NT:
                    act.dma_start(OSC[:, (c + 1) % 2, :], o_scr[c + 1]).then_inc(S(f"o_back{(c + 1) % 2}"), 16)
            act.wait_ge(S("mv_done"), NT)
            nc.scalar.activation(SD[:, :], MV[:, :, 1], ACT.Sqrt, bias=EPSC).then_inc(S("sd_done"), 1)

            act.wait_ge(S("ht_ready"), 2 * H1)
            for name, dst in (("q_d", QT), ("k_d", KD)):
                q0 = WH[name][1]
                for b in range(4):
                    q = q0 + b // 2
                    act.wait_ge(quad_ready, q + 1)
                    nc.scalar.activation(dst[:, b, :], half(q, b % 2), ACT.Copy).then_inc(free(q), 1)
            q0 = WH["v_d"][1]
            for s in range(2):
                act.wait_ge(quad_ready, q0 + s + 1)
                for ob in range(2):
                    nc.scalar.activation(VD[:, 4 * ob:4 * ob + 4, 256 * s:256 * (s + 1)],
                                         half(q0 + s, ob).rearrange("p (t c) -> p t c", t=4), ACT.Copy).then_inc(free(q0 + s), 1)
            act.wait_ge(S("lam_v"), 2)
            nc.scalar.activation(LM[:, 0:2], LM[:, 0:2], ACT.Exp).then_inc(S("lam_a"), 1)
            n_steps = len(STEPS)
            for i in range(n_steps + 3):
                if i < n_steps:
                    n = P * (STEPS[i][1] + 1)
                    for m, buf in enumerate((P0[i % 2], P1[i % 2])):
                        act.wait_ge(S("d_nm"), 2 * i + m + 1)
                        nc.scalar.activation(buf[:, 0:n], ps[:, 2 * BANK * m:2 * BANK * m + n], ACT.Exp,
                                             bias=SM[:, i % 4, 2 + m:3 + m], scale=SCD,
                                             accum_out=SM[:, i % 4, 4 + m:5 + m]).then_inc(S("d_exp"), 1)
                if 1 <= i <= n_steps:
                    s, (h, j) = i - 1, STEPS[i - 1]
                    n = P * (j + 1)
                    act.wait_ge(S("d_pt"), s + 1)
                    wait(act, S("d_o"), s - 1)
                    nc.scalar.activation(PTD[s % 2][:, 0:n], ps[:, 4 * BANK:4 * BANK + n], ACT.Copy).then_inc(S("d_ptk"), 1)
                if i >= 3:
                    s, (h, j) = i - 3, STEPS[i - 3]
                    act.wait_ge(S("d_on"), s + 1)
                    wait(act, S("d_sq"), s - 1)
                    nc.scalar.activation(OSQ[:, s % 2, :], QT[:, h, P * j:P * (j + 1)], ACT.Square,
                                         accum_out=OS1[:, 0, s:s + 1]).then_inc(S("d_sq"), 1)
            act.dma_start(MS[:, :, :], memT.rearrange("(b p) t -> p b t", p=P)).then_inc(S("mem_in"), 16)
            act.wait_ge(S("d_sq"), n_steps)
            nc.scalar.activation(OS1[:, 1, :], OS1[:, 0, :], ACT.Sqrt, bias=EPSC, scale=1.0 / P).then_inc(S("d_sd"), 1)
            for g in range(2 * H1):
                act.wait_ge(S("d_ot"), g + 1)
                c = BANK * (6 + g % 2)
                nc.scalar.activation(PR[:, 4 + g // 2, HALF * (g % 2):HALF * (g % 2 + 1)], ps[:, c:c + BANK], ACT.Copy,
                                     scale=GD[:, g // 2:g // 2 + 1]).then_inc(S("d_od"), 1)
            act.wait_ge(S("mem_in"), 16)
            for b in range(KB):
                norm_square(act, NRMM, b)
            norm_root(act, NRMM)
            norm_hi(act, NRMM)
            q0 = WH["mem_k"][1]
            for b in range(4):
                q = q0 + b // 2
                act.wait_ge(quad_ready, q + 1)
                nc.scalar.activation(KM[:, b, :], half(q, b % 2)[:, 0:MEM], ACT.Copy).then_inc(free(q), 1)
            q0 = WH["mem_v"][1]
            for s in range(2):
                act.wait_ge(quad_ready, q0 + s + 1)
                nc.scalar.activation(VM[:, :, 256 * s:256 * (s + 1)],
                                     half(q0 + s, 0)[:, 0:512].rearrange("p (t c) -> p t c", t=2), ACT.Copy).then_inc(free(q0 + s), 2)
            q0 = WH["q_c"][1]
            for b in range(4):
                q = q0 + b // 2
                act.wait_ge(quad_ready, q + 1)
                nc.scalar.activation(QC[:, b, :], half(q, b % 2), ACT.Copy).then_inc(free(q), 1)
            for j in range(NT + 1):
                if j < NT:
                    act.wait_ge(S("c_nm"), j + 1)
                    for h in range(H1):
                        ins = nc.scalar.activation(PC[:, j % 2, MEM * h:MEM * (h + 1)], ps[:, MEM * h:MEM * (h + 1)],
                                                   ACT.Exp, bias=SMC[:, j % 2, 4 + h:5 + h], scale=SC1,
                                                   accum_out=SMC[:, j % 2, 8 + h:9 + h])
                    ins.then_inc(S("c_exp"), 1)
                if j >= 1:
                    act.wait_ge(S("c_pt"), j)
                    wait(act, S("c_o"), j - 1)
                    nc.scalar.activation(PTC[:, :], ps[:, 2 * BANK:4 * BANK], ACT.Copy).then_inc(S("c_ptk"), 1)
            q0 = WH["z_m"][1]
            for zb in range(13):
                if zb < 12:
                    q = q0 + zb // 2
                    act.wait_ge(quad_ready, q + 1)
                    wait(act, S("y_done"), zb)
                    nc.scalar.activation(SIL[:, :], half(q, zb % 2), ACT.Silu).then_inc(free(q), 1)
                if 1 <= zb <= 8:
                    act.wait_ge(S("y_done"), zb)
                    nc.scalar.activation(YH[:, zb - 1, :], PR[:, zb - 1, :], ACT.Copy).then_inc(S("y_hi"), 1)
            for b in range(0, KB, 2):
                act.dma_start(HX[:, b:b + 2, :], xT[P * b:P * (b + 2), :].rearrange("(b p) t -> p b t", p=P))\
                    .then_inc(S(f"x_again{b // 2}"), 16)
            for zb in range(8, 12):
                act.wait_ge(S("y_done"), zb + 1)
                nc.scalar.activation(YHC[:, zb - 8, :], PR[:, zb, :], ACT.Copy).then_inc(S("y_hi"), 1)
            for b in range(KB):
                q = WH["out_1"][1] + b // 2
                act.wait_ge(free(q), freed(q, b % 2))
                norm_square(act, NRMF, b)
            norm_root(act, NRMF)

        def dve_block1(dve):
            v = Line(dve, S("dve_line"))
            dve.wait_ge(S("par_loaded"), 16)
            for b in range(KB):
                norm_add(dve, NRM1, b)
            norm_apply(dve, NRM1)
            dve.wait_ge(quad_ready, WH["x_m"][1] + 1)
            v.step(nc.vector.memset(XM[:, :, 0:3], 0.0))
            nc.vector.memset(V1[:, :, :, P:P + 1], 1.0).then_inc(S("ones_set"), 1)
            for b in range(4):
                q = WH["x_m"][1] + b // 2
                dve.wait_ge(free(q), freed(q, b % 2))
                v.wait()
                nc.vector.tensor_scalar(XCV[:, b, :], XM[:, b, 0:T], par("conv_w", b), par("conv_b", b), ALU.mult, ALU.add)\
                    .then_inc(S("conv_done"), 1)
                for k in range(1, 4):
                    dve.wait_ge(S("conv_done"), 4 * b + k)
                    nc.vector.scalar_tensor_tensor(XCV[:, b, :], XM[:, b, k:k + T], par("conv_w", 4 * k + b), XCV[:, b, :],
                                                   ALU.mult, ALU.add).then_inc(S("conv_done"), 1)
            rows = Line(dve, S("rows_v"))
            dve.wait_ge(S("gate_sum"), 12)
            nc_v = nc.vector
            rows.step(nc_v.tensor_scalar(R0[:, :], ps[32:36, 0:T], par("b_if", rows=slice(32, 36)), 0.0, ALU.add, ALU.min))
            v.step(nc_v.memset(R4[:, :], 1.0))
            v.wait()
            v.step(nc_v.memset(R4[:, 0:T:P], 0.0))
            v.wait()
            dve.wait_ge(S("rows_a"), 3)
            rows.wait(1)
            rows.step(nc_v.tensor_tensor(R0[:, :], R0[:, :], R1[:, :], ALU.subtract))
            rows.wait()
            rows.step(nc_v.tensor_tensor_scan(R2[:, :], R4[:, :], R0[:, :], 0.0, ALU.mult, ALU.add))
            rows.wait()
            rows.step(nc_v.scalar_tensor_tensor(R3[:, :], ps[0:4, 0:T], par("b_if", rows=slice(0, 4)), R2[:, :],
                                                ALU.add, ALU.subtract))
            rows.step(nc_v.memset(R0[:, :], 0.0))
            rows.wait()
            rows.step(nc_v.tensor_copy(R0[:, P:T:P], R2[:, P - 1:T - P:P]))
            rows.wait()
            rows.step(nc_v.tensor_tensor_scan(R1[:, :], R0[:, :], R3[:, :], 0.0, ALU.add, ALU.max))
            rows.step(nc_v.memset(MPREV[:, 0:1], 0.0))
            rows.wait()
            rows.step(nc_v.tensor_tensor(MPREV[:, 1:NT], R2[:, P - 1:T - P:P], R1[:, P - 1:T - P:P], ALU.add))
            rows.wait()
            v3 = lambda r: r[:, :].rearrange("p (c l) -> p c l", c=NT)
            rows.step(nc_v.tensor_tensor(v3(R4), MPREV[:, :].unsqueeze(2).to_broadcast([4, NT, P]), v3(R1), ALU.subtract))
            rows.step(nc_v.tensor_tensor(R2[:, :], R2[:, :], R1[:, :], ALU.add))
            rows.step(nc_v.tensor_tensor(v3(R0), v3(R3), v3(R1)[:, :, P - 1:P].to_broadcast([4, NT, P]), ALU.subtract))
            rows.wait()
            rows.step(nc_v.tensor_scalar(R1[:, :], R1[:, :], -1.0, None, ALU.mult))
            dve.wait_ge(S("cols_ready"), 1)
            nc_v.tensor_copy(COL[:, :, :], ps[:, 2 * BANK:2 * BANK + 96].rearrange("p (c n) -> p c n", c=NT))\
                .then_inc(S("cols_kept"), 1)
            dve.wait_ge(S("cols_kept"), 1)
            dve.wait_ge(S("skip_done"), 4)
            for c in range(NT):
                dve.wait_ge(S("bc_ready"), c + 1)
                wait(dve, S("num_ready"), c)
                for h in range(H1):
                    ins = nc_v.scalar_tensor_tensor(EW[:, h, :], ps[:, BANK + P * h:BANK + P * (h + 1)], COL[:, c, h:h + 1],
                                                    par("mask_ts", 0, P), ALU.add, ALU.add)
                ins.then_inc(S("e_done"), 1)
                v.step(nc_v.tensor_tensor(QS[:, :, :], ps[:, 0:BANK].rearrange("p (h t) -> p h t", h=H1),
                                          QT[:, :, P * c:P * (c + 1)], ALU.mult))
                v.step(nc_v.tensor_copy(DEC[:, :], ps[:, P - 1:BANK:P]))
                dve.wait_ge(S("kt_ready"), c + 1)
                wait(dve, S("cu_ready"), c)
                for h in range(H1):
                    v.step(nc_v.tensor_scalar(KW[:, h, :], ps[:, 3 * BANK + P * h:3 * BANK + P * (h + 1)],
                                              COL[:, c, 4 + h:5 + h], SC1, ALU.mult, ALU.mult))
                dve.wait_ge(S("w_exp"), c + 1)
                dve.wait_ge(S("sc_ready"), c + 1)
                v.wait()
                nc_v.scalar_tensor_tensor(EW[:, :, :].rearrange("p h t -> p (h t)"), ps[:, 2 * BANK:3 * BANK], SC1,
                                          EW[:, :, :].rearrange("p h t -> p (h t)"), ALU.mult, ALU.mult).then_inc(S("pt_done"), 1)
                dve.wait_ge(S("cu_ready"), c + 1)
                for h in range(H1):
                    if c == 0:
                        ins = nc_v.tensor_copy(CS[:, h, :], cup(h))
                    else:
                        ins = nc_v.scalar_tensor_tensor(CS[:, h, :], CS[:, h, :], DEC[:, h:h + 1], cup(h), ALU.mult, ALU.add)
                    ins.then_inc(S("c_upd"), 1) if h < H1 - 1 else ins.then_inc(S("c_done"), 1)
                dn = ps[:, 4 * BANK:6 * BANK].rearrange("p (b x) -> p b x", b=2)[:, :, 0:2 * (P + 1)]\
                    .rearrange("p b (h w) -> p b h w", w=P + 1)[:, :, :, P]
                v.step(nc_v.tensor_scalar(DN[:, :].rearrange("p (b h) -> p b h", b=2), dn, -1.0, None, ALU.mult))
                v.wait()
                v.step(nc_v.tensor_tensor(DN[:, :].rearrange("p (b h) -> p b h", b=2), dn,
                                          DN[:, :].rearrange("p (b h) -> p b h", b=2), ALU.max))
                v.wait()
                v.step(nc_v.tensor_tensor(DN[:, :], DN[:, :], COL[:, c, 8:12], ALU.max))
                v.wait()
                v.step(nc_v.reciprocal(DN[:, :], DN[:, :]))
                v.wait()
                dve.wait_ge(S(f"o_back{c % 2}"), 16 * (c // 2 + 1))
                for h in range(H1):
                    ins = nc_v.scalar_tensor_tensor(QT[:, h, P * c:P * (c + 1)], num(h)[:, 0:P], DN[:, h:h + 1],
                                                    OSC[:, c % 2, P * h:P * (h + 1)], ALU.mult, ALU.mult)
                ins.then_inc(S("h_done"), 1)
                dve.wait_ge(S("h_done"), c + 1)
                for h in range(H1):
                    v.step(nc_v.bn_stats(ST[:, h, :], QT[:, h, P * c:P * (c + 1)]))
                v.wait()
                for h in range(H1):
                    ins = nc_v.bn_aggr(MV[:, NT * h + c, :], ST[:, h, :])
                ins.then_inc(S("mv_done"), 1)
            dve.wait_ge(S("sd_done"), 1)
            v.step(nc_v.reciprocal(SD[:, :], SD[:, :]))
            v.wait()
            for g in range(2 * H1 + 1):
                if g < 2 * H1:
                    for t in range(4 * g, 4 * g + 4):
                        x = QT[:, t // NT, P * (t % NT):P * (t % NT + 1)]
                        ins = nc_v.tensor_scalar(x, x, MV[:, t, 0:1], SD[:, t:t + 1], ALU.subtract, ALU.mult)
                    ins.then_inc(S("hn_done"), 1)
                if g >= 1:
                    h, a, c = (g - 1) // 2, HALF * ((g - 1) % 2), BANK * (6 + (g - 1) % 2)
                    dve.wait_ge(S("ht_ready"), g)
                    x = PR[:, h, a:a + HALF]
                    nc_v.scalar_tensor_tensor(x, ps[:, c:c + BANK], par("mnorm_g", h), x, ALU.mult, ALU.add)\
                        .then_inc(S("pre_done"), 1)

            for m in range(2):
                nc_v.tensor_tensor_reduce(LTMP[:, :], par("lam", 128 * m, 64), par("lam", 128 * m + 64, 64), 1.0, 0.0,
                                          ALU.mult, ALU.add, LM[:, m:m + 1]).then_inc(S("lam_v"), 1)
                dve.wait_ge(S("lam_v"), m + 1)
            v.step(nc_v.tensor_scalar(GD[:, :], par("dnorm_g", 0, 4), 1.0 - LAM_INIT, None, ALU.mult))
            dve.wait_ge(S("lam_a"), 1)
            v.step(nc_v.scalar_tensor_tensor(LM[:, 2:3], LM[:, 1:2], -LAM_INIT, LM[:, 0:1], ALU.add, ALU.subtract))
            v.wait()
            n_steps = len(STEPS)
            for i in range(n_steps + 2):
                if 1 <= i <= n_steps:
                    s, (h, j) = i - 1, STEPS[i - 1]
                    n = P * (j + 1)
                    dve.wait_ge(S("d_exp"), 2 * s + 2)
                    v.step(nc_v.reciprocal(SM[:, s % 4, 6:8], SM[:, s % 4, 4:6]))
                    v.step(nc_v.tensor_scalar(SM[:, s % 4, 0:1], SM[:, s % 4, 4:5], LM[:, 2:3], None, ALU.mult))
                    v.wait()
                    v.step(nc_v.tensor_scalar(SM[:, s % 4, 1:2], SM[:, s % 4, 0:1], SM[:, s % 4, 7:8], None, ALU.mult))
                    v.wait()
                    nc_v.scalar_tensor_tensor(P0[s % 2][:, 0:n], P1[s % 2][:, 0:n], SM[:, s % 4, 1:2], P0[s % 2][:, 0:n],
                                              ALU.mult, ALU.add).then_inc(S("d_p"), 1)
                if i < n_steps:
                    n = P * (STEPS[i][1] + 1)
                    for m in range(2):
                        dve.wait_ge(S("d_scores"), 2 * i + m + 1)
                        v.step(nc_v.tensor_reduce(SM[:, i % 4, m:m + 1], ps[:, 2 * BANK * m:2 * BANK * m + n], AX, ALU.max))
                        v.wait()
                        nc_v.tensor_scalar(SM[:, i % 4, 2 + m:3 + m], SM[:, i % 4, m:m + 1], -SCD, None, ALU.mult)\
                            .then_inc(S("d_nm"), 1)
                if i >= 2:
                    s, (h, j) = i - 2, STEPS[i - 2]
                    c = BANK * (6 + s % 2)
                    dve.wait_ge(S("d_o"), s + 1)
                    nc_v.tensor_scalar(QT[:, h, P * j:P * (j + 1)], ps[:, c:c + P], SM[:, s % 4, 6:7], None, ALU.mult)\
                        .then_inc(S("d_on"), 1)
            dve.wait_ge(S("d_sd"), 1)
            v.step(nc_v.reciprocal(OS1[:, 1, :], OS1[:, 1, :]))
            v.wait()
            for h in range(H1):
                o = QT[:, h, :].rearrange("p (j d) -> p j d", j=NT)
                nc_v.tensor_tensor(o, o, OS1[:, 1, NT * h:NT * (h + 1)].unsqueeze(2).to_broadcast([P, NT, P]), ALU.mult)\
                    .then_inc(S("d_norm"), 1)
            for b in range(KB):
                norm_add(dve, NRMM, b)
            norm_apply(dve, NRMM)
            for j in range(NT + 1):
                if j < NT:
                    dve.wait_ge(S("c_scores"), j + 1)
                    v.step(nc_v.tensor_reduce(SMC[:, j % 2, 0:4], ps[:, 0:H1 * MEM].rearrange("p (h m) -> p h m", h=H1), AX, ALU.max))
                    v.wait()
                    nc_v.tensor_scalar(SMC[:, j % 2, 4:8], SMC[:, j % 2, 0:4], -SC1, None, ALU.mult).then_inc(S("c_nm"), 1)
                if j >= 1:
                    s = j - 1
                    dve.wait_ge(S("c_exp"), s + 1)
                    v.step(nc_v.reciprocal(SMC[:, s % 2, 8:12], SMC[:, s % 2, 8:12]))
                    v.wait()
                    p = PC[:, s % 2, :].rearrange("p (h m) -> p h m", h=H1)
                    nc_v.tensor_tensor(p, p, SMC[:, s % 2, 8:12].unsqueeze(2).to_broadcast([P, H1, MEM]), ALU.mult)\
                        .then_inc(S("c_p"), 1)
                    dve.wait_ge(S("c_o"), s + 1)
                    nc_v.tensor_copy(QC[:, :, P * s:P * (s + 1)], ps[:, 4 * BANK:5 * BANK].rearrange("p (h q) -> p h q", h=H1))\
                        .then_inc(S("c_oc"), 1)
            q0 = WH["z_m"][1]
            for zb in range(13):
                if zb < 12:
                    q = q0 + zb // 2
                    dve.wait_ge(free(q), freed(q, zb % 2))
                    nc_v.tensor_tensor(PR[:, zb, :], PR[:, zb, :], SIL[:, :], ALU.mult).then_inc(S("y_done"), 1)
                if 1 <= zb <= 8:
                    dve.wait_ge(S("y_hi"), zb)
                    dve.wait_ge(S("y_done"), zb)
                    nc_v.tensor_tensor(YL[:, zb - 1, :], PR[:, zb - 1, :], YH[:, zb - 1, :].bitcast(F32), ALU.subtract)\
                        .then_inc(S("y_lo"), 1)
            for zb in range(8, 12):
                dve.wait_ge(S("y_hi"), zb + 1)
                nc_v.tensor_tensor(YL[:, zb, :], PR[:, zb, :], YHC[:, zb - 8, :].bitcast(F32), ALU.subtract)\
                    .then_inc(S("y_lo"), 1)
            for b in range(KB):
                q = WH["out_1"][1] + b // 2
                dve.wait_ge(quad_ready, q + 1)
                dve.wait_ge(S(f"x_again{b // 2}"), 16)
                nc_v.tensor_tensor(HX[:, b, :], HX[:, b, :], half(q, b % 2), ALU.add).then_inc(free(q), 1)
                if b >= 1:
                    norm_add(dve, NRMF, b - 1)
            norm_add(dve, NRMF, KB - 1)
            norm_apply(dve, NRMF, NRM2 if 2 in blocks else None)

        HH = at("hidden_hi", A + 49152, [P, 4, T], F32R)
        HL = at("hidden_lo", A + 65536, [P, 4, T], F32R)
        FA = at("ff_act", A + 32768, [P, 2, T])
        FT = at("ff_tmp", A + 40960, [P, 2, T])
        hhi = lambda k, a, w: HH[:, k, a:a + w]
        hlo = lambda k, a, w: HL[:, k, a:a + w]

        def pe_group(pe, k, n, up_where, down_where, blocks_before, loop, ready):
            sl = loop and (loop[0], loop[1])
            ql = loop and (loop[0], loop[2])
            outs = 2 * n if k == "f2" else n
            feature_tiles(pe, up_where, outs, range(KB), xhi, xlo, ready=ready, sloop=sl, qloop=ql,
                          o_per_quad=outs // n)
            bl = loop and (loop[0], n)
            feature_tiles(pe, down_where, 8, range(n), hhi, hlo, sloop=sl, qloop=ql,
                          ready=lambda m: (S(k + "_lo"), up(blocks_before + m + 1, bl)))

        def made(eng, k, j, up_quad, blocks_before, loop):
            if k == "f2":
                eng.wait_ge(free(up_quad + j), freed(up_quad + j, 1, loop and (loop[0], loop[2])))
            else:
                eng.wait_ge(S("f3_x"), up(blocks_before + j + 1, loop and (loop[0], 4)))

        def act_group(act, k, n, up_quad, blocks_before, loop):
            ql, bl = loop and (loop[0], loop[2]), loop and (loop[0], n)
            for j in range(n + 1):
                if j < n:
                    q = up_quad + j
                    act.wait_ge(quad_ready, up(q + 1, ql))
                    if j >= 2:
                        made(act, k, j - 2, up_quad, blocks_before, loop)
                    nc.scalar.activation(FA[:, j % 2, :], half(q, 0), ACT.Silu if k == "f2" else ACT.Relu)\
                        .then_inc(free(q), 1 if k == "f2" else 2)
                if j >= 1:
                    made(act, k, j - 1, up_quad, blocks_before, loop)
                    nc.scalar.activation(HH[:, j - 1, :], FT[:, (j - 1) % 2, :], ACT.Copy).then_inc(S(k + "_hi"), 1)

        def dve_group(dve, k, n, up_quad, down_quad, blocks_before, loop, stream_tile, N=None):
            ql, bl = loop and (loop[0], loop[2]), loop and (loop[0], n)
            for j in range(n + 1):
                if j < n:
                    if j >= 2:
                        dve.wait_ge(S(k + "_lo"), up(blocks_before + j - 1, bl))
                    if k == "f2":
                        q = up_quad + j
                        dve.wait_ge(free(q), freed(q, 0, ql))
                        nc.vector.tensor_tensor(FT[:, j % 2, :], FA[:, j % 2, :], half(q, 1), ALU.mult).then_inc(free(q), 1)
                    else:
                        q = up_quad + j
                        dve.wait_ge(free(q), freed(q, 1, ql))
                        nc.vector.tensor_tensor(FT[:, j % 2, :], FA[:, j % 2, :], FA[:, j % 2, :], ALU.mult)\
                            .then_inc(S(k + "_x"), 1)
                if j >= 1:
                    made(dve, k, j - 1, up_quad, blocks_before, loop)
                    dve.wait_ge(S(k + "_hi"), up(blocks_before + j, bl))
                    nc.vector.tensor_tensor(HL[:, j - 1, :], FT[:, (j - 1) % 2, :], HH[:, j - 1, :].bitcast(F32), ALU.subtract)\
                        .then_inc(S(k + "_lo"), 1)
            for b in range(KB):
                q = down_quad + b // 2
                dve.wait_ge(quad_ready, up(q + 1, ql))
                nc.vector.tensor_tensor(stream_tile[:, b, :], stream_tile[:, b, :], half(q, b % 2), ALU.add).then_inc(free(q), 1)
                if N and b >= 1:
                    norm_add(dve, N, b - 1)
            if N:
                norm_add(dve, N, KB - 1)

        def layer(k):
            b, ff = (2, FF2) if k == "f2" else (3, FF3)
            slots, quads = (6, 8) if k == "f2" else (4, 8)
            return lambda g: (WH[f"up_{b}_{g}"], WH[f"down_{b}_{g}"]), ff // 4, ff % 4, slots, quads

        def pe_groups(pe, k, ready):
            at_group, full, rest, slots, quads = layer(k)
            pe_group(pe, k, 4, *at_group(0), 0, None, ready)
            with pe.Fori(1, full) as i:
                pe_group(pe, k, 4, *at_group(0), 0, (i, slots, quads), None)
            if rest:
                pe_group(pe, k, rest, *at_group(full), 4 * full, None, None)

        def act_groups(act, k):
            at_group, full, rest, slots, quads = layer(k)
            act_group(act, k, 4, at_group(0)[0][1], 0, None)
            with act.Fori(1, full) as i:
                act_group(act, k, 4, at_group(0)[0][1], 0, (i, slots, quads))
            if rest:
                act_group(act, k, rest, at_group(full)[0][1], 4 * full, None)

        def dve_groups(dve, k, stream_tile, N):
            at_group, full, rest, slots, quads = layer(k)
            up_q, down_q = at_group(0)[0][1], at_group(0)[1][1]
            last = full if rest else full - 1
            dve_group(dve, k, 4, up_q, down_q, 0, None, stream_tile)
            with dve.Fori(1, last) as i:
                dve_group(dve, k, 4, up_q, down_q, 0, (i, slots, quads), stream_tile)
            dve_group(dve, k, rest or 4, at_group(last)[0][1], at_group(last)[1][1], 4 * last, None, stream_tile, N)

        if 2 in blocks:
            NRM2 = norm_set("n2", lambda b: H[:, b, :], T, lambda b: par("norm_mix_2", b), A + 32768, WH["q_2"][1],
                            hi=lambda b: XHI[:, b, :], lo=lambda b: XLO[:, b, :])
            Q2 = at("q_2", A, [P, 4, T])
            K2 = at("k_2", A + 16384, [P, 4, T])
            V2 = at("v_2", A + 32768, [P, NT, HALF])
            BIAS = at("bias_2", A + 49152, [P, HEADS2, SPAN])
            P2 = at("p_2", A + 69632, [P, 3, SPAN])
            PT2 = at("p_t2", A + 77312, [P, 2, SPAN])
            AT = at("att", A, [P, 4, T])
            ATH = at("att_hi", A + 16384, [P, 4, T], F32R)
            ATL = at("att_lo", A + 32768, [P, 4, T], F32R)
            MX2 = small("max_2", [P, 3, 2])
            L2 = small("sum_2", [P, 3, 2])
            SG = at("gate_sig", A, [P, 4, T])
            MG = at("merged", A + 49152, [P, KB, T])
            VS = at("vs", A + 16384, [P, NT, HALF])
            U2 = at("u_gelu", A + 32768, [P, 4, T])
            SGW = at("sgu_w", A + 81920, [P, 1024])
            SGN = at("sgu_norm", A, [P, 1024])
            TS = at("sgu_tmp", A + 4096, [P, 2, T])
            SH = at("sgu_hi", A + 16384, [P, 4, T], F32R)
            SL = at("sgu_lo", A + 32768, [P, 4, T], F32R)
            TMG = at("merge_tmp", A + 81920, [P, T])
            ST2 = small("stats_2", [P, NT, 6])
            MV2 = small("mean_var_2", [P, NT, 2])
            H2 = at("h2", A, [P, KB, T])
            NRMG = norm_set("n2g", lambda b: H2[:, b, :], T, lambda b: par("norm_ffn_2", b), A + 32768, WH["up_2_0"][1],
                            hi=lambda b: XHI[:, b, :], lo=lambda b: XLO[:, b, :])
            NRMO = norm_set("n2o", lambda b: H2[:, b, :], T, lambda b: par("norm_final_2", b), A + 32768, 0,
                            out=lambda b: H2[:, b, :])
            ahi, alo = (lambda k, a, w: ATH[:, k, a:a + w]), (lambda k, a, w: ATL[:, k, a:a + w])
            shi, slo = (lambda k, a, w: SH[:, k, a:a + w]), (lambda k, a, w: SL[:, k, a:a + w])
            STEPS2 = [(j, h) for j in range(NT) for h in range(HEADS2)]
            FULL2 = FF2 // 4

        def span(j):
            n = min(P * (j + 1), SPAN)
            return P * (j + 1) - n, n, SPAN - n

        def pe_block2(pe):
            norm_sum(pe, NRM2)
            feature_tiles(pe, WH["q_2"], 4, range(KB), xhi, xlo, ready=lambda n: of(NRM2, "lo", n + 1))
            feature_tiles(pe, WH["k_2"], 4, range(KB), xhi, xlo)
            token_tiles(pe, WH["v_2"], 2, xhi, xlo)
            last = WH["v_2"][1] + 1
            quad_start(pe, last + 1)
            quad_start(pe, last + 2)
            n_steps = len(STEPS2)
            for i in range(n_steps + 3):
                if i < n_steps:
                    j, h = STEPS2[i]
                    k0, n, _ = span(j)
                    rows = slice(64 * (h % 2), 64 * (h % 2) + 64)
                    wait(pe, S("a_max"), i - 1)
                    for c in range(0, n, HALF):
                        w = min(HALF, n - c)
                        a = 2 * BANK * (i % 2) + c
                        mm = nc.tensor.matmul(ps[:, a:a + w], Q2[rows, h // 2, P * j:P * (j + 1)],
                                              K2[rows, h // 2, k0 + c:k0 + c + w], start=True, stop=True)
                    mm.then_inc(S("a_scores"), 1)
                if 2 <= i <= n_steps + 1:
                    s, (j, h) = i - 2, STEPS2[i - 2]
                    k0, n, _ = span(j)
                    pe.wait_ge(S("a_weights"), s + 1)
                    wait(pe, S("a_ptk"), s)
                    for k in range(n // P):
                        mm = nc.tensor.transpose(ps[:, 4 * BANK + P * k:4 * BANK + P * (k + 1)],
                                                 P2[:, s % 3, P * k:P * (k + 1)], IDENT)
                    mm.then_inc(S("a_pt"), 1)
                if 3 <= i <= n_steps + 2:
                    s, (j, h) = i - 3, STEPS2[i - 3]
                    k0, n, _ = span(j)
                    pe.wait_ge(S("a_ptk"), s + 1)
                    wait(pe, S("a_att"), s - 1)
                    c = BANK * (6 + s % 2)
                    for k in range(n // P):
                        mm = nc.tensor.matmul(ps[:, c:c + P], V2[:, k0 // P + k, P * (h // 2):P * (h // 2 + 1)],
                                              PT2[:, s % 2, P * k:P * (k + 1)], start=(k == 0), stop=(k == n // P - 1))
                    mm.then_inc(S("a_o"), 1)
            pe.wait_ge(S("a_att"), n_steps)
            pe.wait_ge(S("a_max"), n_steps)
            for pair in range(2):
                feature_tiles(pe, WH[f"gate_0{pair}"], 4, range(KB), xhi, xlo)
                feature_tiles(pe, WH[f"branch_0{pair}"], 4, range(4), ahi, alo,
                              ready=(lambda n: (S("att_lo"), n + 1)) if pair == 0 else None)
            token_tiles(pe, WH["vs_2"], 2, xhi, xlo)
            feature_tiles(pe, WH["u_2"], 4, range(KB), xhi, xlo)
            last = WH["u_2"][1] + 1
            quad_start(pe, last + 1)
            quad_start(pe, last + 2)
            pe.wait_ge(S("vn"), 3 * NT)
            for g in range(4):
                for tt in range(NT):
                    c = 2 * BANK * g + P * tt
                    mm = nc.tensor.matmul(ps[:, c:c + P], VS[:, tt, P * g:P * (g + 1)], SGW[:, P * g:P * (g + 1)],
                                          start=True, stop=True)
                mm.then_inc(S("mixed"), 1)
            pe.wait_ge(S("sgu_v"), 8)
            for pair in range(2):
                feature_tiles(pe, WH[f"gate_1{pair}"], 4, range(KB), xhi, xlo)
                feature_tiles(pe, WH[f"branch_1{pair}"], 4, range(4), shi, slo,
                              ready=(lambda n: (S("sgu_lo_done"), n + 1)) if pair == 0 else None)
            feature_tiles(pe, WH["out_2"], 8, range(KB), xhi, xlo, ready=lambda n: (S("mg_lo"), n + 1))
            norm_sum(pe, NRMG)
            ready = lambda n: of(NRMG, "lo", n + 1)
            pe_groups(pe, "f2", ready)
            norm_sum(pe, NRMO)

        def act_block2(act):
            if 1 not in blocks:
                for b in range(KB):
                    act.dma_start(H[:, b, :], xT[P * b:P * (b + 1), :]).then_inc(S("h_in"), 16)
                act.wait_ge(S("h_in"), 16 * KB)
                act.wait_ge(S("par_loaded"), 16)
            for b in range(KB):
                if 1 in blocks:
                    act.wait_ge(*of(NRMF, "x", b + 1))
                norm_square(act, NRM2, b)
            act.dma_start(h_scr.rearrange("(b p) t -> p b t", p=P), H[:, :, :]).then_inc(S("h_spilled"), 16)
            act.dma_start(BIAS[:, :, :], bias2.rearrange("p (h k) -> p h k", h=HEADS2)).then_inc(S("bias_loaded"), 16)
            norm_root(act, NRM2)
            norm_hi(act, NRM2)
            act.wait_ge(S("h_spilled"), 16)
            for name, dst, scale in (("q_2", Q2, 64.0 ** -0.5), ("k_2", K2, 1.0)):
                q0 = WH[name][1]
                for b in range(4):
                    q = q0 + b // 2
                    act.wait_ge(quad_ready, q + 1)
                    nc.scalar.activation(dst[:, b, :], half(q, b % 2), ACT.Copy, scale=scale).then_inc(free(q), 1)
            q0 = WH["v_2"][1]
            for s in range(2):
                act.wait_ge(quad_ready, q0 + s + 1)
                for ob in range(2):
                    nc.scalar.activation(V2[:, 4 * ob:4 * ob + 4, 256 * s:256 * (s + 1)],
                                         half(q0 + s, ob).rearrange("p (t c) -> p t c", t=4), ACT.Copy).then_inc(free(q0 + s), 1)
            n_steps = len(STEPS2)
            for i in range(n_steps + 3):
                if 2 <= i <= n_steps + 1:
                    s, (j, h) = i - 2, STEPS2[i - 2]
                    _, n, _ = span(j)
                    act.wait_ge(S("a_pt"), s + 1)
                    wait(act, S("a_o"), s - 1)
                    nc.scalar.activation(PT2[:, s % 2, 0:n], ps[:, 4 * BANK:4 * BANK + n], ACT.Copy).then_inc(S("a_ptk"), 1)
                if i < n_steps:
                    j, h = STEPS2[i]
                    _, n, _ = span(j)
                    act.wait_ge(S("a_nm"), i + 1)
                    nc.scalar.activation(P2[:, i % 3, 0:n], P2[:, i % 3, 0:n], ACT.Exp, bias=MX2[:, i % 3, 1:2],
                                         accum_out=L2[:, i % 3, 0:1]).then_inc(S("a_exp"), 1)
            act.wait_ge(S("a_att"), n_steps)
            for b in range(4):
                nc.scalar.activation(ATH[:, b, :], AT[:, b, :], ACT.Copy).then_inc(S("att_hi_done"), 1)

            def gates(branch, pair):
                q0 = WH[f"gate_{branch}{pair}"][1]
                for b in range(4):
                    q = q0 + b // 2
                    act.wait_ge(quad_ready, q + 1)
                    if pair:
                        before = WH[f"branch_{branch}0"][1] + b // 2
                        act.wait_ge(free(before), freed(before, b % 2))
                    nc.scalar.activation(SG[:, b, :], half(q, b % 2), ACT.Sigmoid,
                                         bias=par("b_gate_2", 8 * branch + 4 * pair + b)).then_inc(free(q), 1)

            act.wait_ge(S("att_lo"), 4)
            gates(0, 0)
            gates(0, 1)
            q0 = WH["vs_2"][1]
            for q in range(WH["branch_01"][1], WH["branch_01"][1] + 2):
                act.wait_ge(free(q), freed(q, 1))
            act.dma_start(SGW[:, :], sgu[:, 0:1024]).then_inc(S("sgu_loaded"), 16)
            act.dma_start(SGN[:, :], sgu[:, 1024:2048]).then_inc(S("sgu_loaded"), 16)
            for s in range(2):
                act.wait_ge(quad_ready, q0 + s + 1)
                for ob in range(2):
                    nc.scalar.activation(VS[:, 4 * ob:4 * ob + 4, 256 * s:256 * (s + 1)],
                                         half(q0 + s, ob).rearrange("p (t c) -> p t c", t=4), ACT.Gelu_apprx_tanh)\
                        .then_inc(free(q0 + s), 1)
            q0 = WH["u_2"][1]
            for b in range(4):
                q = q0 + b // 2
                act.wait_ge(quad_ready, q + 1)
                nc.scalar.activation(U2[:, b, :], half(q, b % 2), ACT.Gelu_apprx_tanh).then_inc(free(q), 1)
            act.wait_ge(S("vs_mv"), NT)
            nc.scalar.activation(MV2[:, :, 1], MV2[:, :, 1], ACT.Sqrt, bias=EPSC).then_inc(S("vs_sd"), 1)
            for g in range(4):
                act.wait_ge(S("sgu_v"), 2 * g + 2)
                if g == 0:
                    act.wait_ge(S("mixed"), 4)
                nc.scalar.activation(SH[:, g, :], U2[:, g, :], ACT.Copy).then_inc(S("sgu_hi_done"), 1)
            gates(1, 0)
            gates(1, 1)
            for q in range(WH["branch_11"][1], WH["branch_11"][1] + 2):
                act.wait_ge(free(q), freed(q, 1))
            act.dma_start(H2[:, :, :], h_scr.rearrange("(b p) t -> p b t", p=P)).then_inc(S("h2_loaded"), 16)
            for b in range(KB):
                act.wait_ge(S("merged"), b + 1)
                nc.scalar.activation(XHI[:, b, :], MG[:, b, :], ACT.Copy).then_inc(S("mg_hi"), 1)
            for b in range(KB):
                q = WH["out_2"][1] + b // 2
                act.wait_ge(free(q), freed(q, b % 2))
                norm_square(act, NRMG, b)
            norm_root(act, NRMG)
            norm_hi(act, NRMG)
            act.wait_ge(*of(NRMG, "lo", KB))
            act_groups(act, "f2")
            q0 = WH[f"down_2_{(FF2 - 1) // 4}"][1]
            for b in range(KB):
                q = q0 + b // 2
                act.wait_ge(free(q), freed(q, b % 2))
                norm_square(act, NRMO, b)
            norm_root(act, NRMO)

        def dve_block2(dve):
            v = Line(dve, S("dve_line2"))
            dve.wait_ge(S("par_loaded"), 16)
            if 1 not in blocks:
                for b in range(KB):
                    norm_add(dve, NRM2, b)
            norm_apply(dve, NRM2)
            dve.wait_ge(S("bias_loaded"), 16)
            n_steps = len(STEPS2)
            for i in range(n_steps + 4):
                if i < n_steps:
                    j, h = STEPS2[i]
                    _, n, c = span(j)
                    dve.wait_ge(S("a_scores"), i + 1)
                    wait(dve, S("a_pt"), i - 2)
                    a = 2 * BANK * (i % 2)
                    nc.vector.tensor_tensor_reduce(P2[:, i % 3, 0:n], ps[:, a:a + n], BIAS[:, h, c:SPAN], 1.0, 4 * NEG,
                                                   ALU.add, ALU.max, MX2[:, i % 3, 0:1]).then_inc(S("a_max"), 1)
                    dve.wait_ge(S("a_max"), i + 1)
                    nc.vector.tensor_scalar(MX2[:, i % 3, 1:2], MX2[:, i % 3, 0:1], -1.0, None, ALU.mult).then_inc(S("a_nm"), 1)
                if 1 <= i <= n_steps:
                    s = i - 1
                    _, n, _ = span(STEPS2[s][0])
                    dve.wait_ge(S("a_exp"), s + 1)
                    v.step(nc.vector.reciprocal(L2[:, s % 3, 1:2], L2[:, s % 3, 0:1]))
                    v.wait()
                    nc.vector.tensor_scalar(P2[:, s % 3, 0:n], P2[:, s % 3, 0:n], L2[:, s % 3, 1:2], None, ALU.mult)\
                        .then_inc(S("a_weights"), 1)
                if i >= 4:
                    s, (j, h) = i - 4, STEPS2[i - 4]
                    rows, c = slice(64 * (h % 2), 64 * (h % 2) + 64), BANK * (6 + s % 2)
                    dve.wait_ge(S("a_o"), s + 1)
                    nc.vector.tensor_copy(AT[rows, h // 2, P * j:P * (j + 1)], ps[rows, c:c + P]).then_inc(S("a_att"), 1)
            for b in range(4):
                dve.wait_ge(S("att_hi_done"), b + 1)
                ins = nc.vector.tensor_tensor(ATL[:, b, :], AT[:, b, :], ATH[:, b, :].bitcast(F32), ALU.subtract)
                ins.then_inc(S("att_lo"), 1)

            def merge(branch, pair):
                for b in range(4):
                    q, o = WH[f"branch_{branch}{pair}"][1] + b // 2, 4 * pair + b
                    gate = WH[f"gate_{branch}{pair}"][1] + b // 2
                    dve.wait_ge(quad_ready, q + 1)
                    dve.wait_ge(free(gate), freed(gate, b % 2))
                    if branch == 0:
                        nc.vector.tensor_tensor(MG[:, o, :], SG[:, b, :], half(q, b % 2), ALU.mult).then_inc(free(q), 1)
                    else:
                        wait(dve, S("merged"), o)
                        nc.vector.tensor_tensor(TMG[:, :], SG[:, b, :], half(q, b % 2), ALU.mult).then_inc(free(q), 1)
                        dve.wait_ge(free(q), freed(q, b % 2))
                        nc.vector.tensor_tensor(MG[:, o, :], MG[:, o, :], TMG[:, :], ALU.add).then_inc(S("merged"), 1)

            merge(0, 0)
            merge(0, 1)
            dve.wait_ge(S("sgu_loaded"), 32)
            q0 = WH["vs_2"][1]
            for s in range(2):
                dve.wait_ge(free(q0 + s), freed(q0 + s, 1))
            for tt in range(NT):
                v.step(nc.vector.bn_stats(ST2[:, tt, :], VS[:, tt, :]))
            v.wait()
            for tt in range(NT):
                nc.vector.bn_aggr(MV2[:, tt, :], ST2[:, tt, :]).then_inc(S("vs_mv"), 1)
            dve.wait_ge(S("vs_sd"), 1)
            v.step(nc.vector.reciprocal(MV2[:, :, 1], MV2[:, :, 1]))
            v.wait()
            for tt in range(NT):
                x = VS[:, tt, :]
                nc.vector.tensor_scalar(x, x, MV2[:, tt, 0:1], MV2[:, tt, 1:2], ALU.subtract, ALU.mult).then_inc(S("vn"), 1)
                dve.wait_ge(S("vn"), 3 * tt + 1)
                nc.vector.tensor_tensor(x, x, SGN[:, 0:HALF], ALU.mult).then_inc(S("vn"), 1)
                dve.wait_ge(S("vn"), 3 * tt + 2)
                nc.vector.tensor_tensor(x, x, SGN[:, HALF:2 * HALF], ALU.add).then_inc(S("vn"), 1)
            uq = WH["u_2"][1]
            for g in range(4):
                dve.wait_ge(S("mixed"), g + 1)
                dve.wait_ge(free(uq + g // 2), freed(uq + g // 2, g % 2))
                wait(dve, S("sgu_v"), 2 * g)
                mixed = ps[:, 2 * BANK * g:2 * BANK * (g + 1)].rearrange("p (t c) -> p t c", t=NT)
                bias = SGW[:, HALF + P * g:HALF + P * (g + 1)].unsqueeze(1).to_broadcast([P, NT, P])
                nc.vector.tensor_tensor(TS[:, g % 2, :].rearrange("p (t c) -> p t c", t=NT), mixed, bias, ALU.add)\
                    .then_inc(S("sgu_v"), 1)
                dve.wait_ge(S("sgu_v"), 2 * g + 1)
                nc.vector.tensor_tensor(U2[:, g, :], U2[:, g, :], TS[:, g % 2, :], ALU.mult).then_inc(S("sgu_v"), 1)
            for g in range(4):
                dve.wait_ge(S("sgu_hi_done"), g + 1)
                nc.vector.tensor_tensor(SL[:, g, :], U2[:, g, :], SH[:, g, :].bitcast(F32), ALU.subtract)\
                    .then_inc(S("sgu_lo_done"), 1)
            merge(1, 0)
            merge(1, 1)
            for b in range(KB):
                dve.wait_ge(S("mg_hi"), b + 1)
                nc.vector.tensor_tensor(XLO[:, b, :], MG[:, b, :], XHI[:, b, :].bitcast(F32), ALU.subtract).then_inc(S("mg_lo"), 1)
            dve.wait_ge(S("h2_loaded"), 16)
            for b in range(KB):
                q = WH["out_2"][1] + b // 2
                dve.wait_ge(quad_ready, q + 1)
                nc.vector.tensor_tensor(H2[:, b, :], H2[:, b, :], half(q, b % 2), ALU.add).then_inc(free(q), 1)
                if b >= 1:
                    norm_add(dve, NRMG, b - 1)
            norm_add(dve, NRMG, KB - 1)
            norm_apply(dve, NRMG)
            dve.wait_ge(*of(NRMG, "lo", KB))
            dve_groups(dve, "f2", H2, NRMO)
            norm_apply(dve, NRMO)

        if 3 in blocks:
            H2I = H2 if 2 in blocks else at("h2", A, [P, KB, T])
            MT = at("meta", A + 49152, [P, KB, META])
            XH3 = at("xhi3", X, [P, KB, LW], F32R)
            XL3 = at("xlo3", X + 33280, [P, KB, LW], F32R)
            NRM3M = norm_set("n3m", lambda b: MT[:, b, :], META, lambda b: par("norm_mix_g_3", b), A + 49664, WH["x_0"][1],
                             hi=lambda b: XH3[:, b, T:LW], lo=lambda b: XL3[:, b, T:LW])
            NRM3 = norm_set("n3", lambda b: H2I[:, b, :], T, lambda b: par("norm_mix_g_3", b), A + 32768, WH["x_0"][1],
                            hi=lambda b: XH3[:, b, 0:T], lo=lambda b: XL3[:, b, 0:T])
            x3hi, x3lo = (lambda k, a, w: XH3[:, k, a:a + w]), (lambda k, a, w: XL3[:, k, a:a + w])
            PADC = CCK - 1
            CC = at("c_in", A, [P, 4, PADC + LW])
            CCO = at("c_out", A + 17152, [P, 4, T])
            SGC = at("c_gate", A + 50240, [P, 2, LW])
            XL_ = at("x_lru", A + 33536, [P, 4, 3 + LW])
            YL3 = at("y_lru", A + 33536, [P, 4, T])
            GL = at("g_lru", A + 50240, [P, 4, T])
            TX = at("l_x", A + 66624, [P, LW])
            TI = at("l_i", A + 70784, [P, LW])
            TU = at("l_u", A + 74944, [P, LW])
            TR = at("l_r", A + 79104, [P, LW])
            LRUW = at("lru_w", A + 83264, [P, 2, 4, P])
            NC4 = small("lru_rate", [P, 2, 4])
            NCT = small("lru_rate_tmp", [P, 4])
            NRML = norm_set("nl", lambda b: YL3[:, b, :], T, lambda b: par("out_norm_lru_g_3", b), A + 66624, WH["out_3"][1], nb=4,
                            hi=lambda b: XHI[:, b, :], lo=lambda b: XLO[:, b, :])
            NRMV = norm_set("nv", lambda b: CCO[:, b, :], T, None, A, WH["out_3"][1], nb=4, bank=2)
            NRMC = norm_set("nc", lambda b: CCO[:, b, :], T, lambda b: par("out_norm_cc_g_3", b), A, WH["out_3"][1], nb=4,
                            hi=lambda b: XHI[:, 4 + b, :], lo=lambda b: XLO[:, 4 + b, :])
            H3 = at("h3", A, [P, KB, T])
            NRMP = norm_set("n3p", lambda b: H3[:, b, :], T, lambda b: par("norm_mlp_g_3", b), A + 32768, WH["up_3_0"][1],
                            hi=lambda b: XHI[:, b, :], lo=lambda b: XLO[:, b, :])
            NRME = norm_set("n3o", lambda b: H3[:, b, :], T, lambda b: par("norm_final_g_3", b), A + 32768, 0,
                            out=lambda b: H3[:, b, :])
            TRIOS = [(name[0] if name[0] != "v" else "vg"[n], int(name[-1]) + (n if name[0] != "v" else 0))
                     for name, _ in PAIRS3 for n in range(2)]
            QUAD3 = {("l" if k == "g" and i >= 12 else k, b): WH["x_0"][1] + i for i, (k, b) in enumerate(TRIOS)}
            CMEAN = QUAD * ((WH["out_3"][1] + 1) % 2) + 2 * BANK
            PIECES = [(g, a, w) for a, w in ((0, HALF), (HALF, HALF), (T, META)) for g in range(2)]

        def trio(q, a=0, w=T):
            c = 3 * BANK * (q % 2)
            return ps[:, c + a:c + a + w]

        def piece_cols(a, w):
            s = 0 if a == T else a + META
            return slice(s, s + w)

        def pe_pair(pe, name, ready=None):
            slot, quad = WH[name]
            r = slot % 2
            for o in range(2):
                q = quad + o
                if q >= 2:
                    pe.wait_ge(free(q), 2 * (q // 2))
                c0 = 3 * BANK * (q % 2)
                if o == 0:
                    slot_start(pe, slot, None)
                for k in range(KB):
                    if ready and o == 0:
                        pe.wait_ge(*ready(k))
                    w_hi, w_lo = WHI[:, r, KB * o + k, :], WLO[:, r, KB * o + k, :]
                    for m, (w, x) in enumerate(((w_hi, x3hi), (w_hi, x3lo), (w_lo, x3hi))):
                        for a, width in ((0, HALF), (HALF, HALF), (T, META)):
                            mm = nc.tensor.matmul(ps[:, c0 + a:c0 + a + width], w, x(k, a, width),
                                                  start=(k == 0 and m == 0), stop=(k == KB - 1 and m == 2))
                            if o == k == m == a == 0 and slot > 0:
                                mm.then_inc(slot_used, 1)
                mm.then_inc(quad_ready, 1)

        def pe_gates(pe, b):
            pe.wait_ge(S("l_conv"), 4 * (b + 1))
            for i, (g, a, w) in enumerate(PIECES):
                n = len(PIECES) * b + i
                wait(pe, S("l_gate"), n - 1)
                c = BANK * (6 + n % 2)
                nc.tensor.matmul(ps[:, c:c + w], LRUW[:, g, b, :], TX[:, piece_cols(a, w)], start=True, stop=True)\
                    .then_inc(S("l_piece"), 1)

        def pe_block3(pe):
            norm_sum(pe, NRM3M)
            norm_sum(pe, NRM3)
            pe.wait_ge(*of(NRM3M, "lo", KB))
            pe_pair(pe, "x_0", lambda n: of(NRM3, "lo", n + 1))
            pe.wait_ge(S("lru_w_loaded"), 16)
            pe_gates(pe, 0)
            pe_pair(pe, "vg_0")
            pe_pair(pe, "x_2")
            pe_gates(pe, 1)
            pe_pair(pe, "vg_1")
            pe_pair(pe, "vg_2")
            pe_gates(pe, 2)
            pe_pair(pe, "vg_3")
            pe_gates(pe, 3)
            pe_pair(pe, "g_0")
            pe_pair(pe, "g_2")
            last = QUAD3["l", 3]
            for q in (last - 1, last):
                pe.wait_ge(free(q), 2 * (q // 2) + 2)
            pe.wait_ge(S("cc_conv"), 4 * CCK)
            for c in range(0, T, HALF):
                for b in range(4):
                    mm = nc.tensor.matmul(ps[:, CMEAN + c:CMEAN + c + HALF], ONES, CCO[:, b, c:c + HALF],
                                          start=(b == 0), stop=(b == 3))
            mm.then_inc(S("cc_sum"), 1)
            norm_sum(pe, NRML)
            norm_sum(pe, NRMV)
            norm_sum(pe, NRMC)
            feature_tiles(pe, WH["out_3"], 8, range(KB), xhi, xlo,
                          ready=lambda n: of(NRML, "lo", n + 1) if n < 4 else of(NRMC, "lo", n - 3))
            norm_sum(pe, NRMP)
            pe_groups(pe, "f3", lambda n: of(NRMP, "lo", n + 1))
            norm_sum(pe, NRME)

        def act_block3(act):
            if 2 not in blocks:
                for b in range(KB):
                    act.dma_start(H2I[:, b, :], xT[P * b:P * (b + 1), :]).then_inc(S("h2_in"), 16)
                act.wait_ge(S("h2_in"), 16 * KB)
                act.wait_ge(S("par_loaded"), 16)
            else:
                act.wait_ge(*of(NRMO, "sum", 1))
            act.dma_start(MT[:, :, :], metaT.rearrange("(b p) t -> p b t", p=P)).then_inc(S("meta_loaded"), 16)
            act.dma_start(LRUW[:, :, :, :].rearrange("p g b c -> p (g b c)"), lru_w).then_inc(S("lru_w_loaded"), 16)
            act.wait_ge(S("meta_loaded"), 16)
            for b in range(KB):
                norm_square(act, NRM3M, b)
            norm_root(act, NRM3M)
            norm_hi(act, NRM3M)
            for b in range(KB):
                if 2 in blocks:
                    act.wait_ge(*of(NRMO, "x", b + 1))
                norm_square(act, NRM3, b)
            act.dma_start(h_scr.rearrange("(b p) t -> p b t", p=P), H2I[:, :, :]).then_inc(S("h2_spilled"), 16)
            norm_root(act, NRM3)
            norm_hi(act, NRM3)
            nc.scalar.activation(NCT[:, :], par("lru_a_param_3", 0, 4), ACT.Abs).then_inc(S("rate_a"), 1)
            act.wait_ge(S("rate_a"), 1)
            nc.scalar.activation(NCT[:, :], NCT[:, :], ACT.Exp, scale=-1.0).then_inc(S("rate_a"), 1)
            act.wait_ge(S("rate_a"), 2)
            nc.scalar.activation(NCT[:, :], NCT[:, :], ACT.Ln, bias=1.0).then_inc(S("rate_a"), 1)
            act.wait_ge(S("h2_spilled"), 16)

            def keep(kind, b, dst, pad, func):
                q = QUAD3[kind, b]
                act.wait_ge(quad_ready, q + 1)
                nc.scalar.activation(dst[:, pad + META:pad + LW], trio(q), func).then_inc(free(q), 1)
                nc.scalar.activation(dst[:, pad:pad + META], trio(q, T, META), func).then_inc(free(q), 1)

            def keep_x(b):
                keep("x", b, XL_[:, b, :], 3, ACT.Copy)

            def keep_vg(b):
                keep("v", b, CC[:, b, :], PADC, ACT.Copy)
                wait(act, S("c_gated"), b - 1)
                keep("g", b, SGC[:, b % 2, :], 0, ACT.Sigmoid)

            def recurrence(b):
                wait(act, S("l_scan"), b)
                for i, (g, a, w) in enumerate(PIECES):
                    n = len(PIECES) * b + i
                    act.wait_ge(S("l_piece"), n + 1)
                    c = BANK * (6 + n % 2)
                    dst, bias = (TU, par("lru_gate_a_b_3", b)) if g == 0 else (TI, par("lru_gate_x_b_3", b))
                    nc.scalar.activation(dst[:, piece_cols(a, w)], ps[:, c:c + w], ACT.Sigmoid, bias=bias).then_inc(S("l_gate"), 1)
                act.wait_ge(S("l_gate"), len(PIECES) * (b + 1))
                nc.scalar.activation(TR[:, :], TU[:, :], ACT.Exp, scale=NC4[:, 1, b:b + 1]).then_inc(S("l_a"), 1)
                act.wait_ge(S("l_a"), b + 1)
                nc.scalar.activation(TU[:, :], TU[:, :], ACT.Tanh, scale=NC4[:, 0, b:b + 1]).then_inc(S("l_u"), 1)
                act.wait_ge(S("l_ix"), b + 1)
                nc.scalar.activation(TX[:, :], TR[:, :], ACT.Square).then_inc(S("l_sq"), 1)
                act.wait_ge(S("l_t"), b + 1)
                nc.scalar.activation(TU[:, :], TU[:, :], ACT.Sqrt).then_inc(S("l_m"), 1)

            keep_x(0)
            keep_x(1)
            act.wait_ge(S("rate_v"), 3)
            recurrence(0)
            keep_vg(0)
            keep_x(2)
            keep_x(3)
            recurrence(1)
            keep_vg(1)
            keep_vg(2)
            recurrence(2)
            keep_vg(3)
            recurrence(3)
            act.wait_ge(S("c_gated"), 4)
            for b in range(4):
                q = QUAD3["l", b]
                act.wait_ge(quad_ready, q + 1)
                nc.scalar.activation(GL[:, b, :], trio(q), ACT.Gelu_apprx_tanh).then_inc(free(q), 2)
            for b in range(4):
                act.wait_ge(S("y_lru_done"), b + 1)
                norm_square(act, NRML, b)
            norm_root(act, NRML)
            for b in range(4):
                act.wait_ge(S("cc_mean"), b + 1)
                norm_square(act, NRMV, b)
            norm_hi(act, NRML)
            norm_root(act, NRMV)
            for b in range(4):
                act.wait_ge(S("cc_inv"), b + 1)
                nc.scalar.activation(CCO[:, b, :], CCO[:, b, :], ACT.Silu, bias=par("cc_ln_b_3", b),
                                     scale=par("cc_ln_g_3", b)).then_inc(S("cc_silu"), 1)
            for b in range(4):
                act.wait_ge(S("cc_silu"), b + 1)
                norm_square(act, NRMC, b)
            norm_root(act, NRMC)
            norm_hi(act, NRMC)
            act.wait_ge(*of(NRMC, "lo", 4))
            act.dma_start(H3[:, :, :], h_scr.rearrange("(b p) t -> p b t", p=P)).then_inc(S("h3_loaded"), 16)
            for b in range(KB):
                q = WH["out_3"][1] + b // 2
                act.wait_ge(free(q), freed(q, b % 2))
                norm_square(act, NRMP, b)
            norm_root(act, NRMP)
            norm_hi(act, NRMP)
            act.wait_ge(*of(NRMP, "lo", KB))
            act_groups(act, "f3")
            q0 = WH[f"down_3_{FF3 // 4 - 1}"][1]
            for b in range(KB):
                q = q0 + b // 2
                act.wait_ge(free(q), freed(q, b % 2))
                norm_square(act, NRME, b)
            norm_root(act, NRME)

        def dve_block3(dve):
            v = Line(dve, S("dve_line3"))
            dve.wait_ge(S("par_loaded"), 16)
            for b in range(KB):
                norm_add(dve, NRM3M, b)
            norm_apply(dve, NRM3M)
            for b in range(KB):
                norm_add(dve, NRM3, b)
            norm_apply(dve, NRM3)
            dve.wait_ge(S("h2_spilled"), 16)
            dve.wait_ge(*of(NRM3, "lo", KB))
            v.step(nc.vector.memset(CC[:, :, 0:PADC], 0.0))
            v.step(nc.vector.memset(XL_[:, :, 0:3], 0.0))
            v.wait()
            v.step(nc.vector.tensor_scalar(NC4[:, 0, :], par("lru_a_param_3", 0, 4), -1.0, 0.0, ALU.mult, ALU.max))
            v.wait()
            dve.wait_ge(S("rate_a"), 3)
            nc.vector.tensor_tensor(NC4[:, 1, :], NC4[:, 0, :], NCT[:, :], ALU.add).then_inc(S("rate_v"), 1)
            dve.wait_ge(S("rate_v"), 1)
            nc.vector.tensor_scalar(NC4[:, 0, :], NC4[:, 1, :], LRU_C, None, ALU.mult).then_inc(S("rate_v"), 1)
            dve.wait_ge(S("rate_v"), 2)
            nc.vector.tensor_scalar(NC4[:, 1, :], NC4[:, 1, :], -LRU_C, None, ALU.mult).then_inc(S("rate_v"), 1)

            def kept(kind, b):
                q = QUAD3[kind, b]
                dve.wait_ge(free(q), 2 * (q // 2) + 2)

            def short_convolution(b):
                kept("x", b)
                if b:
                    dve.wait_ge(S("y_kept"), b)
                nc.vector.tensor_scalar(TX[:, :], XL_[:, b, 0:LW], par("lru_conv_w_3", b), par("lru_conv_b_3", b),
                                        ALU.mult, ALU.add).then_inc(S("l_conv"), 1)
                for k in range(1, 4):
                    dve.wait_ge(S("l_conv"), 4 * b + k)
                    nc.vector.scalar_tensor_tensor(TX[:, :], XL_[:, b, k:k + LW], par("lru_conv_w_3", 4 * k + b), TX[:, :],
                                                   ALU.mult, ALU.add).then_inc(S("l_conv"), 1)

            def recurrence(b, step):
                if step == 0:
                    dve.wait_ge(S("l_gate"), len(PIECES) * (b + 1))
                    dve.wait_ge(S("l_conv"), 4 * b + 4)
                    nc.vector.tensor_tensor(TI[:, :], TI[:, :], TX[:, :], ALU.mult).then_inc(S("l_ix"), 1)
                elif step == 1:
                    dve.wait_ge(S("l_sq"), b + 1)
                    nc.vector.scalar_tensor_tensor(TU[:, :], TX[:, :], 1.0, TU[:, :], ALU.add, ALU.mult).then_inc(S("l_t"), 1)
                else:
                    dve.wait_ge(S("l_m"), b + 1)
                    dve.wait_ge(S("l_ix"), b + 1)
                    v.step(nc.vector.tensor_tensor(TI[:, :], TI[:, :], TU[:, :], ALU.mult))
                    v.wait()
                    nc.vector.tensor_tensor_scan(TX[:, :], TR[:, :], TI[:, :], 0.0, ALU.mult, ALU.add).then_inc(S("l_scan"), 1)
                    dve.wait_ge(S("l_scan"), b + 1)
                    nc.vector.tensor_copy(YL3[:, b, :], TX[:, META:LW]).then_inc(S("y_kept"), 1)

            def gate_input(b):
                kept("v", b)
                kept("g", b)
                c = CC[:, b, PADC:PADC + LW]
                nc.vector.tensor_tensor(c, c, SGC[:, b % 2, :], ALU.mult).then_inc(S("c_gated"), 1)

            def taps(b, first, end):
                dve.wait_ge(S("c_gated"), b + 1)
                for k in range(first, end):
                    x, w = CC[:, b, META + k:META + k + T], par("cc_conv_w_3", 4 * k + b)
                    if k == 0:
                        ins = nc.vector.tensor_scalar(CCO[:, b, :], x, w, par("cc_conv_b_3", b), ALU.mult, ALU.add)
                    else:
                        dve.wait_ge(S("cc_conv"), CCK * b + k)
                        ins = nc.vector.scalar_tensor_tensor(CCO[:, b, :], x, w, CCO[:, b, :], ALU.mult, ALU.add)
                    ins.then_inc(S("cc_conv"), 1)

            short_convolution(0)
            for step in range(3):
                recurrence(0, step)
            for b in range(3):
                gate_input(b)
                short_convolution(b + 1)
                for step in range(3):
                    taps(b, CCK * step // 3, CCK * (step + 1) // 3)
                    recurrence(b + 1, step)
            gate_input(3)
            taps(3, 0, CCK)
            dve.wait_ge(S("y_kept"), 4)
            for b in range(4):
                kept("l", b)
                nc.vector.tensor_tensor(YL3[:, b, :], YL3[:, b, :], GL[:, b, :], ALU.mult).then_inc(S("y_lru_done"), 1)
            for b in range(4):
                norm_add(dve, NRML, b)
            dve.wait_ge(S("cc_sum"), 1)
            for b in range(4):
                nc.vector.scalar_tensor_tensor(CCO[:, b, :], ps[:, CMEAN:CMEAN + T], -1.0 / (4 * P), CCO[:, b, :],
                                               ALU.mult, ALU.add).then_inc(S("cc_mean"), 1)
            for b in range(4):
                norm_add(dve, NRMV, b)
            norm_apply(dve, NRML)
            inv = norm_inv(dve, NRMV)
            for b in range(4):
                nc.vector.tensor_tensor(CCO[:, b, :], CCO[:, b, :], inv, ALU.mult).then_inc(S("cc_inv"), 1)
            for b in range(4):
                norm_add(dve, NRMC, b)
            norm_apply(dve, NRMC)
            dve.wait_ge(S("h3_loaded"), 16)
            for b in range(KB):
                q = WH["out_3"][1] + b // 2
                dve.wait_ge(quad_ready, q + 1)
                nc.vector.tensor_tensor(H3[:, b, :], H3[:, b, :], half(q, b % 2), ALU.add).then_inc(free(q), 1)
                if b >= 1:
                    norm_add(dve, NRMP, b - 1)
            norm_add(dve, NRMP, KB - 1)
            norm_apply(dve, NRMP)
            dve.wait_ge(*of(NRMP, "lo", KB))
            dve_groups(dve, "f3", H3, NRME)
            norm_apply(dve, NRME)

        @block.tensor
        def _(pe):
            if 1 in blocks:
                pe_block1(pe)
            if 2 in blocks:
                pe_block2(pe)
            if 3 in blocks:
                pe_block3(pe)

        @block.vector
        def _(dve):
            if 1 in blocks:
                dve_block1(dve)
            if 2 in blocks:
                dve_block2(dve)
            if 3 in blocks:
                dve_block3(dve)

        @block.scalar
        def _(act):
            act.dma_start(PAR[:, :], params).then_inc(S("par_loaded"), 16)
            if 1 in blocks:
                act_block1(act)
            if 2 in blocks:
                act_block2(act)
            if 3 in blocks:
                act_block3(act)
            for b in range(KB):
                act.wait_ge(*of(NRME, "x", b + 1))
                act.dma_start(outT[P * b:P * (b + 1), :], H3[:, b, :]).then_inc(S("stored"), 16)
            act.wait_ge(S("stored"), 16 * KB)


def kernel(**inputs):
    import numpy as np
    import concourse.bacc as bacc
    from concourse.bass_utils import run_bass_kernel_spmd as run

    a = {k: np.asarray(v) for k, v in inputs.items()}
    a = {k: (v[0] if v.ndim > 1 and v.shape[0] == 1 else v) for k, v in a.items()}
    tiles, _ = plan(BLOCKS)
    stream = np.empty((len(tiles) // TILES, P, TILES, P), np.float32)
    for n, (w, k, c) in enumerate(tiles):
        stream[n // TILES, :, n % TILES, :] = a[w][P * k:P * (k + 1), P * c:P * (c + 1)]

    params = np.zeros((P, NPARAM), np.float32)

    def put(name, value):
        at, n = PARAMS[name]
        params[:, at:at + n] = value

    for name in ("norm_g", "conv_b", "mnorm_g", "skip_m", "dnorm_g", "mem_norm_g", "final_g", "norm_mix_2", "b_gate_2",
                 "norm_ffn_2", "norm_final_2", "norm_mix_g_3", "lru_conv_b_3", "lru_gate_a_b_3", "lru_gate_x_b_3",
                 "lru_a_param_3", "cc_conv_b_3", "cc_ln_g_3", "cc_ln_b_3", "out_norm_lru_g_3", "out_norm_cc_g_3",
                 "norm_mlp_g_3", "norm_final_g_3", "conv_w", "lru_conv_w_3", "cc_conv_w_3"):
        put(name, a[name].reshape(-1, P).T)
    params[0:4, PARAMS["b_if"][0]] = a["b_if"][0:4]
    params[32:36, PARAMS["b_if"][0]] = a["b_if"][4:8]
    put("lam", np.concatenate([a["lam_q1"], a["lam_k1"], a["lam_q2"], a["lam_k2"]])[None, :])
    w_if = np.zeros((P, 12, 36), np.float32)
    w_if[:, :, 0:4] = a["w_if"].reshape(12, P, 8)[:, :, 0:4].transpose(1, 0, 2)
    w_if[:, :, 32:36] = a["w_if"].reshape(12, P, 8)[:, :, 4:8].transpose(1, 0, 2)
    put("w_if", w_if.reshape(P, -1))
    i = np.arange(P)
    put("ident", i[:, None] == i[None, :])
    put("ones", 1.0)
    put("mask_ts", np.where(i[:, None] <= i[None, :], 0.0, NEG))
    put("mask_qk", np.where(i[None, :] <= i[:, None], 0.0, NEG))
    put("eps", EPS)

    wqkv = np.stack([a["wq_m"], a["wk_m"], a["wv_m"]]).transpose(2, 0, 1, 3).reshape(P, -1)

    row, col = np.arange(P)[:, None], np.arange(SPAN)[None, :]
    rel = np.clip(SPAN - P + row - col, -128, 128) + 128
    unseen = ((row < 64) & (col >= SPAN - 64)) | ((row >= 64) & (col < 64))
    bias2 = np.where(unseen[:, None, :], np.float32(NEG), a["att_rel_bias_2"][:, rel].transpose(1, 0, 2)).astype(np.float32)

    low = i[:, None] <= i[None, :]
    sgu = np.concatenate([np.where(low[:, None, :], a["sgu_w_2"].transpose(2, 0, 1), np.float32(0)).reshape(P, -1)]
                         + [np.broadcast_to(a[n].reshape(1, -1), (P, 512)) for n in ("sgu_b_2", "sgu_norm_gain_2", "sgu_norm_bias_2")],
                         axis=1).astype(np.float32)

    lru_w = np.zeros((2, 4, P, P), np.float32)
    for g, name in enumerate(("lru_gate_a_w_3", "lru_gate_x_w_3")):
        for h in range(8):
            o = 64 * (h % 2)
            lru_w[g, h // 2, o:o + 64, o:o + 64] = a[name][h]
    lru_w = lru_w.transpose(2, 0, 1, 3).reshape(P, -1)

    arrays = {"xT": a["x"].T, "memT": a["mem"].T, "stream": stream.reshape(-1, P, SLOT), "params": params, "wqkv": wqkv,
              "sgu": sgu, "bias2": bias2.reshape(P, -1), "lru_w": lru_w, "metaT": a["meta_tokens_3"].T}
    arrays = {k: np.ascontiguousarray(v, dtype=np.float32) for k, v in arrays.items()}
    nc = bacc.Bacc("TRN2", target_bir_lowering=False, num_devices=1)
    args = [nc.dram_tensor(k, v.shape, F32, kind="ExternalInput").ap() for k, v in arrays.items()]
    args.append(nc.dram_tensor("outT", (D, T), F32, kind="ExternalOutput").ap())
    args.append(nc.dram_tensor("o_scr", (NT, P, 512), F32, kind="Internal").ap())
    args.append(nc.dram_tensor("h_scr", (D, T), F32, kind="Internal").ap())
    build(nc, *args, blocks=BLOCKS)
    r = run(nc, [arrays], core_ids=[0])
    return np.ascontiguousarray(r.results[0]["outT"].T)[None]
```
